# Optimizing a Trainium2 kernel written in Bass

```python
import math
import jax, jax.numpy as jnp
from jax import lax
import numpy as np

D_MODEL = 1024
BATCH = 1
SEQ = 256
DEPTH = 2

N_GROUPS = 4
MIX_HEADS = 4
HEAD_DIM = D_MODEL // (N_GROUPS * MIX_HEADS)
GROUP_WIDTH = MIX_HEADS * HEAD_DIM
MIX_WIDTH = N_GROUPS * GROUP_WIDTH
Q_BLOCK = 128
MLSTM_CHUNK = 64
MLSTM_CONV = 4
NSA_CMP_BLOCK = 32
NSA_CMP_STRIDE = 16
NSA_SEL_BLOCK = 64
NSA_N_SEL = 16
NSA_WINDOW = 512
NUM_BUCKETS = 32
MAX_DISTANCE = 128
D_FF = 2816
N_EXPERTS = 8
TOP_K = 2
D_FF_EXPERT = 3584
MOE_ROW_BLOCK = 128
NORM_EPS = 1e-6
MASK_VALUE = 1e30
N_DENSE = (DEPTH + 1) // 2
N_MOE = DEPTH // 2
IN_WIDTHS = (2 * GROUP_WIDTH, GROUP_WIDTH, GROUP_WIDTH, 2 * MIX_HEADS,
             GROUP_WIDTH, GROUP_WIDTH, GROUP_WIDTH, MIX_HEADS,
             GROUP_WIDTH, GROUP_WIDTH, GROUP_WIDTH,
             GROUP_WIDTH, 6 * HEAD_DIM, 3 * MIX_HEADS)
IN_WIDTH = sum(IN_WIDTHS)

kernel_name = "hybrid_parallel_heads_mlstm_fox_sb_nsa_moe"

def rmsnorm(x, g):
    xf = x.astype(jnp.float32)
    y = xf * lax.rsqrt(jnp.mean(xf * xf, axis=-1, keepdims=True) + NORM_EPS)
    return (y * g.astype(jnp.float32)).astype(x.dtype)

def masked_softmax(s, valid):
    p = jax.nn.softmax(jnp.where(valid, s, -MASK_VALUE), axis=-1)
    return jnp.where(valid, p, 0.0)

def t5_bias(dist, table):
    n = jnp.maximum(dist, 0)
    max_exact = NUM_BUCKETS // 2
    large = max_exact + (jnp.log(jnp.maximum(n, 1).astype(jnp.float32) / max_exact)
                         / math.log(MAX_DISTANCE / max_exact) * (NUM_BUCKETS - max_exact)).astype(jnp.int32)
    bucket = jnp.where(n < max_exact, n, jnp.minimum(large, NUM_BUCKETS - 1))
    return table[bucket].astype(jnp.float32)

def block_sweep(fn, seq):
    out = lax.map(fn, jnp.arange(seq // Q_BLOCK))
    n, b, qb, h, d = out.shape
    return jnp.moveaxis(out, 0, 1).reshape(b, n * qb, h, d)

def causal_conv(x, w):
    k, s = w.shape[0], x.shape[1]
    xp = jnp.pad(x, ((0, 0), (k - 1, 0), (0, 0)))
    return sum(w[j] * xp[:, k - 1 - j:k - 1 - j + s] for j in range(k))

def mlstm_chunkwise(q, k, v, ig, fg):
    B, S, H, Dh = q.shape
    L = MLSTM_CHUNK
    nc = S // L

    def chunks(a):
        return jnp.moveaxis(a.reshape(B, nc, L, H, *a.shape[3:]), 3, 1)

    q, k, v, ig = chunks(q), chunks(k), chunks(v), chunks(ig)
    b = jnp.cumsum(jax.nn.log_sigmoid(chunks(fg)), axis=-1)
    g = b[..., -1]
    w = g[..., None] - b + ig
    m_loc = jnp.max(w, axis=-1)
    ew = jnp.exp(w - m_loc[..., None])
    c_chunk = jnp.einsum('bhcl,bhcld,bhcle->bhcde', ew, v, k)
    n_chunk = jnp.einsum('bhcl,bhcle->bhce', ew, k)

    def step(carry, xs):
        C, n, m = carry
        c_c, n_c, ml_c, g_c = xs
        m_new = jnp.maximum(g_c + m, ml_c)
        a = jnp.exp(g_c + m - m_new)
        bb = jnp.exp(ml_c - m_new)
        C_new = a[..., None, None] * C + bb[..., None, None] * c_c
        n_new = a[..., None] * n + bb[..., None] * n_c
        return (C_new, n_new, m_new), (C, n, m)

    init = (jnp.zeros((B, H, Dh, Dh), jnp.float32), jnp.zeros((B, H, Dh), jnp.float32),
            jnp.zeros((B, H), jnp.float32))
    xs = tuple(jnp.moveaxis(a, 2, 0) for a in (c_chunk, n_chunk, m_loc, g))
    _, (C_prev, n_prev, m_prev) = lax.scan(step, init, xs)
    C_prev = jnp.moveaxis(C_prev, 0, 2)
    n_prev = jnp.moveaxis(n_prev, 0, 2)
    m_prev = jnp.moveaxis(m_prev, 0, 2)

    tri = jnp.tril(jnp.ones((L, L), bool))
    d_log = jnp.where(tri, b[..., :, None] - b[..., None, :] + ig[..., None, :], -MASK_VALUE)
    m_inter = b + m_prev[..., None]
    m_t = jnp.maximum(jnp.max(d_log, axis=-1), m_inter)
    s = jnp.einsum('bhcld,bhcsd->bhcls', q, k) * jnp.exp(d_log - m_t[..., None])
    inter_w = jnp.exp(m_inter - m_t)
    num = jnp.einsum('bhcls,bhcsd->bhcld', s, v) + inter_w[..., None] * jnp.einsum('bhcde,bhcle->bhcld', C_prev, q)
    den = jnp.sum(s, axis=-1) + inter_w * jnp.einsum('bhce,bhcle->bhcl', n_prev, q)
    h = num / jnp.maximum(jnp.abs(den), jnp.exp(-m_t))[..., None]
    return jnp.moveaxis(h, 1, 3).reshape(B, S, H, Dh)

def mlstm_mixer(qk_raw, v_raw, o_pre, if_pre, conv_w, gate_b, out_g):
    B, S, _ = v_raw.shape
    H, Dh = MIX_HEADS, HEAD_DIM
    qk = jax.nn.silu(causal_conv(qk_raw, conv_w))
    q, k = jnp.split(qk, 2, axis=-1)
    q = q.reshape(B, S, H, Dh).astype(jnp.float32)
    k = k.reshape(B, S, H, Dh).astype(jnp.float32) * (Dh ** -0.5)
    v = v_raw.reshape(B, S, H, Dh).astype(jnp.float32)
    gates = if_pre.astype(jnp.float32) + gate_b.astype(jnp.float32)
    h = mlstm_chunkwise(q, k, v, gates[..., :H], gates[..., H:])
    h = rmsnorm(h, out_g.reshape(H, Dh)).reshape(B, S, GROUP_WIDTH)
    return (h * jax.nn.sigmoid(o_pre.astype(jnp.float32))).astype(v_raw.dtype)

def fox_mixer(q, k, v, f_pre, f_b, q_g, k_g):
    B, S, _ = q.shape
    H, Dh = MIX_HEADS, HEAD_DIM
    q = rmsnorm(q.reshape(B, S, H, Dh), q_g)
    k = rmsnorm(k.reshape(B, S, H, Dh), k_g)
    v = v.reshape(B, S, H, Dh)
    F = jnp.cumsum(jax.nn.log_sigmoid(f_pre.astype(jnp.float32) + f_b.astype(jnp.float32)), axis=1)
    F = jnp.transpose(F, (0, 2, 1))
    kpos = jnp.arange(S)
    scale = Dh ** -0.5

    def blk(i):
        t0 = i * Q_BLOCK
        t = t0 + jnp.arange(Q_BLOCK)
        qb = lax.dynamic_slice_in_dim(q, t0, Q_BLOCK, axis=1)
        Fq = lax.dynamic_slice_in_dim(F, t0, Q_BLOCK, axis=2)
        s = jnp.einsum('bthd,bshd->bhts', qb, k).astype(jnp.float32) * scale + (Fq[..., :, None] - F[..., None, :])
        p = masked_softmax(s, kpos[None, :] <= t[:, None])
        return jnp.einsum('bhts,bshd->bthd', p.astype(v.dtype), v)

    return block_sweep(blk, S).reshape(B, S, GROUP_WIDTH)

def stick_breaking_mixer(q, k, v):
    B, S, _ = q.shape
    H, Dh = MIX_HEADS, HEAD_DIM
    q = q.reshape(B, S, H, Dh)
    k = k.reshape(B, S, H, Dh)
    v = v.reshape(B, S, H, Dh)
    kpos = jnp.arange(S)
    scale = Dh ** -0.5

    def blk(i):
        t0 = i * Q_BLOCK
        t = t0 + jnp.arange(Q_BLOCK)
        qb = lax.dynamic_slice_in_dim(q, t0, Q_BLOCK, axis=1)
        z = jnp.einsum('bthd,bshd->bhts', qb, k).astype(jnp.float32) * scale
        strict = kpos[None, :] < t[:, None]
        log_rest = jnp.where(strict, jax.nn.log_sigmoid(-z), 0.0)
        suffix = lax.cumsum(log_rest, axis=3, reverse=True) - log_rest
        a = jnp.where(strict, jnp.exp(jax.nn.log_sigmoid(z) + suffix), 0.0)
        return jnp.einsum('bhts,bshd->bthd', a.astype(v.dtype), v)

    return block_sweep(blk, S).reshape(B, S, GROUP_WIDTH)

def nsa_mixer(q, kv, g_pre, rel_bias, q_g, k_g, cmp_pos, cmp_wk, cmp_wv, gate_b):
    B, S, _ = q.shape
    H, Dh = MIX_HEADS, HEAD_DIM
    q = rmsnorm(q.reshape(B, S, H, Dh), q_g)
    kc_tok, vc_tok, k_sel, v_sel, k_win, v_win = jnp.split(kv, 6, axis=-1)
    k_sel = rmsnorm(k_sel, k_g[1])
    k_win = rmsnorm(k_win, k_g[2])
    n_cmp = (S - NSA_CMP_BLOCK) // NSA_CMP_STRIDE + 1
    cmp_start = jnp.arange(n_cmp) * NSA_CMP_STRIDE
    cmp_idx = cmp_start[:, None] + jnp.arange(NSA_CMP_BLOCK)[None, :]

    def compress(tok, w):
        return (tok[:, cmp_idx] + cmp_pos).reshape(B, n_cmp, NSA_CMP_BLOCK * Dh) @ w

    k_cmp = rmsnorm(compress(kc_tok, cmp_wk), k_g[0])
    v_cmp = compress(vc_tok, cmp_wv)
    cmp_end = cmp_start + NSA_CMP_BLOCK - 1
    n_sel = S // NSA_SEL_BLOCK
    k_top = min(NSA_N_SEL, n_sel)
    sel_start = jnp.arange(n_sel) * NSA_SEL_BLOCK
    overlap = jnp.clip(jnp.minimum(cmp_end[:, None] + 1, sel_start[None, :] + NSA_SEL_BLOCK)
                       - jnp.maximum(cmp_start[:, None], sel_start[None, :]), 0).astype(jnp.float32) / NSA_CMP_BLOCK
    k_win_p = jnp.pad(k_win, ((0, 0), (NSA_WINDOW, 0), (0, 0)))
    v_win_p = jnp.pad(v_win, ((0, 0), (NSA_WINDOW, 0), (0, 0)))
    gates = jax.nn.sigmoid(g_pre.astype(jnp.float32) + gate_b.astype(jnp.float32)).reshape(B, S, H, 3)
    scale = Dh ** -0.5
    gather = jax.vmap(lambda a, idx: a[idx])
    blk_id = jnp.arange(n_sel)

    def blk(i):
        t0 = i * Q_BLOCK
        t = t0 + jnp.arange(Q_BLOCK)
        qb = lax.dynamic_slice_in_dim(q, t0, Q_BLOCK, axis=1)
        s_c = (jnp.einsum('bthd,bnd->bhtn', qb, k_cmp).astype(jnp.float32) * scale
               + jnp.transpose(t5_bias(t[:, None] - cmp_end[None, :], rel_bias), (2, 0, 1)))
        p_c = masked_softmax(s_c, cmp_end[None, :] <= t[:, None])
        o_cmp = jnp.einsum('bhtn,bnd->bthd', p_c.astype(v_cmp.dtype), v_cmp)
        imp = jnp.einsum('bhtn,nj->btj', p_c, overlap)
        cur = t // NSA_SEL_BLOCK
        forced = (blk_id[None, :] == 0) | (blk_id[None, :] == cur[:, None]) | (blk_id[None, :] == cur[:, None] - 1)
        score = jnp.where(forced, MASK_VALUE, jnp.where(sel_start[None, :] <= t[:, None], imp, -MASK_VALUE))
        _, top = lax.top_k(score, k_top)
        tok = (top[..., None] * NSA_SEL_BLOCK + jnp.arange(NSA_SEL_BLOCK)).reshape(B, Q_BLOCK, k_top * NSA_SEL_BLOCK)
        ks = gather(k_sel, tok)
        vs = gather(v_sel, tok)
        dist_s = t[None, :, None] - tok
        s_s = (jnp.einsum('bthd,btkd->bhtk', qb, ks).astype(jnp.float32) * scale
               + jnp.transpose(t5_bias(dist_s, rel_bias), (0, 3, 1, 2)))
        p_s = masked_softmax(s_s, (dist_s >= 0)[:, None])
        o_sel = jnp.einsum('bhtk,btkd->bthd', p_s.astype(vs.dtype), vs)
        kw = lax.dynamic_slice_in_dim(k_win_p, t0, Q_BLOCK + NSA_WINDOW, axis=1)
        vw = lax.dynamic_slice_in_dim(v_win_p, t0, Q_BLOCK + NSA_WINDOW, axis=1)
        spos = t0 - NSA_WINDOW + jnp.arange(Q_BLOCK + NSA_WINDOW)
        dist_w = t[:, None] - spos[None, :]
        valid_w = (dist_w >= 0) & (dist_w < NSA_WINDOW) & (spos[None, :] >= 0)
        s_w = (jnp.einsum('bthd,bsd->bhts', qb, kw).astype(jnp.float32) * scale
               + jnp.transpose(t5_bias(dist_w, rel_bias), (2, 0, 1)))
        p_w = masked_softmax(s_w, valid_w)
        o_win = jnp.einsum('bhts,bsd->bthd', p_w.astype(vw.dtype), vw)
        g = lax.dynamic_slice_in_dim(gates, t0, Q_BLOCK, axis=1)
        return (g[..., 0:1] * o_cmp + g[..., 1:2] * o_sel + g[..., 2:3] * o_win).astype(q.dtype)

    return block_sweep(blk, S).reshape(B, S, GROUP_WIDTH)

def swiglu(h, wg, wu, wd):
    return (jax.nn.silu(h @ wg) * (h @ wu)) @ wd

def moe_swiglu(h, router_w, router_b, wg, wu, wd):
    B, S, D = h.shape
    T = B * S
    xf = h.reshape(T, D)
    logits = (xf @ router_w).astype(jnp.float32) + router_b.astype(jnp.float32)
    top_logit, top_e = lax.top_k(logits, TOP_K)
    top_w = jax.nn.softmax(top_logit, axis=-1)
    n_assign = T * TOP_K
    e_flat = top_e.reshape(-1)
    tok_flat = jnp.repeat(jnp.arange(T, dtype=jnp.int32), TOP_K)
    w_flat = top_w.reshape(-1)
    order = jnp.argsort(e_flat)
    e_s = e_flat[order]
    counts = jnp.bincount(e_flat, length=N_EXPERTS)
    padded = (counts + MOE_ROW_BLOCK - 1) // MOE_ROW_BLOCK * MOE_ROW_BLOCK
    start = jnp.cumsum(counts) - counts
    pstart = jnp.cumsum(padded) - padded
    dest = pstart[e_s] + jnp.arange(n_assign) - start[e_s]
    n_blocks = -(-(n_assign + N_EXPERTS * MOE_ROW_BLOCK) // MOE_ROW_BLOCK)
    n_rows = n_blocks * MOE_ROW_BLOCK
    row_tok = jnp.zeros((n_rows,), jnp.int32).at[dest].set(tok_flat[order])
    row_w = jnp.zeros((n_rows,), jnp.float32).at[dest].set(w_flat[order])
    blk_expert = jnp.minimum(jnp.searchsorted(jnp.cumsum(padded), jnp.arange(n_blocks) * MOE_ROW_BLOCK,
                                              side='right'), N_EXPERTS - 1)

    def expert_block(args):
        tok_b, e = args
        xb = xf[tok_b]
        return (jax.nn.silu(xb @ wg[e]) * (xb @ wu[e])) @ wd[e]

    y = lax.map(expert_block, (row_tok.reshape(n_blocks, MOE_ROW_BLOCK), blk_expert)).reshape(n_rows, D)
    out = jnp.zeros((T, D), y.dtype).at[row_tok].add(y * row_w[:, None].astype(y.dtype))
    return out.reshape(B, S, D).astype(h.dtype)

def setup_inputs(seed: int = 0) -> dict:
    key = jax.random.key(seed)
    ks = iter(jax.random.split(key, 40))
    f32 = jnp.float32

    def nrm(shape, scale):
        return jax.random.normal(next(ks), shape, f32) * scale

    def gain(shape):
        return 1.0 + nrm(shape, 0.05)

    D, H, Dh = D_MODEL, MIX_HEADS, HEAD_DIM
    return {
        "x": nrm((BATCH, SEQ, D), 1.0),
        "c": nrm((BATCH, D), 1.0),
        "rel_bias": nrm((NUM_BUCKETS, H), 0.5),
        "ada_w": nrm((DEPTH, D, 6 * D), 0.5 * D ** -0.5),
        "ada_b": nrm((DEPTH, 6 * D), 0.02),
        "norm1_g": gain((DEPTH, D)),
        "norm2_g": gain((DEPTH, D)),
        "w_in": nrm((DEPTH, D, IN_WIDTH), D ** -0.5),
        "w_out": nrm((DEPTH, MIX_WIDTH, D), MIX_WIDTH ** -0.5),
        "mlstm_conv_w": nrm((DEPTH, MLSTM_CONV, 2 * GROUP_WIDTH), MLSTM_CONV ** -0.5),
        "mlstm_gate_b": jnp.concatenate([nrm((DEPTH, H), 0.1), 3.0 + nrm((DEPTH, H), 0.5)], axis=-1),
        "mlstm_out_g": gain((DEPTH, GROUP_WIDTH)),
        "fox_f_b": 3.0 + nrm((DEPTH, H), 0.5),
        "fox_q_g": gain((DEPTH, Dh)),
        "fox_k_g": gain((DEPTH, Dh)),
        "nsa_q_g": gain((DEPTH, Dh)),
        "nsa_k_g": gain((DEPTH, 3, Dh)),
        "nsa_cmp_pos": nrm((DEPTH, NSA_CMP_BLOCK, Dh), 0.1),
        "nsa_cmp_wk": nrm((DEPTH, NSA_CMP_BLOCK * Dh, Dh), (NSA_CMP_BLOCK * Dh) ** -0.5),
        "nsa_cmp_wv": nrm((DEPTH, NSA_CMP_BLOCK * Dh, Dh), (NSA_CMP_BLOCK * Dh) ** -0.5),
        "nsa_gate_b": nrm((DEPTH, 3 * H), 0.1),
        "ffn_wg": nrm((N_DENSE, D, D_FF), D ** -0.5),
        "ffn_wu": nrm((N_DENSE, D, D_FF), D ** -0.5),
        "ffn_wd": nrm((N_DENSE, D_FF, D), D_FF ** -0.5),
        "moe_router_w": nrm((N_MOE, D, N_EXPERTS), D ** -0.5),
        "moe_router_b": nrm((N_MOE, N_EXPERTS), 0.01),
        "moe_wg": nrm((N_MOE, N_EXPERTS, D, D_FF_EXPERT), D ** -0.5),
        "moe_wu": nrm((N_MOE, N_EXPERTS, D, D_FF_EXPERT), D ** -0.5),
        "moe_wd": nrm((N_MOE, N_EXPERTS, D_FF_EXPERT, D), D_FF_EXPERT ** -0.5),
    }

def reference(x, c, rel_bias, ada_w, ada_b, norm1_g, norm2_g, w_in, w_out,
              mlstm_conv_w, mlstm_gate_b, mlstm_out_g, fox_f_b, fox_q_g, fox_k_g,
              nsa_q_g, nsa_k_g, nsa_cmp_pos, nsa_cmp_wk, nsa_cmp_wv, nsa_gate_b,
              ffn_wg, ffn_wu, ffn_wd, moe_router_w, moe_router_b, moe_wg, moe_wu, moe_wd):
    split_at = [int(v) for v in np.cumsum(IN_WIDTHS)[:-1]]
    cond = jax.nn.silu(c)
    for l in range(DEPTH):
        mod = cond @ ada_w[l] + ada_b[l]
        sh1, sc1, g1, sh2, sc2, g2 = [m[:, None, :] for m in jnp.split(mod, 6, axis=-1)]
        h = rmsnorm(x, norm1_g[l]) * (1.0 + sc1) + sh1
        (m_qk, m_v, m_o, m_if, f_q, f_k, f_v, f_f,
         s_q, s_k, s_v, n_q, n_kv, n_g) = jnp.split(h @ w_in[l], split_at, axis=-1)
        y_a = mlstm_mixer(m_qk, m_v, m_o, m_if, mlstm_conv_w[l], mlstm_gate_b[l], mlstm_out_g[l])
        y_b = fox_mixer(f_q, f_k, f_v, f_f, fox_f_b[l], fox_q_g[l], fox_k_g[l])
        y_c = stick_breaking_mixer(s_q, s_k, s_v)
        y_d = nsa_mixer(n_q, n_kv, n_g, rel_bias, nsa_q_g[l], nsa_k_g[l], nsa_cmp_pos[l],
                        nsa_cmp_wk[l], nsa_cmp_wv[l], nsa_gate_b[l])
        mix = jnp.concatenate([y_a, y_b, y_c, y_d], axis=-1)
        x = x + g1 * (mix @ w_out[l])
        h = rmsnorm(x, norm2_g[l]) * (1.0 + sc2) + sh2
        if l % 2 == 0:
            f = swiglu(h, ffn_wg[l // 2], ffn_wu[l // 2], ffn_wd[l // 2])
        else:
            f = moe_swiglu(h, moe_router_w[l // 2], moe_router_b[l // 2], moe_wg[l // 2], moe_wu[l // 2], moe_wd[l // 2])
        x = x + g2 * f
    return x


_drawn_inputs = setup_inputs


def setup_inputs(seed=0):
    import zlib

    import numpy as np

    out = dict(_drawn_inputs(seed))
    spreads = {}
    factors = {'mlstm_out_g': 5.916,
     'fox_f_b': 27.128,
     'fox_q_g': 8.0,
     'fox_k_g': 7.729,
     'nsa_q_g': 8.0,
     'nsa_k_g': 8.0,
     'nsa_cmp_pos': 3.383,
     'nsa_gate_b': 8.0,
     'moe_router_b': 19.22,
     'rel_bias': 3.7}
    for name, (base, spread) in spreads.items():
        noise = np.random.default_rng([zlib.crc32(name.encode()), seed]).standard_normal(out[name].shape)
        drawn = base * np.exp(spread * noise) if base else spread * noise
        out[name] = __import__('jax').numpy.asarray(drawn.astype(out[name].dtype))
    for name, factor in factors.items():
        out[name] = (out[name] * factor).astype(out[name].dtype)
    return out
```

```python
from contextlib import ExitStack

import concourse.bass as bass
from concourse import mybir

F32 = mybir.dt.float32
U32 = mybir.dt.uint32
ALU = mybir.AluOpType
ACT = mybir.ActivationFunctionType
AX = mybir.AxisListType

D = 1024
KC = D // 128
TT = 2
S = 256
DEPTH = 2
H = 4
DH = 64
W_IN = 3224
D_FF = 2816
N_EXP = 8
D_FE = 3584
EPS = 1e-6
NCMP = 15
RING = 7
LOADS = 21
SLOT = KC * 512
ACT_CHUNKS, VEC_CHUNKS = (0, 1, 4, 5), (2, 3, 6, 7)
CONST = {}
_at = 0
for _n, _w in (("ident", 128), ("ones", 1), ("minus_ones", 1), ("minus_tri", 128), ("causal", 384),
               ("causal_T", 384), ("strict_T", 384), ("valid_cmp", 30), ("iota8", 8)):
    CONST[_n] = (_at, _w)
    _at += _w
CONST_W = _at
PAR = {}
_at = 0
for _n, _w in (("norm1", 8), ("norm2", 8), ("conv", 16), ("gate_bias", 1), ("out_g", 8), ("fox_q", 1),
               ("fox_k", 1), ("nsa_q", 1), ("nsa_k", 3), ("cmp_pos", 32), ("nsa_gate_b", 12),
               ("router_b", 8), ("ada_b", 48)):
    PAR[_n] = (_at, _w)
    _at += _w
PAR_W = _at
WIN = ((0, 512), (512, 512), (1032, 512), (1544, 256), (1804, 512), (2316, 512), (2828, 384))
MIX_LOADS = ([("ada", i) for i in range(4)] + [("win", 0), ("win", 1), ("win", 2), ("ada", 4), ("ada", 5),
             ("win", 3), ("ada", 6), ("ada", 7), ("win", 4), ("ada", 8), ("ada", 9), ("win", 5),
             ("ada", 10), ("ada", 11), ("win", 6), ("wout", 0), ("wout", 1)])
FF_UNITS = tuple((384 * u, 384 if u < 6 else 512) for u in range(7))
FE_UNITS = tuple((512 * u, 512) for u in range(7))
GROUPS = [(None, 0)] + [(c, g) for c in range(6) for g in range(2)] + [(6, g) for g in range(3)]
NG = len(GROUPS)
ADA_AFTER = {6: 4, 7: 5, 8: 6, 9: 7, 10: 8, 11: 9, 12: 10, 13: 11}
HEADS = [(k, h) for k in ("mlstm", "fox", "stick", "sel", "win") for h in range(H)]
NH = len(HEADS)


def count(kinds, i):
    return sum(k in kinds for k, _ in HEADS[:i + 1])


SOFT = ("fox", "sel", "win")
BKINDS = SOFT + ("stick",)
PKINDS = SOFT + ("mlstm",)
N_B, N_P, N_STICK = count(BKINDS, NH), count(PKINDS, NH), H


class Ordered:

    def __init__(self, eng, own):
        self.eng, self.own, self.n, self.base = eng, own, {}, {}

    def __call__(self, ins, sem=None):
        sem = self.own if sem is None else sem
        key = id(sem)
        self.n[key] = self.n.get(key, 0) + 1
        ins.then_inc(sem, 1)
        self.eng.wait_ge(sem, self.n[key] + self.base.get(key, 0))

    def also(self, sem):
        self.n[id(sem)] = self.n.get(id(sem), 0) + 1
        self.eng.sem_inc(sem, 1)


def program(nc, t, out):
    ctx = ExitStack()
    with ctx:
        def sb(name, shape, dt=F32):
            return ctx.enter_context(nc.sbuf_tensor(name, shape, dt))

        def sem(name):
            return ctx.enter_context(nc.semaphore(name))

        ring = sb("ring", [128, RING, SLOT])
        wide = sb("wide", [128, 512])
        x = sb("x_res", [128, TT, D])
        xn = sb("x_norm", [128, TT, D])
        mix = xn
        hT = sb("h_T", [128, KC, S])
        const = sb("const", [128, CONST_W])
        par = sb("par", [128, DEPTH, PAR_W])
        bias = sb("rel_bias_tiles", [128, H, 384])
        biasc = sb("rel_bias_cmp", [128, TT * H, NCMP])
        table = sb("table", [32, H])
        onehot, future, relrow = (hT[0:p, 2 * k:2 * k + 2, :].rearrange("p a n -> p (a n)") for k, p in enumerate((32, H, H)))
        negm = sb("neg_m_run", [H, S])
        ccol = sb("c_col", [128, KC])
        cond = sb("cond", [128, KC])
        acc = sb("ada_acc", [128, 2, 512])
        modc = sb("mod_cols", [128, 48])
        scaleA = sb("mod_scale", [128, 2, KC])
        gate = sb("gate_rows", [128, 2, D])
        cmp_region = sb("cmp_region", [128, 32 * DH])
        cmpw = cmp_region[:, :].rearrange("p (j d) -> p j d", d=DH)
        nT = cmp_region[:, 0:4 * S].rearrange("p (v n) -> p v n", n=S)
        yacc = cmp_region[:, :].rearrange("p (t n) -> p t n", t=TT)
        pcT = cmp_region[:, 6 * S:7 * S].rearrange("p (t n) -> p t n", t=TT)
        small = sb("small", [128, 64])
        ss = sb("sumsq", [128, 32])
        rs = sb("rstd", [128, 32])
        prob = sb("prob", [128, 2, 384])
        probT = sb("prob_T", [128, 2, 384])
        pf, pTf = (a[:, :, :].rearrange("p a n -> p (a n)") for a in (prob, probT))
        graw, gz = wide[0:36, 0:S], wide[0:8, S:2 * S]
        gl, ig0, nmrow = pTf[0:8, 0:S], pTf[0:H, S:2 * S], pTf[0:H, 2 * S:3 * S]
        ucap = pf[0:H, 2 * S:3 * S]
        reverse = pf[:, 384:512]
        wgate = pf[:, 0:KC * 48].rearrange("p (k n) -> p k n", k=KC)
        cumf = sb("cum_logf", [8, S])
        gcol = sb("gate_cols", [128, TT, 16])
        expnm = sb("exp_neg_m", [128, TT, H])
        ng = sb("nsa_gates", [128, TT, 16])
        qk_region = sb("m_s_region", [128, 4 * (3 + S)])
        qkraw = qk_region[:, :].rearrange("p (a n) -> p a n", a=4)
        sT = qk_region[:, 0:4 * S].rearrange("p (a n) -> p a n", a=4)
        hbuf = qk_region[:, 0:1024].rearrange("p (a n) -> p a n", a=2)
        mqkT = sb("m_qk_T", [128, 4, S])
        mv = sb("m_v", [128, TT, H, DH + 1])
        mo = sb("m_o", [128, TT, 256])
        mh = acc[:, 0, :].rearrange("p (t h d) -> p t h d", t=TT, h=H)
        fqk = xn[:, 0, :].rearrange("p (t v d) -> p t v d", t=TT, v=8)
        nqk = xn[:, 1, 0:896].rearrange("p (t v d) -> p t v d", t=TT, v=7)
        kvT = sb("cmp_kv_T", [128, S])
        fT = sb("f_qk_T", [128, 4, S])
        conv = fT
        negf = sb("neg_cum_logf", [8, S])
        fv = sb("f_v", [128, TT, 256])
        sv = sb("s_v", [128, TT, 256])
        hsig = sv[:, :, :].rearrange("p t n -> p (t n)")
        hbT = mqkT[:, :, :].rearrange("p (a b) n -> p a (b n)", a=2)
        nv = sb("n_v", [128, TT, 2, DH])
        cmpx = xn[:, 0, 0:32 * NCMP].rearrange("p (j n) -> p j n", n=NCMP)
        kcn = sb("k_cmp", [NCMP, 2, DH])
        kcT = sb("k_cmp_T", [128, NCMP])
        vpad = sb("v_cmp_T", [DH, H, 32])
        vblk = sb("v_cmp_blocks", [128, H, DH])
        pc = sb("p_cmp", [128, TT, H, 32])
        nmax = sb("neg_max", [128, 2, TT])
        lsum = sb("exp_sums", [128, 5, H, TT])
        rl = sb("inv_sums", [128, H, TT])
        rw = sb("router_w", [128, KC, N_EXP])
        lg = sb("router_logits", [128, TT, N_EXP])
        top8 = sb("top8", [128, TT, 8])
        topi = sb("top_index", [128, TT, 8], U32)
        topf = sb("top_index_f", [128, TT, 8])
        tw = sb("top_weights", [128, TT, 4])
        wts = sb("expert_weights", [128, TT, N_EXP])
        wtmp = sb("expert_onehot", [128, N_EXP])
        scratch = nc.dram_tensor("rel_scratch", [H, 512], F32)

        ps = [ctx.enter_context(nc.psum_tensor(f"bank{i}", [128, 512], F32)) for i in range(8)]

        def cst(name, p=128):
            a, w = CONST[name]
            return const[0:p, a:a + w]

        def prm(l, name, p0=0, p1=128):
            a, w = PAR[name]
            return par[p0:p1, l, a:a + w]

        ident, ones = cst("ident"), cst("ones")
        ones_all, minus_all = (cst(n).to_broadcast([128, 128]) for n in ("ones", "minus_ones"))

        const_in = sem("const_in")
        rel_saved = sem("rel_saved")
        bias_in = sem("bias_in")
        bias_turned = sem("bias_turned")
        bias_ready = sem("bias_ready")
        layer_in = sem("layer_in")
        router_in = sem("router_in")
        out_saved = sem("out_saved")
        ring_full = [sem(f"ring_full{i}") for i in range(RING)]
        ring_free = [sem(f"ring_free{i}") for i in range(RING)]
        vec_seq = sem("vec_seq")
        act_seq = sem("act_seq")
        pool_seq = sem("pool_seq")
        rel_row = sem("rel_row_psum")
        rel_ready = sem("rel_row_ready")
        cond_exp = sem("cond_exp")
        x_sumsq = sem("x_sumsq")
        xn_ready = sem("xn_ready")
        xT_done = sem("xT_done")
        mod_ready = sem("mod_ready")
        hT_act = sem("hT_act")
        hT_vec = sem("hT_vec")
        acc_ready = sem("acc_ready")
        acc_reduced = sem("acc_reduced")
        mod_evac = sem("mod_evac")
        proj_done = sem("proj_done")
        proj_evac = sem("proj_evac")
        gate_abs = sem("gate_abs")
        gate_ln = sem("gate_ln")
        gate_rows = sem("gate_rows_ready")
        gate_T = sem("gate_T")
        gate_cols = sem("gate_cols_ready")
        nm_exp = sem("nm_exp")
        conv_done = sem("conv_done")
        conv_exp = sem("conv_exp")
        mqk_ready = sem("mqk_ready")
        sumsq_ready = sem("sumsq_ready")
        rstd_ready = sem("rstd_ready")
        fox_norm = sem("fox_norm")
        fox_T = sem("fox_T")
        fox_T_evac = sem("fox_T_evac")
        nsa_norm = sem("nsa_norm")
        nsa_T = sem("nsa_T")
        nsa_T_evac = sem("nsa_T_evac")
        gates_exp = sem("gates_exp")
        cmpx_ready = sem("cmpx_ready")
        cmp_done = sem("cmp_done")
        kcn_ready = sem("kcn_ready")
        vpad_ready = sem("vpad_ready")
        kv_T = sem("kv_T")
        kv_T_evac = sem("kv_T_evac")
        cmp_scores = sem("cmp_scores")
        cmp_shift = sem("cmp_shift")
        cmp_exp = sem("cmp_exp")
        cmp_probs = sem("cmp_probs")
        cmp_pT = sem("cmp_pT")
        cmp_pT_evac = sem("cmp_pT_evac")
        cmp_out = sem("cmp_out")
        head_scores = sem("head_scores")
        head_free = [sem(f"head_free{i}") for i in range(2)]
        head_shift = [sem(f"head_shift{i}") for i in range(2)]
        head_exp = sem("head_exp")
        stick_sp = sem("stick_softplus")
        stick_masked = sem("stick_masked")
        head_second = sem("head_second")
        head_pT = sem("head_pT")
        head_pv = sem("head_pv")
        o_free = sem("o_free")
        mo_exp = sem("mo_exp")
        mix_ready = sem("mix_ready")
        mixT_done = sem("mixT_done")
        mixT_act = sem("mixT_act")
        mixT_vec = sem("mixT_vec")
        wout_done = sem("wout_done")
        x_mixed = sem("x_mixed")
        ffn = {n: sem("ffn_" + n) for n in ("g", "u", "exp", "h", "T", "T_evac", "y", "y_read", "seq", "d")}
        moe = {n: sem("moe_" + n) for n in ("g", "u", "exp", "h", "T", "T_evac", "y", "y_read", "seq", "d")}
        moe_vec = sem("moe_vec_seq")
        x_final = sem("x_final")
        router_done = sem("router_done")
        router_shift = sem("router_shift")
        router_exp = sem("router_exp")

        def slot_of(i):
            return i % RING

        def loaded(eng, stage, i):
            eng.wait_ge(ring_full[slot_of(i)], stage * (16 * LOADS // RING) + 16 * (i // RING + 1))

        def slot_view(i, w):
            return ring[:, slot_of(i), 0:KC * w].rearrange("p (k n) -> p k n", k=KC)

        def slot_down(i, w):
            return ring[:, slot_of(i), 0:(w // 128) * D].rearrange("p (f n) -> p f n", n=D)

        block = ctx.enter_context(nc.Block())

        @block.sync
        def _(sp):
            sp.dma_start(const[:, :], t["const"]).then_inc(const_in, 16)
            sp.dma_start(par[:, :, :], t["par"].rearrange("l p n -> p l n")).then_inc(const_in, 16)
            sp.dma_start(onehot, t["onehot"]).then_inc(const_in, 16)
            sp.dma_start(reverse, t["reverse"]).then_inc(const_in, 16)
            sp.dma_start(future, t["future"]).then_inc(const_in, 16)
            sp.dma_start(table[:, :], t["rel_bias"]).then_inc(const_in, 16)
            sp.dma_start(ccol[:, :], t["c_cols"]).then_inc(const_in, 16)
            for tt in range(TT):
                sp.dma_start(x[:, tt, :], t["x"][0, tt * 128:tt * 128 + 128, :]).then_inc(const_in, 16)

            def put(stage, i, dst, src, first):
                if not (first and i < RING):
                    sp.wait_ge(ring_free[slot_of(i)], stage * (LOADS // RING) + i // RING)
                sp.dma_start(dst, src).then_inc(ring_full[slot_of(i)], 16)

            def mixer_loads(l, stage):
                for i, (kind, c) in enumerate(MIX_LOADS):
                    if kind == "ada":
                        src, w = t["ada_w"][l, :, c * 512:c * 512 + 512], 512
                    elif kind == "win":
                        c0, w = WIN[c]
                        src = t["w_in"][l, :, c0:c0 + w]
                    else:
                        src, w = t["w_out"][l, :, c * 512:c * 512 + 512], 512
                    if i == RING:
                        if l:
                            sp.wait_ge(x_final, l)
                            sp.wait_ge(cmp_done, l)
                        for j, g in enumerate((2, 5)):
                            row = t["ada_b"][l:l + 1, g * D:(g + 1) * D]
                            sp.dma_start(gate[:, j, :], row.to_broadcast([128, D])).then_inc(layer_in, 16)
                        sp.dma_start(wgate[:, :, :], t["w_gates"][l].rearrange("(k p) n -> p k n", p=128)).then_inc(layer_in, 16)
                        sp.dma_start(cmpw[0:DH, :, :], t["nsa_cmp_wk"][l].rearrange("(j d) e -> d j e", d=DH)).then_inc(layer_in, 16)
                        sp.dma_start(cmpw[DH:128, :, :], t["nsa_cmp_wv"][l].rearrange("(j d) e -> d j e", d=DH)).then_inc(layer_in, 16)
                    put(stage, i, slot_view(i, w), src.rearrange("(k p) n -> p k n", p=128), stage == 0 if isinstance(stage, int) else False)

            def swiglu_loads(stage, wg, wu, wd, units):
                for u, (c0, w) in enumerate(units):
                    for j, m in enumerate((wg, wu)):
                        put(stage, 3 * u + j, slot_view(3 * u + j, w),
                            m[:, c0:c0 + w].rearrange("(k p) n -> p k n", p=128), False)
                    put(stage, 3 * u + 2, slot_down(3 * u + 2, w),
                        wd[c0:c0 + w, :].rearrange("(f p) n -> p f n", p=128), False)

            mixer_loads(0, 0)
            swiglu_loads(1, t["ffn_wg"][0], t["ffn_wu"][0], t["ffn_wd"][0], FF_UNITS)
            mixer_loads(1, 2)
            sp.dma_start(rw[:, :, :], t["moe_router_w"][0].rearrange("(k p) n -> p k n", p=128)).then_inc(router_in, 16)
            wge, wue, wde = (t[n].rearrange("a e r c -> (a e r) c") for n in ("moe_wg", "moe_wu", "moe_wd"))
            with sp.Fori(0, N_EXP) as e:
                swiglu_loads(e + 3, wge[bass.ds(e * D, D), :], wue[bass.ds(e * D, D), :],
                             wde[bass.ds(e * D_FE, D_FE), :], FE_UNITS)
            sp.wait_ge(x_final, 2)
            for tt in range(TT):
                sp.dma_start(out[0, tt * 128:tt * 128 + 128, :], x[:, tt, :]).then_inc(out_saved, 16)
            sp.wait_ge(out_saved, 16 * TT)

        @block.gpsimd
        def _(pool):
            do = Ordered(pool, pool_seq)
            for a in (vpad[:, :, :], vblk[:, :, :], pc[:, :, :, :]):
                do(nc.gpsimd.memset(a, 0.0))
            do(nc.gpsimd.memset(mv[:, :, :, DH:DH + 1], 1.0))
            pool.wait_ge(rel_ready, 1)
            pool.dma_start(scratch.ap(), relrow[:, :]).then_inc(rel_saved, 16)
            pool.wait_ge(rel_saved, 16)
            sc = scratch.ap()
            for h in range(H):
                for col, w, at in ((0, 128, 128), (128, 256, 0)):
                    src = bass.AP(sc.tensor, h * 512 + at, [[1, 128], [1, w]])
                    pool.dma_start(bias[:, h, col:col + w], src).then_inc(bias_in, 16)

        @block.scalar
        def _(act):
            do = Ordered(act, act_seq)
            act.wait_ge(const_in, 144)
            act.activation(cond[:, :], ccol[:, :], ACT.Exp, scale=-1.0).then_inc(cond_exp, 1)

            def rstd(n, p, cols, width):
                do(act.activation(small[0:p, 32:32 + cols], ss[0:p, 0:cols], ACT.Ln, scale=1.0 / width, bias=epsb[0:p, :]))
                return act.activation(rs[0:p, 0:cols], small[0:p, 32:32 + cols], ACT.Exp, scale=-0.5)

            def norm(l, which):
                n = 2 * l + which
                if n:
                    act.wait_ge(x_mixed if which else x_final, l + 1 if which else l)
                for tt in range(TT):
                    do(act.activation(dump, x[:, tt, :], ACT.Square, accum_out=ss[:, tt:tt + 1]))
                do(rstd(n, 128, TT, D), x_sumsq)
                act.wait_ge(mod_ready, n + 1)
                for k in ACT_CHUNKS:
                    act.wait_ge(xT_done, KC * n + (k | 1) + 1)
                    do(act.activation(hT[:, k, :], ps[k // 2][:, 256 * (k % 2):256 * (k % 2) + 256], ACT.Identity,
                                      scale=scaleA[:, which, k:k + 1], bias=modc[:, (24 if which else 0) + k:(24 if which else 0) + k + 1]), hT_act)

            def mixer(l):
                for n, (c, g) in enumerate(GROUPS):
                    act.wait_ge(proj_done, NG * l + n + 1)
                    b = ps[n % 4]
                    halves = b[:, :].rearrange("p (a n) -> p a n", a=2)
                    if c is None:
                        do(act.activation(graw[:, :], b[0:36, 0:S], ACT.Copy))
                        do(act.activation(ng[:, :, 0:12], b[:, 256:288].rearrange("p (a n) -> p a n", a=2)[:, :, 0:12], ACT.Copy), proj_evac)
                    elif c == 0:
                        do(act.activation(qkraw[:, 2 * g:2 * g + 2, 3:3 + S], halves, ACT.Copy), proj_evac)
                    elif c == 1:
                        do(act.activation(mv[:, g, :, 0:DH], b[:, 0:256].rearrange("p (h d) -> p h d", h=H), ACT.Copy))
                        do(act.activation(mo[:, g, :], b[:, 256:512], ACT.Copy), proj_evac)
                    elif c == 2:
                        do(act.activation(fqk[:, g, :, :], b[:, :].rearrange("p (h d) -> p h d", h=8), ACT.Copy), proj_evac)
                    elif c == 3:
                        do(act.activation(fv[:, g, :], b[:, 0:256], ACT.Copy), proj_evac)
                    elif c == 4:
                        do(act.activation(sT[:, 2 * g:2 * g + 2, :], halves, ACT.Copy, scale=1.0 if g else DH ** -0.5), proj_evac)
                    elif c == 5:
                        do(act.activation(sv[:, g, :], b[:, 0:256], ACT.Copy))
                        do(act.activation(nqk[:, g, 0:4, :], b[:, 256:512].rearrange("p (h d) -> p h d", h=H), ACT.Copy), proj_evac)
                    elif g == 0:
                        do(act.activation(kvT[:, :], b[:, 0:S], ACT.Copy), proj_evac)
                    else:
                        kv = b[:, 0:256].rearrange("p (a b d) -> p a b d", a=2, b=2)
                        do(act.activation(nqk[:, g - 1, 4:6, :], kv[:, :, 0, :], ACT.Copy))
                        do(act.activation(nqk[:, g - 1, 6, :], kv[:, 0, 0, :], ACT.Copy))
                        do(act.activation(nv[:, g - 1, :, :], kv[:, :, 1, :], ACT.Copy), proj_evac)
                    if n == 1:
                        act.wait_ge(gate_abs, l + 1)
                        do(act.activation(gl[:, :], gl[:, :], ACT.Exp, scale=-1.0))
                        do(act.activation(gl[:, :], gl[:, :], ACT.Ln, bias=1.0), gate_ln)
                    if n == 4:
                        act.wait_ge(conv_done, l + 1)
                        do(act.activation(mqkT[:, :, :], conv[:, :, :], ACT.Exp, scale=-1.0), conv_exp)
                        act.wait_ge(gate_cols, l + 1)
                        do(act.activation(expnm[:, :, :], gcol[:, :, 4:8], ACT.Exp), nm_exp)
                    if n == 9:
                        act.wait_ge(sumsq_ready, 4 * l + 1)
                        do(rstd(0, 128, 16, DH), rstd_ready)
                act.wait_ge(sumsq_ready, 4 * l + 2)
                do(rstd(0, 128, 14, DH), rstd_ready)
                do(act.activation(ng[:, :, 0:12], ng[:, :, 0:12], ACT.Exp, scale=-1.0), gates_exp)
                act.wait_ge(sumsq_ready, 4 * l + 3)
                do(rstd(0, NCMP, 1, DH), rstd_ready)

                def exp_shifted(i):
                    kind, h = HEADS[i]
                    act.wait_ge(head_shift[i % 2], NH // 2 * l + i // 2 + 1)
                    e = prob[:, i % 2, :]
                    if kind == "mlstm":
                        do(act.activation(e[:, 0:256], e[:, 0:256], ACT.Exp, bias=gcol[:, 0, h:h + 1]))
                        do(act.activation(e[:, 256:384], e[:, 256:384], ACT.Exp, bias=gcol[:, 1, h:h + 1]), head_exp)
                    elif kind == "stick":
                        do(act.activation(probT[:, i % 2, :], probT[:, i % 2, :], ACT.Exp), head_exp)
                    else:
                        for tt, (a, b) in enumerate(((0, 128), (128, 384))):
                            do(act.activation(e[:, a:b], e[:, a:b], ACT.Exp, bias=nmax[:, i % 2, tt:tt + 1],
                                              accum_out=lsum[:, i // H, h, tt:tt + 1]), head_exp if tt else None)

                for i in range(NH + 1):
                    if i < NH and HEADS[i][0] == "stick":
                        act.wait_ge(head_scores, NH * l + i + 1)
                        act.wait_ge(head_second, N_B * l + count(BKINDS, i - 2))
                        e = prob[:, i % 2, :]
                        do(act.activation(e, ps[i % 2][:, 0:384], ACT.Abs))
                        do(act.activation(e, e, ACT.Exp, scale=-1.0))
                        do(act.activation(e, e, ACT.Ln, bias=1.0), stick_sp)
                    if i >= 1 and HEADS[i - 1][0] == "stick":
                        exp_shifted(i - 1)
                    if i < NH and HEADS[i][0] != "stick":
                        exp_shifted(i)
                    if i == H + 2:
                        act.wait_ge(sumsq_ready, 4 * l + 4)
                        do(rstd(0, 128, 8, DH), rstd_ready)
                        do(act.activation(mo[:, :, :], mo[:, :, :], ACT.Exp, scale=-1.0), mo_exp)
                act.wait_ge(cmp_shift, l + 1)
                do(act.activation(pc[:, :, :, 0:NCMP], pc[:, :, :, 0:NCMP], ACT.Exp), cmp_exp)
                for k in ACT_CHUNKS:
                    act.wait_ge(mixT_done, KC * l + (k | 1) + 1)
                    do(act.activation(hT[:, k, :], ps[k // 2][:, 256 * (k % 2):256 * (k % 2) + 256], ACT.Copy,
                                      scale=prm(l, "out_g")[:, k:k + 1]), mixT_act)

            def swiglu(f, units, ntt, base, do):
                steps = [(u, tt) for u in range(len(units)) for tt in range(ntt)]
                for j in range(len(steps) + 1):
                    if j < len(steps):
                        w = units[steps[j][0]][1]
                        act.wait_ge(f["g"], base + j + 1)
                        if j:
                            act.wait_ge(f["h"], base + j)
                        do(act.activation(hsig[:, 0:w], ps[4][:, 0:w], ACT.Exp, scale=-1.0), f["exp"])
                    if j:
                        w = units[steps[j - 1][0]][1]
                        act.wait_ge(f["T"], base + j)
                        if j >= 3:
                            act.wait_ge(f["d"], base + j - 2)
                        do(act.activation(hbT[:, (j - 1) % 2, 0:w], ps[6 + (j - 1) % 2][:, 0:w], ACT.Copy), f["T_evac"])

            epsb = small[:, 63:64]
            dump = hT[:, 0:4, :].rearrange("p k n -> p (k n)")
            act.wait_ge(rel_saved, 16)
            act.wait_ge(vec_seq, 1)
            norm(0, 0)
            mixer(0)
            norm(0, 1)
            swiglu(ffn, FF_UNITS, TT, 0, do)
            norm(1, 0)
            mixer(1)
            norm(1, 1)
            act.wait_ge(router_shift, 1)
            do(act.activation(tw[:, :, 0:1], tw[:, :, 0:1], ACT.Exp), router_exp)
            steps = TT * len(FE_UNITS)
            with act.Fori(0, N_EXP) as e:
                doe = Ordered(act, moe["seq"])
                for s in ("exp", "T_evac"):
                    doe.base[id(moe[s])] = e * steps
                swiglu(moe, FE_UNITS, TT, e * steps, doe)

        @block.tensor
        def _(pe):
            mm = nc.tensor.matmul

            def transpose_norm(n):
                pe.wait_ge(xn_ready, n + 1)
                for k in range(KC):
                    for tt in range(TT):
                        o = ps[k // 2][:, 256 * (k % 2) + 128 * tt:256 * (k % 2) + 128 * tt + 128]
                        last = nc.tensor.transpose(o, xn[:, tt, 128 * k:128 * k + 128], ident)
                    last.then_inc(xT_done, 1)

            def ada_reduce(l, c):
                pe.wait_ge(acc_ready, 12 * l + c + 1)
                if 12 * l + c >= 2:
                    pe.wait_ge(mod_evac, 12 * l + c - 1)
                b = ps[6 + c % 2]
                if c in (4, 5, 10, 11):
                    last = mm(b[:, :], ones_all, acc[:, c % 2, :], start=True, stop=True)
                else:
                    for q in range(4):
                        last = mm(b[:, q:q + 1], acc[:, c % 2, 128 * q:128 * q + 128], ones, start=True, stop=True)
                last.then_inc(acc_reduced, 1)

            def mixer(l):
                stage = 2 * l
                transpose_norm(2 * l)
                for c in range(4):
                    ada_reduce(l, c)
                pe.wait_ge(hT_act, 4 * (2 * l + 1))
                pe.wait_ge(hT_vec, 4 * (2 * l + 1))
                pe.wait_ge(layer_in, 80 * (l + 1))
                for n, (c, g) in enumerate(GROUPS):
                    b = ps[n % 4]
                    if n >= 4:
                        pe.wait_ge(proj_evac, NG * l + n - 3)
                    if c is None:
                        for k in range(KC):
                            mm(b[0:36, 0:S], wgate[:, k, 0:36], hT[:, k, :], start=k == 0, stop=k == KC - 1)
                        for tt in range(TT):
                            for k in range(KC):
                                last = mm(b[:, 256 + 16 * tt:268 + 16 * tt], hT[:, k, 128 * tt:128 * tt + 128], wgate[:, k, 36:48],
                                          start=k == 0, stop=k == KC - 1)
                        last.then_inc(proj_done, 1)
                        continue
                    i = MIX_LOADS.index(("win", c))
                    w = slot_view(i, WIN[c][1])
                    loaded(pe, stage, i)
                    if c in (0, 4):
                        for q in range(2):
                            for k in range(KC):
                                last = mm(b[:, 256 * q:256 * q + 256], w[:, k, 128 * (2 * g + q):128 * (2 * g + q) + 128],
                                          hT[:, k, :], start=k == 0, stop=k == KC - 1)
                    elif c == 6 and g == 0:
                        for k in range(KC):
                            last = mm(b[:, 0:S], w[:, k, 0:128], hT[:, k, :], start=k == 0, stop=k == KC - 1)
                    else:
                        tt, c0 = (g - 1, 128) if c == 6 else (g, 0)
                        cols = 512 if WIN[c][1] == 512 else 256
                        for k in range(KC):
                            last = mm(b[:, 0:cols], hT[:, k, 128 * tt:128 * tt + 128], w[:, k, c0:c0 + cols],
                                      start=k == 0, stop=k == KC - 1)
                    last.then_inc(proj_done, 1)
                    if g == (2 if c == 6 else 1):
                        pe.wait_ge(proj_done, NG * l + n + 1)
                        pe.sem_inc(ring_free[slot_of(i)], 1)
                    if n == 4:
                        pe.wait_ge(gate_rows, l + 1)
                        for tt in range(TT):
                            for r, at, w_ in ((ucap, 0, 4), (nmrow, 4, 4), (cumf, 8, 8)):
                                last = nc.tensor.transpose(ps[5][:, 16 * tt + at:16 * tt + at + w_], r[0:w_, 128 * tt:128 * tt + 128],
                                                           ident[0:w_, 0:w_])
                        last.then_inc(gate_T, 1)
                    if n in ADA_AFTER:
                        ada_reduce(l, ADA_AFTER[n])
                    if n == 13:
                        pe.wait_ge(fox_norm, l + 1)
                        for a in range(2):
                            for q in range(2):
                                for tt in range(TT):
                                    v = 4 * a + 2 * q
                                    last = nc.tensor.transpose(ps[4 + a][:, 256 * q + 128 * tt:256 * q + 128 * tt + 128],
                                                               fqk[:, tt, v:v + 2, :].rearrange("p v d -> p (v d)"), ident)
                            last.then_inc(fox_T, 1)
                pe.wait_ge(mod_evac, 12 * l + 12)
                pe.wait_ge(cmpx_ready, l + 1)
                for j in range(32):
                    mm(ps[6][0:NCMP, 0:DH], cmpx[0:DH, j, :], cmpw[0:DH, j, :], start=j == 0, stop=j == 31)
                for j in range(32):
                    last = mm(ps[7][0:DH, 0:NCMP], cmpw[DH:128, j, :], cmpx[DH:128, j, :], start=j == 0, stop=j == 31)
                last.then_inc(cmp_done, 1)
                pe.wait_ge(nsa_norm, l + 1)
                pe.wait_ge(fox_T_evac, 2 * (l + 1))
                for a in range(2):
                    for q in range(2):
                        v = 2 * q if a == 0 else 4 + q
                        for tt in range(TT):
                            last = nc.tensor.transpose(ps[4 + a][:, 256 * q + 128 * tt:256 * q + 128 * tt + 128],
                                                       nqk[:, tt, v:v + 2, :].rearrange("p v d -> p (v d)"), ident)
                    last.then_inc(nsa_T, 1)
                pe.wait_ge(kcn_ready, l + 1)
                pe.wait_ge(vpad_ready, l + 1)
                nc.tensor.transpose(ps[6][:, 0:NCMP], kcn[:, :, :].rearrange("p a d -> p (a d)"), ident[0:NCMP, 0:NCMP])
                last = nc.tensor.transpose(ps[7][:, 0:DH], vpad[:, :, :].rearrange("p h n -> p (h n)"), ident[0:DH, 0:DH])
                last.then_inc(kv_T, 1)

                def first(i):
                    kind, h = HEADS[i]
                    b = ps[i % 2]
                    if i >= 2:
                        pe.wait_ge(head_free[i % 2], NH // 2 * l + i // 2)
                    elif i == 0:
                        pe.wait_ge(proj_evac, NG * l + NG)
                        pe.wait_ge(mqk_ready, l + 1)
                    if kind in ("mlstm", "stick"):
                        T_ = mqkT if kind == "mlstm" else sT
                        p0 = DH * (h % 2)
                        q, k = T_[p0:p0 + DH, h // 2, :], T_[p0:p0 + DH, 2 + h // 2, :]
                        mm(b[:, 0:256], k[:, 0:128], q, start=True, stop=False, skip_group_check=True)
                        last = mm(b[:, 256:384], k[:, 128:256], q[:, 128:256], start=False, stop=True, skip_group_check=True)
                        if kind == "mlstm":
                            last = mm(ps[2 + i % 2][:, 0:256], ident[0:H, h:h + 1].to_broadcast([H, 128]), negm[:, :],
                                      start=True, stop=True)
                    else:
                        r = slice(DH * (h % 2), DH * (h % 2) + DH)
                        if kind == "fox":
                            q, k = fT[r, h // 2, :], fT[r, 2 + h // 2, :]
                        else:
                            q, k = nT[r, h // 2, :], nT[r, 2 + ((h % 2) ^ (kind == "win")), :]
                        fox = kind == "fox"
                        mm(b[:, 0:128], q[:, 0:128], k[:, 0:128], start=True, stop=not fox, skip_group_check=True)
                        last = mm(b[:, 128:384], q[:, 128:256], k, start=False, stop=not fox, skip_group_check=True)
                        if fox:
                            sel = ident[0:8, H + h:H + h + 1].to_broadcast([8, 128])
                            mm(b[:, 0:128], sel, negf[:, 0:128], start=False, stop=True, skip_group_check=True)
                            last = mm(b[:, 128:384], sel, negf[:, :], start=False, stop=True, skip_group_check=True)
                    last.then_inc(head_scores, 1)

                def second(i):
                    kind, h = HEADS[i]
                    if kind == "mlstm":
                        return
                    e = prob[:, i % 2, :]
                    if kind == "stick":
                        pe.wait_ge(stick_masked, N_STICK * l + h + 1)
                        b = ps[i % 2]
                        tri = cst("minus_tri")
                        mm(b[:, 0:256], tri, e[:, 0:256], start=False, stop=False, skip_group_check=True)
                        mm(b[:, 128:256], minus_all, e[:, 256:384], start=False, stop=False, skip_group_check=True)
                        last = mm(b[:, 256:384], tri, e[:, 256:384], start=False, stop=True, skip_group_check=True)
                    else:
                        pe.wait_ge(head_exp, NH * l + i + 1)
                        for q in range(3):
                            last = nc.tensor.transpose(ps[2 + i % 2][:, 128 * q:128 * q + 128], e[:, 128 * q:128 * q + 128], ident)
                    last.then_inc(head_second, 1)

                def third(i):
                    kind, h = HEADS[i]
                    gi = i // H
                    if kind == "stick":
                        pe.wait_ge(head_exp, NH * l + i + 1)
                    else:
                        pe.wait_ge(head_pT, N_P * l + count(PKINDS, i))
                    if h == 0:
                        if gi >= 2:
                            pe.wait_ge(o_free, 5 * l + gi - 1)
                        elif gi == 0:
                            pe.wait_ge(nsa_T_evac, 2 * l + 2)
                        else:
                            pe.wait_ge(kv_T_evac, l + 1)
                    if kind == "mlstm":
                        v = [mv[:, tt, h, :] for tt in range(TT)]
                    elif kind in ("fox", "stick"):
                        v = [(fv if kind == "fox" else sv)[:, tt, DH * h:DH * h + DH] for tt in range(TT)]
                    else:
                        v = [nv[:, tt, int(kind == "win"), :] for tt in range(TT)]
                    w = v[0].shape[-1]
                    pt = probT[:, i % 2, :]
                    o = [ps[4 + 2 * (gi % 2) + tt][:, w * h:w * h + w] for tt in range(TT)]
                    mm(o[0], pt[:, 0:128], v[0], start=True, stop=True)
                    mm(o[1], pt[:, 128:256], v[0], start=True, stop=False)
                    last = mm(o[1], pt[:, 256:384], v[1], start=False, stop=True)
                    last.then_inc(head_pv, 1)

                for i in range(NH + 2):
                    if i < NH:
                        first(i)
                    if 0 <= i - 1 < NH:
                        second(i - 1)
                    if i >= 2:
                        third(i - 2)

                for b in range(2):
                    pe.wait_ge(head_free[b], NH // 2 * (l + 1))
                for tt in range(TT):
                    for h in range(H):
                        c0 = 16 * (2 * tt + h // 2)
                        r = slice(DH * (h % 2), DH * (h % 2) + DH)
                        last = mm(ps[h % 2][:, c0:c0 + NCMP], nT[r, h // 2, 128 * tt:128 * tt + 128], kcT[r, :], start=True, stop=True)
                last.then_inc(cmp_scores, 1)
                pe.wait_ge(cmp_probs, l + 1)
                for tt in range(TT):
                    last = nc.tensor.transpose(ps[3][:, 128 * tt:128 * tt + 128], pc[:, tt, :, :].rearrange("p h n -> p (h n)"), ident)
                last.then_inc(cmp_pT, 1)
                pe.wait_ge(cmp_pT_evac, l + 1)
                for tt in range(TT):
                    last = mm(ps[2][:, 256 * tt:256 * tt + 256], pcT[:, tt, :], vblk[:, :, :].rearrange("p h d -> p (h d)"),
                              start=True, stop=True)
                last.then_inc(cmp_out, 1)

                pe.wait_ge(mix_ready, l + 1)
                for k in range(KC):
                    for tt in range(TT):
                        o = ps[k // 2][:, 256 * (k % 2) + 128 * tt:256 * (k % 2) + 128 * tt + 128]
                        last = nc.tensor.transpose(o, mix[:, tt, 128 * k:128 * k + 128], ident)
                    last.then_inc(mixT_done, 1)
                pe.wait_ge(mixT_act, 4 * (l + 1))
                pe.wait_ge(mixT_vec, 4 * (l + 1))
                for half in range(2):
                    i = MIX_LOADS.index(("wout", half))
                    loaded(pe, stage, i)
                    for tt in range(TT):
                        for k in range(KC):
                            last = mm(ps[4 + 2 * half + tt][:, :], hT[:, k, 128 * tt:128 * tt + 128], slot_view(i, 512)[:, k, :],
                                      start=k == 0, stop=k == KC - 1)
                        last.then_inc(wout_done, 1)
                    pe.wait_ge(wout_done, 4 * l + 2 * half + 2)
                    pe.sem_inc(ring_free[slot_of(i)], 1)

            def swiglu(f, stage, units, ntt, base, base_y):
                steps = [(u, tt) for u in range(len(units)) for tt in range(ntt)]

                def lhs(k, tt):
                    return hT[:, k, 128 * tt:128 * tt + 128]

                def up(j, part):
                    u, tt = steps[j]
                    w = units[u][1]
                    i = 3 * u + part
                    if tt == 0:
                        loaded(pe, stage, i)
                    if j:
                        pe.wait_ge(f["h"], base + j)
                    for k in range(KC):
                        last = mm(ps[4 + part][:, 0:w], lhs(k, tt), slot_view(i, w)[:, k, :], start=k == 0, stop=k == KC - 1)
                    s = f["gu"[part]]
                    last.then_inc(s, 1)
                    if tt == ntt - 1:
                        pe.wait_ge(s, base + j + 1)
                        pe.sem_inc(ring_free[slot_of(i)], 1)

                def turn(j):
                    u, tt = steps[j]
                    pe.wait_ge(f["h"], base + j + 1)
                    if j >= 2:
                        pe.wait_ge(f["T_evac"], base + j - 1)
                    for q in range(units[u][1] // 128):
                        last = nc.tensor.transpose(ps[6 + j % 2][:, 128 * q:128 * q + 128], hbuf[:, j % 2, 128 * q:128 * q + 128], ident)
                    last.then_inc(f["T"], 1)

                def down(j):
                    u, tt = steps[j]
                    nf = units[u][1] // 128
                    i = 3 * u + 2
                    if tt == 0:
                        loaded(pe, stage, i)
                    pe.wait_ge(f["T_evac"], base + j + 1)
                    for half in range(2):
                        for q in range(nf):
                            last = mm(ps[2 * tt + half][:, :], hbT[:, j % 2, 128 * q:128 * q + 128],
                                      slot_down(i, nf * 128)[:, q, 512 * half:512 * half + 512],
                                      start=u == 0 and q == 0, stop=u == len(units) - 1 and q == nf - 1)
                    last.then_inc(f["d"], 1)
                    if tt == ntt - 1:
                        pe.wait_ge(f["d"], base + j + 1)
                        pe.sem_inc(ring_free[slot_of(i)], 1)

                for j in range(len(steps) + 1):
                    if j < len(steps):
                        up(j, 0)
                    if j:
                        turn(j - 1)
                    if j < len(steps):
                        up(j, 1)
                    if j:
                        down(j - 1)
                pe.wait_ge(f["d"], base + len(steps))
                pe.sem_inc(f["y"], 1)
                pe.wait_ge(f["y_read"], base_y + 1)

            pe.wait_ge(const_in, 144)
            mm(ps[0][0:H, :], table[:, :], onehot, start=True, stop=True).then_inc(rel_row, 1)
            pe.wait_ge(bias_in, 8 * 16)
            for h in range(H):
                last = mm(ps[4 + h][:, 0:384], reverse, bias[:, h, :], start=True, stop=True)
            last.then_inc(bias_turned, 1)
            pe.wait_ge(bias_ready, 1)
            mixer(0)
            transpose_norm(1)
            pe.wait_ge(hT_act, 8)
            pe.wait_ge(hT_vec, 8)
            swiglu(ffn, 1, FF_UNITS, TT, 0, 0)
            mixer(1)
            transpose_norm(3)
            pe.wait_ge(hT_act, 16)
            pe.wait_ge(hT_vec, 16)
            pe.wait_ge(router_in, 16)
            for tt in range(TT):
                for k in range(KC):
                    last = mm(ps[7][:, 8 * tt:8 * tt + 8], hT[:, k, 128 * tt:128 * tt + 128], rw[:, k, :], start=k == 0, stop=k == KC - 1)
            last.then_inc(router_done, 1)
            pe.wait_ge(router_shift, 1)
            steps = TT * len(FE_UNITS)
            with pe.Fori(0, N_EXP) as e:
                swiglu(moe, e + 3, FE_UNITS, TT, e * steps, e)

        @block.vector
        def _(dve):
            do = Ordered(dve, vec_seq)
            V = nc.vector
            TTop, TS, STT = V.tensor_tensor, V.tensor_scalar, V.scalar_tensor_tensor
            do(V.memset(small[:, 63:64], EPS))
            dve.wait_ge(const_in, 144)
            dve.wait_ge(rel_row, 1)
            do(TTop(relrow[:, :], ps[0][0:H, :], future, ALU.add), rel_ready)
            dve.wait_ge(bias_turned, 1)
            for h in range(H):
                do(V.tensor_copy(bias[:, h, :], ps[4 + h][:, 0:384]), bias_ready if h == H - 1 else None)
            dve.wait_ge(cond_exp, 1)
            do(TS(cond[:, :], cond[:, :], 1.0, None, ALU.add))
            do(V.reciprocal(cond[:, :], cond[:, :]))
            do(TTop(cond[:, :], cond[:, :], ccol[:, :], ALU.mult))

            def ada_sum(l, stage, c):
                i = MIX_LOADS.index(("ada", c))
                loaded(dve, stage, i)
                if 12 * l + c >= 2:
                    dve.wait_ge(acc_reduced, 12 * l + c - 1)
                w, a = slot_view(i, 512), acc[:, c % 2, :]
                do(TS(a, w[:, 0, :], cond[:, 0:1], None, ALU.mult))
                for k in range(1, KC):
                    ins = STT(a, w[:, k, :], cond[:, k:k + 1], a, ALU.mult, ALU.add)
                    do(ins, acc_ready if k == KC - 1 else None)
                dve.sem_inc(ring_free[slot_of(i)], 1)

            def ada_take(l, c):
                dve.wait_ge(acc_reduced, 12 * l + c + 1)
                b = ps[6 + c % 2]
                if c in (4, 5, 10, 11):
                    if c == 4:
                        dve.wait_ge(layer_in, 80 * (l + 1))
                    g = gate[:, c // 6, 512 * (c % 2):512 * (c % 2) + 512]
                    do(TTop(g, b[:, :], g, ALU.add), mod_evac)
                else:
                    do(TTop(modc[:, 4 * c:4 * c + 4], b[:, 0:4], prm(l, "ada_b")[:, 4 * c:4 * c + 4], ALU.add), mod_evac)

            def mod_scale(l, which):
                sc = modc[:, 24 * which + 8:24 * which + 16]
                do(STT(scaleA[:, which, :], sc, 1.0, prm(l, "norm2" if which else "norm1"), ALU.add, ALU.mult), mod_ready)

            def normalise(n):
                dve.wait_ge(x_sumsq, n + 1)
                for tt in range(TT):
                    do(TS(xn[:, tt, :], x[:, tt, :], rs[:, tt:tt + 1], None, ALU.mult), xn_ready if tt else None)

            def modulate(n, which):
                for k in VEC_CHUNKS:
                    dve.wait_ge(xT_done, KC * n + (k | 1) + 1)
                    do(TS(hT[:, k, :], ps[k // 2][:, 256 * (k % 2):256 * (k % 2) + 256], scaleA[:, which, k:k + 1],
                          modc[:, 24 * which + k:24 * which + k + 1], ALU.mult, ALU.add), hT_vec)

            def bc(ap, n):
                s = list(ap.shape)
                return (ap.rearrange("p (a o) -> p a o", o=1) if len(s) == 2 else ap.rearrange("p a (b o) -> p a b o", o=1)).to_broadcast(s + [n])

            def sumsq(src, dst, n):
                for a in range(0, n, 8):
                    m = min(8, n - a)
                    sq = wide[0:src.shape[0], 0:m * DH].rearrange("p (a d) -> p a d", d=DH)
                    do(TTop(sq, src[:, a:a + m, :], src[:, a:a + m, :], ALU.mult))
                    last = V.tensor_reduce(dst[:, a:a + m], sq, AX.X, ALU.add)
                    if a + m < n:
                        do(last)
                return last

            def mixer(l):
                stage = 2 * l
                normalise(2 * l)
                do(V.memset(qkraw[:, :, 0:3], 0.0))
                for c in range(4):
                    ada_sum(l, stage, c)
                    if c:
                        ada_take(l, c - 1)
                ada_take(l, 3)
                mod_scale(l, 0)
                modulate(2 * l, 0)
                dve.wait_ge(proj_evac, NG * l + 1)
                gb = prm(l, "gate_bias")
                do(TS(gz[:, :], graw[0:8, :], gb[0:8, :], None, ALU.add))
                do(TS(ig0[:, :], graw[32:36, :], gb[32:36, :], None, ALU.add))
                nb = prm(l, "nsa_gate_b").rearrange("p (o n) -> p o n", o=1).to_broadcast([128, TT, 12])
                do(TTop(ng[:, :, 0:12], ng[:, :, 0:12], nb, ALU.add))
                do(STT(gl[:, :], gz[:, :], -1.0, gz[:, :], ALU.mult, ALU.max), gate_abs)
                dve.wait_ge(gate_ln, l + 1)
                do(STT(gz[:, :], gz[:, :], 0.0, gl[:, :], ALU.min, ALU.subtract))
                do(TS(gl[:, :], gl[:, :], 0.0, 1.0, ALU.mult, ALU.add))
                do(V.tensor_tensor_scan(cumf[:, :], gl[:, :], gz[:, :], 0.0, ALU.mult, ALU.add))
                do(TS(negf[:, :], cumf[:, :], -1.0, None, ALU.mult))
                do(TTop(ucap, cumf[0:H, :], ig0, ALU.subtract))
                do(V.tensor_tensor_scan(negm[:, :], ucap, ucap, 0.0, ALU.min, ALU.min))
                do(TTop(ucap, ig0, cumf[0:H, :], ALU.subtract))
                do(TTop(nmrow, negm[:, :], cumf[0:H, :], ALU.subtract), gate_rows)
                dve.wait_ge(proj_evac, NG * l + 3)
                if l == 0:
                    dve.wait_ge(pool_seq, 4)
                cw = prm(l, "conv")
                for q in range(4):
                    o = conv[:, q, :]
                    do(TS(o, qkraw[:, q, 3:3 + S], cw[:, 4 * q:4 * q + 1], None, ALU.mult))
                    for j in range(1, 4):
                        ins = STT(o, qkraw[:, q, 3 - j:3 - j + S], cw[:, 4 * q + j:4 * q + j + 1], o, ALU.mult, ALU.add)
                        do(ins, conv_done if (q, j) == (3, 3) else None)
                dve.wait_ge(gate_T, l + 1)
                do(V.tensor_copy(gcol[:, :, :], ps[5][:, 0:32].rearrange("p (a n) -> p a n", a=2)), gate_cols)
                ada_sum(l, stage, 4)
                ada_sum(l, stage, 5)
                dve.wait_ge(conv_exp, l + 1)
                wv = mqkT
                do(TS(wv[:, :, :], wv[:, :, :], 1.0, None, ALU.add))
                do(V.reciprocal(wv[:, :, :], wv[:, :, :]))
                do(TTop(mqkT[:, 0:2, :], conv[:, 0:2, :], wv[:, 0:2, :], ALU.mult))
                do(STT(mqkT[:, 2:4, :], conv[:, 2:4, :], DH ** -0.5, wv[:, 2:4, :], ALU.mult, ALU.mult), mqk_ready)
                ada_take(l, 4)
                ada_sum(l, stage, 6)
                ada_take(l, 5)
                ada_sum(l, stage, 7)
                dve.wait_ge(proj_evac, NG * l + 7)
                fall = fqk[:, :, :, :].rearrange("p t v d -> p (t v) d")
                do(sumsq(fall, ss[:, 0:16], 16), sumsq_ready)
                ada_take(l, 6)
                ada_sum(l, stage, 8)
                ada_take(l, 7)
                ada_sum(l, stage, 9)
                dve.wait_ge(rstd_ready, 4 * l + 1)
                do(TTop(fall, fall, bc(rs[:, 0:16], DH), ALU.mult), fox_norm)
                fg = small[:, 0:1]
                do(TS(fg, prm(l, "fox_q"), DH ** -0.5, None, ALU.mult))
                do(TS(small[:, 2:3], prm(l, "nsa_q"), DH ** -0.5, None, ALU.mult))
                ada_take(l, 8)
                ada_sum(l, stage, 10)
                ada_take(l, 9)
                ada_sum(l, stage, 11)
                ada_take(l, 10)
                ada_take(l, 11)
                mod_scale(l, 1)
                for a in range(2):
                    dve.wait_ge(fox_T, 2 * l + a + 1)
                    do(TS(fT[:, 2 * a:2 * a + 2, :], ps[4 + a][:, :].rearrange("p (h n) -> p h n", h=2),
                          prm(l, "fox_k") if a else fg, None, ALU.mult), fox_T_evac)
                dve.wait_ge(proj_evac, NG * l + 14)
                for n in range(NCMP):
                    last = TTop(cmpx[:, :, n], kvT[:, 16 * n:16 * n + 32], prm(l, "cmp_pos"), ALU.add)
                    do(last, cmpx_ready if n == NCMP - 1 else None)
                dve.wait_ge(proj_evac, NG * l + NG)
                nall = nqk[:, :, :, :].rearrange("p t v d -> p (t v) d")
                do(sumsq(nall, ss[:, 0:14], 14), sumsq_ready)
                dve.wait_ge(rstd_ready, 4 * l + 2)
                do(TTop(nall, nall, bc(rs[:, 0:14], DH), ALU.mult), nsa_norm)
                dve.wait_ge(cmp_done, l + 1)
                do(V.tensor_copy(kcn[:, :, :], ps[6][0:NCMP, 0:DH].rearrange("p (o d) -> p o d", o=1).to_broadcast([NCMP, 2, DH])))
                vv = ps[7][0:DH, 0:NCMP].rearrange("p (o n) -> p o n", o=1).to_broadcast([DH, H, NCMP])
                do(V.tensor_copy(vpad[:, :, 0:NCMP], vv), vpad_ready)
                do(sumsq(kcn[:, 0:1, :], ss[0:NCMP, 0:1], 1), sumsq_ready)
                dve.wait_ge(rstd_ready, 4 * l + 3)
                do(TS(kcn[:, :, :], kcn[:, :, :], rs[0:NCMP, 0:1], None, ALU.mult), kcn_ready)
                dve.wait_ge(nsa_T, 2 * l + 1)
                do(TS(nT[:, 0:2, :], ps[4][:, :].rearrange("p (h n) -> p h n", h=2), small[:, 2:3], None, ALU.mult), nsa_T_evac)
                dve.wait_ge(nsa_T, 2 * l + 2)
                for q in range(2):
                    do(TS(nT[:, 2 + q, :], ps[5][:, 256 * q:256 * q + 256], prm(l, "nsa_k")[:, 1 + q:2 + q], None, ALU.mult),
                       nsa_T_evac if q else None)
                dve.wait_ge(kv_T, l + 1)
                do(TS(kcT[:, :], ps[6][:, 0:NCMP], prm(l, "nsa_k")[:, 0:1], None, ALU.mult))
                for h in range(H):
                    r = slice(32 * h, 32 * h + NCMP)
                    do(V.tensor_copy(vblk[r, h, :], ps[7][r, 0:DH]), kv_T_evac if h == H - 1 else None)
                dve.wait_ge(gates_exp, l + 1)
                do(TS(ng[:, :, 0:12], ng[:, :, 0:12], 1.0, None, ALU.add))
                do(V.reciprocal(ng[:, :, 0:12], ng[:, :, 0:12]))

                if l == 0:
                    do(V.memset(biasc[:, :, :], -1e30))
                    do(V.tensor_copy(biasc[:, 0:4, 0:7], bias[:, :, 31:128:16]))
                    do(V.tensor_copy(biasc[:, 4:8, :], bias[:, :, 128 + 31:384:16]))

                def part1(i):
                    kind, h = HEADS[i]
                    e, b = prob[:, i % 2, :], ps[i % 2][:, 0:384]
                    if kind == "stick":
                        dve.wait_ge(stick_sp, N_STICK * l + h + 1)
                        do(STT(e, b, 0.0, e, ALU.max, ALU.add))
                        do(STT(e, cst("strict_T"), 0.0, e, ALU.is_ge, ALU.mult), stick_masked)
                        return
                    dve.wait_ge(head_scores, NH * l + i + 1)
                    if i >= 2 and HEADS[i - 2][0] in BKINDS:
                        dve.wait_ge(head_second, N_B * l + count(BKINDS, i - 2))
                    if kind == "mlstm":
                        m = ps[2 + i % 2]
                        mask = cst("causal_T")
                        do(TTop(e[:, 0:256], m[:, 0:256], mask[:, 0:256], ALU.add))
                        do(TTop(e[:, 256:384], m[:, 128:256], mask[:, 256:384], ALU.add), head_shift[i % 2])
                        return
                    if kind == "fox":
                        for tt, (c0, c1) in enumerate(((0, 128), (128, 384))):
                            do(STT(e[:, c0:c1], b[:, c0:c1], gcol[:, tt, 12 + h:13 + h], cst("causal")[:, c0:c1], ALU.add, ALU.add),
                               head_free[i % 2] if tt else None)
                    else:
                        do(TTop(e, b, bias[:, h, :], ALU.add), head_free[i % 2])
                    do(V.tensor_reduce(nmax[:, i % 2, 0:1], e[:, 0:128], AX.X, ALU.max, negate=True))
                    do(V.tensor_reduce(nmax[:, i % 2, 1:2], e[:, 128:384], AX.X, ALU.max, negate=True), head_shift[i % 2])

                def part2(i):
                    kind, h = HEADS[i]
                    e, b, pt = prob[:, i % 2, :], ps[i % 2][:, 0:384], probT[:, i % 2, :]
                    if i >= 2:
                        dve.wait_ge(head_pv, NH * l + i - 1)
                    if kind == "mlstm":
                        dve.wait_ge(head_exp, NH * l + i + 1)
                        do(TTop(pt, b, e, ALU.mult), head_pT)
                        do.also(head_free[i % 2])
                    elif kind == "stick":
                        dve.wait_ge(head_second, N_B * l + count(BKINDS, i))
                        do(TTop(pt, b, cst("strict_T"), ALU.add), head_shift[i % 2])
                        do.also(head_free[i % 2])
                    else:
                        dve.wait_ge(head_second, N_B * l + count(BKINDS, i))
                        do(V.tensor_copy(pt, ps[2 + i % 2][:, 0:384]), head_pT)

                def finish(gi):
                    kind = HEADS[H * gi][0]
                    dve.wait_ge(head_pv, NH * l + H * gi + H)
                    o = [ps[4 + 2 * (gi % 2) + tt] for tt in range(TT)]
                    cols = {"mlstm": 0, "fox": 256, "stick": 512}.get(kind, 768)
                    dst = [mix[:, tt, cols:cols + 256].rearrange("p (h d) -> p h d", h=H) for tt in range(TT)]
                    if kind == "mlstm":
                        for tt in range(TT):
                            ov = o[tt][:, 0:H * (DH + 1)].rearrange("p (h d) -> p h d", h=H)
                            dn = small[:, 8:12]
                            do(V.tensor_copy(dn.rearrange("p (h o) -> p h o", o=1), ov[:, :, DH:DH + 1]))
                            do(STT(dn, dn, -1.0, dn, ALU.mult, ALU.max))
                            do(TTop(dn, dn, expnm[:, tt, :], ALU.max))
                            do(V.reciprocal(dn, dn))
                            do(TTop(mh[:, tt, :, :], ov[:, :, 0:DH], bc(dn, DH), ALU.mult), o_free if tt else None)
                        mall = mh[:, :, :, :].rearrange("p t h d -> p (t h) d")
                        do(sumsq(mall, ss[:, 0:8], 8), sumsq_ready)
                        return
                    if kind == "stick":
                        for tt in range(TT):
                            do(V.tensor_copy(dst[tt], o[tt][:, 0:256].rearrange("p (h d) -> p h d", h=H)), o_free if tt else None)
                        return
                    do(V.reciprocal(rl[:, :, :], lsum[:, gi, :, :]))
                    if kind in ("sel", "win"):
                        gcolumn = 1 if kind == "sel" else 2
                        gv = ng[:, :, 0:12].rearrange("p t (h c) -> p h t c", c=3)[:, :, :, gcolumn]
                        do(TTop(rl[:, :, :], rl[:, :, :], gv, ALU.mult))
                    for tt in range(TT):
                        ov = o[tt][:, 0:256].rearrange("p (h d) -> p h d", h=H)
                        r = rl[:, :, tt:tt + 1].to_broadcast([128, H, DH])
                        if kind == "win":
                            wd = wide[:, 256 * tt:256 * tt + 256].rearrange("p (h d) -> p h d", h=H)
                            do(TTop(wd, ov, r, ALU.mult), o_free if tt else None)
                            do(TTop(dst[tt], dst[tt], wd, ALU.add))
                        else:
                            do(TTop(dst[tt], ov, r, ALU.mult), o_free if tt else None)

                def finish_mlstm():
                    dve.wait_ge(rstd_ready, 4 * l + 4)
                    mall = mh[:, :, :, :].rearrange("p t h d -> p (t h) d")
                    do(TTop(mall, mall, bc(rs[:, 0:8], DH), ALU.mult))
                    dve.wait_ge(mo_exp, l + 1)
                    do(TS(mo[:, :, :], mo[:, :, :], 1.0, None, ALU.add))
                    do(V.reciprocal(mo[:, :, :], mo[:, :, :]))
                    do(TTop(mix[:, :, 0:256], mh[:, :, :, :].rearrange("p t h d -> p t (h d)"), mo[:, :, :], ALU.mult))

                for i in range(NH + 2):
                    if i < NH:
                        part1(i)
                    if 0 <= i - 1 < NH:
                        part2(i - 1)
                    if i >= 2 and (i - 2) % H == H - 1:
                        finish((i - 2) // H)
                    if i == H + 3:
                        finish_mlstm()

                dve.wait_ge(cmp_scores, l + 1)
                pcv = pc[:, :, :, 0:NCMP].rearrange("p t h n -> p (t h) n")
                for q in range(2):
                    sc = ps[q][:, 0:64].rearrange("p (a n) -> p a n", a=4)[:, :, 0:NCMP]
                    do(TTop(pcv[:, q:8:2, :], sc, biasc[:, q:8:2, :], ALU.add))
                do(V.tensor_reduce(small[:, 16:24], pcv, AX.X, ALU.max))
                do(TTop(pcv, pcv, bc(small[:, 16:24], NCMP), ALU.subtract), cmp_shift)
                dve.wait_ge(cmp_exp, l + 1)
                do(V.tensor_reduce(small[:, 16:24], pcv, AX.X, ALU.add))
                do(V.reciprocal(small[:, 16:24], small[:, 16:24]))
                g0 = ng[:, :, 0:12].rearrange("p t (h c) -> p t h c", c=3)[:, :, :, 0]
                s3 = small[:, 16:24].rearrange("p (t h) -> p t h", t=TT)
                do(TTop(s3, s3, g0, ALU.mult))
                do(TTop(pcv, pcv, bc(small[:, 16:24], NCMP), ALU.mult))
                for tt in range(TT):
                    valid = cst("valid_cmp")[:, NCMP * tt:NCMP * tt + NCMP].rearrange("p (o n) -> p o n", o=1).to_broadcast([128, H, NCMP])
                    do(TTop(pc[:, tt, :, 0:NCMP], pc[:, tt, :, 0:NCMP], valid, ALU.mult), cmp_probs if tt else None)
                dve.wait_ge(cmp_pT, l + 1)
                do(V.tensor_copy(pcT[:, :, :], ps[3][:, 0:256].rearrange("p (t n) -> p t n", t=TT)), cmp_pT_evac)
                dve.wait_ge(cmp_out, l + 1)
                do(TTop(mix[:, :, 768:1024], mix[:, :, 768:1024], ps[2][:, :].rearrange("p (t n) -> p t n", t=TT), ALU.add), mix_ready)
                for k in VEC_CHUNKS:
                    dve.wait_ge(mixT_done, KC * l + (k | 1) + 1)
                    do(TS(hT[:, k, :], ps[k // 2][:, 256 * (k % 2):256 * (k % 2) + 256], prm(l, "out_g")[:, k:k + 1], None, ALU.mult), mixT_vec)
                for half in range(2):
                    for tt in range(TT):
                        dve.wait_ge(wout_done, 4 * l + 2 * half + tt + 1)
                        xs = x[:, tt, 512 * half:512 * half + 512]
                        do(TTop(wide[:, 0:512], ps[4 + 2 * half + tt][:, :], gate[:, 0, 512 * half:512 * half + 512], ALU.mult))
                        do(TTop(xs, xs, wide[:, 0:512], ALU.add), x_mixed if (half, tt) == (1, 1) else None)

            def swiglu(f, units, ntt, base, do):
                for j in range(len(units) * ntt):
                    w = units[j // ntt][1]
                    sg, hb = hsig[:, 0:w], hbuf[:, j % 2, 0:w]
                    dve.wait_ge(f["exp"], base + j + 1)
                    do(TS(sg, sg, 1.0, None, ALU.add))
                    do(V.reciprocal(sg, sg))
                    if j >= 2:
                        dve.wait_ge(f["T"], base + j - 1)
                    do(TTop(hb, ps[4][:, 0:w], sg, ALU.mult))
                    dve.wait_ge(f["u"], base + j + 1)
                    do(TTop(hb, hb, ps[5][:, 0:w], ALU.mult), f["h"])

            def add_residual(tt, half, y):
                xs, g = x[:, tt, 512 * half:512 * half + 512], gate[:, 1, 512 * half:512 * half + 512]
                do(TTop(wide[:, 0:512], y, g, ALU.mult))
                do(TTop(xs, xs, wide[:, 0:512], ALU.add), x_final if (tt, half) == (1, 1) else None)

            mixer(0)
            normalise(1)
            modulate(1, 1)
            swiglu(ffn, FF_UNITS, TT, 0, do)
            dve.wait_ge(ffn["y"], 1)
            for tt in range(TT):
                for half in range(2):
                    add_residual(tt, half, ps[2 * tt + half][:, :])
            dve.sem_inc(ffn["y_read"], 1)
            mixer(1)
            normalise(3)
            modulate(3, 1)
            dve.wait_ge(router_done, 1)
            for tt in range(TT):
                do(TTop(lg[:, tt, :], ps[7][:, 8 * tt:8 * tt + 8], prm(1, "router_b"), ALU.add))
                do(V.max(top8[:, tt, :], lg[:, tt, :]))
                do(V.max_index(topi[:, tt, :], top8[:, tt, :], lg[:, tt, :]))
            do(V.tensor_copy(topf[:, :, :], topi[:, :, :]))
            do(TTop(tw[:, :, 0:1], top8[:, :, 1:2], top8[:, :, 0:1], ALU.subtract), router_shift)
            dve.wait_ge(router_exp, 1)
            do(TS(tw[:, :, 1:2], tw[:, :, 0:1], 1.0, None, ALU.add))
            do(V.reciprocal(tw[:, :, 1:2], tw[:, :, 1:2]))
            do(TTop(tw[:, :, 2:3], tw[:, :, 0:1], tw[:, :, 1:2], ALU.mult))
            for tt in range(TT):
                do(TS(wts[:, tt, :], cst("iota8"), topf[:, tt, 0:1], tw[:, tt, 1:2], ALU.is_equal, ALU.mult))
                do(TS(wtmp[:, :], cst("iota8"), topf[:, tt, 1:2], tw[:, tt, 2:3], ALU.is_equal, ALU.mult))
                do(TTop(wts[:, tt, :], wts[:, tt, :], wtmp[:, :], ALU.add))
            do(V.memset(yacc[:, :, :], 0.0))
            steps = TT * len(FE_UNITS)
            per = 3 * steps + 4
            with dve.Fori(0, N_EXP) as e:
                doe = Ordered(dve, moe_vec)
                doe.base[id(moe_vec)] = e * per
                doe.base[id(moe["h"])] = e * steps
                swiglu(moe, FE_UNITS, TT, e * steps, doe)
                dve.wait_ge(moe["y"], e + 1)
                for tt in range(TT):
                    for half in range(2):
                        ya = yacc[:, tt, 512 * half:512 * half + 512]
                        doe(STT(ya, ps[2 * tt + half][:, :], wts[:, tt, bass.ds(e, 1)], ya, ALU.mult, ALU.add))
                assert doe.n[id(moe_vec)] == per
                dve.sem_inc(moe["y_read"], 1)
            for tt in range(TT):
                for half in range(2):
                    add_residual(tt, half, yacc[:, tt, 512 * half:512 * half + 512])


_RAW = ["x", "ada_w", "ada_b", "w_in", "w_out", "rel_bias", "nsa_cmp_wk", "nsa_cmp_wv", "ffn_wg", "ffn_wu", "ffn_wd",
        "moe_router_w", "moe_wg", "moe_wu", "moe_wd"]


def constants():
    import math

    import numpy as np
    f = np.float32
    c = np.zeros((128, CONST_W), f)

    def put(name, a):
        at, w = CONST[name]
        assert a.shape[1] == w, name
        c[:a.shape[0], at:at + w] = a

    p, j = np.arange(128)[:, None], np.arange(128)[None, :]
    zero = np.zeros((128, 128), f)
    big = f(-1e30)
    put("ident", np.eye(128, dtype=f))
    put("ones", np.ones((128, 1), f))
    put("minus_ones", -np.ones((128, 1), f))
    put("minus_tri", np.where(p >= j, f(-1), f(0)))
    for name, m in (("causal", j > p), ("causal_T", j < p), ("strict_T", j <= p)):
        d = np.where(m, big, f(0))
        put(name, np.concatenate([d, zero, d], 1))
    dist = 255 - np.arange(512)
    n = np.maximum(dist, 0)
    large = 16 + (np.log(np.maximum(n, 1).astype(f) / f(16)) / f(math.log(128 / 16)) * f(16)).astype(np.int32)
    bucket = np.where(n < 16, n, np.minimum(large, 31))
    onehot = ((np.arange(32)[:, None] == bucket[None, :]).astype(f))
    future = np.ascontiguousarray(np.broadcast_to(np.where(dist < 0, big, f(0)), (H, 512)))
    ends = 16 * np.arange(NCMP) + 31
    put("valid_cmp", np.concatenate([(ends[None, :] <= p + 128 * tt).astype(f) for tt in range(TT)], 1))
    put("iota8", np.broadcast_to(np.arange(8, dtype=f), (128, 8)))
    return c, onehot, future


def parameters(i):
    import numpy as np
    out = np.zeros((DEPTH, 128, PAR_W), np.float32)
    for l in range(DEPTH):
        def at(name, p0, p1, k0=0, k1=None):
            a, w = PAR[name]
            return out[l, p0:p1, a + k0:a + (w if k1 is None else k1)]
        at("norm1", 0, 128)[:] = i["norm1_g"][l].reshape(8, 128).T
        at("norm2", 0, 128)[:] = i["norm2_g"][l].reshape(8, 128).T
        at("conv", 0, 128)[:] = i["mlstm_conv_w"][l].reshape(4, 4, 128).transpose(2, 1, 0).reshape(128, 16)
        at("gate_bias", 0, 4)[:, 0] = i["mlstm_gate_b"][l, 4:8]
        at("gate_bias", 4, 8)[:, 0] = i["fox_f_b"][l]
        at("gate_bias", 32, 36)[:, 0] = i["mlstm_gate_b"][l, 0:4]
        at("out_g", 0, 128)[:] = 1
        at("out_g", 0, 128, 0, 2)[:] = i["mlstm_out_g"][l].reshape(2, 128).T
        for p0 in (0, 64):
            at("fox_q", p0, p0 + 64)[:, 0] = i["fox_q_g"][l]
            at("fox_k", p0, p0 + 64)[:, 0] = i["fox_k_g"][l]
            at("nsa_q", p0, p0 + 64)[:, 0] = i["nsa_q_g"][l]
            at("nsa_k", p0, p0 + 64)[:] = i["nsa_k_g"][l][[0, 1, 2] if p0 == 0 else [0, 2, 1]].T
        at("cmp_pos", 0, 64)[:] = i["nsa_cmp_pos"][l].T
        at("cmp_pos", 64, 128)[:] = i["nsa_cmp_pos"][l].T
        at("nsa_gate_b", 0, 128)[:] = i["nsa_gate_b"][l][None]
        if l % 2:
            at("router_b", 0, 128)[:] = i["moe_router_b"][l // 2][None]
        at("ada_b", 0, 128)[:] = i["ada_b"][l].reshape(48, 128).T
    return out


def kernel(**inputs):
    import numpy as np
    import concourse.bacc as bacc
    from concourse.bass_utils import run_bass_kernel_spmd

    a = {n: np.ascontiguousarray(v) for n, v in inputs.items()}
    w_in = a["w_in"]
    gates = np.zeros((DEPTH, D, 48), w_in.dtype)
    gates[:, :, 0:4] = w_in[:, :, 1028:1032]
    gates[:, :, 4:8] = w_in[:, :, 1800:1804]
    gates[:, :, 32:36] = w_in[:, :, 1024:1028]
    gates[:, :, 36:48] = w_in[:, :, 3212:3224]
    arrays = {n: a[n] for n in _RAW}
    arrays["reverse"] = np.ascontiguousarray(np.eye(128, dtype=np.float32)[::-1])
    arrays["c_cols"] = np.ascontiguousarray(a["c"].reshape(KC, 128).T)
    arrays["w_gates"] = gates
    arrays["const"], arrays["onehot"], arrays["future"] = constants()
    arrays["par"] = parameters(a)

    nc = bacc.Bacc("TRN2", target_bir_lowering=False, num_devices=1)
    t = {n: nc.dram_tensor("in_" + n, v.shape, mybir.dt.from_np(v.dtype), kind="ExternalInput").ap() for n, v in arrays.items()}
    out = nc.dram_tensor("out", (1, S, D), F32, kind="ExternalOutput").ap()
    program(nc, t, out)
    r = run_bass_kernel_spmd(nc, [{"in_" + n: v for n, v in arrays.items()}], core_ids=[0])
    return r.results[0]["out"]
```

```python
from contextlib import ExitStack

import concourse.bass as bass
from concourse import mybir

F32 = mybir.dt.float32
U32 = mybir.dt.uint32
ALU = mybir.AluOpType
ACT = mybir.ActivationFunctionType
AX = mybir.AxisListType

D = 1024
KC = D // 128
TT = 2
S = 256
DEPTH = 2
H = 4
DH = 64
W_IN = 3224
D_FF = 2816
N_EXP = 8
D_FE = 3584
EPS = 1e-6
NCMP = 15
RING = 7
LOADS = 21
BLK = 128
OVER = 3
SLOT = KC * 512
ACT_CHUNKS, VEC_CHUNKS = (0, 1, 4, 5), (2, 3, 6, 7)
CONST = {}
_at = 0
for _n, _w in (("ident", 128), ("ones", 1), ("minus_ones", 1), ("minus_tri", 128), ("causal", 384),
               ("causal_T", 384), ("strict_T", 384), ("valid_cmp", 30), ("iota", 128)):
    CONST[_n] = (_at, _w)
    _at += _w
CONST_W = _at
PAR = {}
_at = 0
for _n, _w in (("norm1", 8), ("norm2", 8), ("conv", 16), ("gate_bias", 1), ("out_g", 8), ("fox_q", 1),
               ("fox_k", 1), ("nsa_q", 1), ("nsa_k", 3), ("cmp_pos", 32), ("nsa_gate_b", 12),
               ("router_b", 8), ("ada_b", 48)):
    PAR[_n] = (_at, _w)
    _at += _w
PAR_W = _at
WIN = ((0, 512), (512, 512), (1032, 512), (1544, 256), (1804, 512), (2316, 512), (2828, 384))
FF_UNITS = tuple((384 * u, 384 if u < 6 else 512) for u in range(7))
FE_UNITS = tuple((512 * u, 512) for u in range(7))
GROUPS = [(None, 0)] + [(c, g) for c in range(6) for g in range(2)] + [(6, g) for g in range(3)]
NG = len(GROUPS)
ADA_AFTER = {6: 4, 7: 5, 8: 6, 9: 7, 10: 8, 11: 9, 12: 10, 13: 11}
HEADS = [(k, h) for k in ("mlstm", "fox", "stick", "sel", "win") for h in range(H)]
NH = len(HEADS)


def count(kinds, i):
    return sum(k in kinds for k, _ in HEADS[:i + 1])


SOFT = ("fox", "sel", "win")
BKINDS = SOFT + ("stick",)
PKINDS = SOFT + ("mlstm",)
N_B, N_P, N_STICK = count(BKINDS, NH), count(PKINDS, NH), H
ADA, WOUT = [("ada", c) for c in range(12)], [("wout", 0), ("wout", 1)]
WINS = [("win", c) for c in range(7)]
SEQ = [(0,) + k for k in ADA[:4] + WINS[:3] + ADA[4:6] + WINS[3:4] + ADA[6:8] + WINS[4:5] + ADA[8:10]
       + WINS[5:6] + ADA[10:] + WINS[6:] + WOUT]
for _u in range(7):
    SEQ += [(0, "ffn", 3 * _u + j) for j in range(3)] + [(1,) + k for k in ADA[2 * _u:2 * _u + 2]]
SEQ += [(1,) + k for k in WINS + WOUT]
AT = {k: n for n, k in enumerate(SEQ)}
FIRST_EXPERT = len(SEQ)
assert FIRST_EXPERT % RING == 0 and LOADS % RING == 0


class Step:

    def __init__(self, w, tile, y, loads, rounds, first, last, begin, end):
        self.w, self.tile, self.y, self.loads, self.rounds = w, tile, y, loads, rounds
        self.first, self.last, self.begin, self.end = first, last, begin, end


def dense_steps():
    return [Step(w, tt, 2 * tt, [AT[(0, "ffn", 3 * u + p)] for p in range(3)], 0, tt == 0, tt == TT - 1, u == 0, u == 6)
            for u, (_, w) in enumerate(FF_UNITS) for tt in range(TT)]


def expert_steps(tile, rounds):
    return [Step(w, tile, 0, [3 * u + p for p in range(3)], rounds, True, True, u == 0, u == 6)
            for u, (_, w) in enumerate(FE_UNITS)]


class Ordered:

    def __init__(self, eng, own):
        self.eng, self.own, self.n, self.base = eng, own, {}, {}

    def __call__(self, ins, sem=None):
        sem = self.own if sem is None else sem
        key = id(sem)
        self.n[key] = self.n.get(key, 0) + 1
        ins.then_inc(sem, 1)
        self.eng.wait_ge(sem, self.n[key] + self.base.get(key, 0))

    def also(self, sem):
        self.n[id(sem)] = self.n.get(id(sem), 0) + 1
        self.eng.sem_inc(sem, 1)


def program(nc, t, out):
    ctx = ExitStack()
    with ctx:
        def sb(name, shape, dt=F32):
            return ctx.enter_context(nc.sbuf_tensor(name, shape, dt))

        def sem(name):
            return ctx.enter_context(nc.semaphore(name))

        ring = sb("ring", [128, RING, SLOT])
        wide = sb("wide", [128, 512])
        x = sb("x_res", [128, TT, D])
        xn = sb("x_norm", [128, TT, D])
        mix = xn
        hT = sb("h_T", [128, KC, S])
        const = sb("const", [128, CONST_W])
        par = sb("par", [128, DEPTH, PAR_W])
        bias = sb("rel_bias_tiles", [128, H, 384])
        biasc = sb("rel_bias_cmp", [128, TT * H, NCMP])
        table = sb("table", [32, H])
        onehot, future, relrow = (hT[0:p, 2 * k:2 * k + 2, :].rearrange("p a n -> p (a n)") for k, p in enumerate((32, H, H)))
        negm = sb("neg_m_run", [H, S])
        ccol = sb("c_col", [128, KC])
        cond = sb("cond", [128, KC])
        acc = sb("ada_acc", [128, 2, 512])
        modc = sb("mod_cols", [128, 48])
        scaleA = sb("mod_scale", [128, 2, KC])
        gate = sb("gate_rows", [128, 2, D])
        cmp_region = sb("cmp_region", [128, 32 * DH])
        cmpw = cmp_region[:, :].rearrange("p (j d) -> p j d", d=DH)
        nT = cmp_region[:, 0:4 * S].rearrange("p (v n) -> p v n", n=S)
        yacc = cmp_region[:, :].rearrange("p (t n) -> p t n", t=TT)
        pcT = cmp_region[:, 6 * S:7 * S].rearrange("p (t n) -> p t n", t=TT)
        small = sb("small", [128, 64])
        ss = sb("sumsq", [128, 32])
        rs = sb("rstd", [128, 32])
        prob = sb("prob", [128, 2, 384])
        probT = sb("prob_T", [128, 2, 384])
        pf, pTf = (a[:, :, :].rearrange("p a n -> p (a n)") for a in (prob, probT))
        graw, gz = wide[0:36, 0:S], wide[0:8, S:2 * S]
        gl, ig0, nmrow = pTf[0:8, 0:S], pTf[0:H, S:2 * S], pTf[0:H, 2 * S:3 * S]
        ucap = pf[0:H, 2 * S:3 * S]
        reverse = pf[:, 384:512]
        wgate = pf[:, 0:KC * 48].rearrange("p (k n) -> p k n", k=KC)
        cumf = sb("cum_logf", [8, S])
        gcol = sb("gate_cols", [128, TT, 16])
        expnm = sb("exp_neg_m", [128, TT, H])
        ng = sb("nsa_gates", [128, TT, 16])
        qk_region = sb("m_s_region", [128, 4 * (3 + S)])
        qkraw = qk_region[:, :].rearrange("p (a n) -> p a n", a=4)
        sT = qk_region[:, 0:4 * S].rearrange("p (a n) -> p a n", a=4)
        hbuf = qk_region[:, 0:1024].rearrange("p (a n) -> p a n", a=2)
        mqkT = sb("m_qk_T", [128, 4, S])
        mv = sb("m_v", [128, TT, H, DH + 1])
        mo = sb("m_o", [128, TT, 256])
        mh = acc[:, 0, :].rearrange("p (t h d) -> p t h d", t=TT, h=H)
        fqk = xn[:, 0, :].rearrange("p (t v d) -> p t v d", t=TT, v=8)
        nqk = xn[:, 1, 0:896].rearrange("p (t v d) -> p t v d", t=TT, v=7)
        kvT = sb("cmp_kv_T", [128, S])
        fT = sb("f_qk_T", [128, 4, S])
        conv = fT
        negf = sb("neg_cum_logf", [8, S])
        fv = sb("f_v", [128, TT, 256])
        sv = sb("s_v", [128, TT, 256])
        hsig = sv[:, :, :].rearrange("p t n -> p (t n)")
        hbT = mqkT[:, :, :].rearrange("p (a b) n -> p a (b n)", a=2)
        nv = sb("n_v", [128, TT, 2, DH])
        cmpx = xn[:, 0, 0:32 * NCMP].rearrange("p (j n) -> p j n", n=NCMP)
        kcn = sb("k_cmp", [NCMP, 2, DH])
        kcT = sb("k_cmp_T", [128, NCMP])
        vpad = sb("v_cmp_T", [DH, H, 32])
        vblk = sb("v_cmp_blocks", [128, H, DH])
        pc = sb("p_cmp", [128, TT, H, 32])
        nmax = sb("neg_max", [128, 2, TT])
        lsum = sb("exp_sums", [128, 5, H, TT])
        rl = sb("inv_sums", [128, H, TT])
        rw = sb("router_w", [128, KC, N_EXP])
        topi = sb("top_index", [128, TT, 8], U32)
        at = [0]

        def listed(*shape):
            n = shape[-1]
            a = pf[:, at[0]:at[0] + (n if len(shape) == 1 else shape[0] * n)]
            at[0] += a.shape[-1]
            return a if len(shape) == 1 else a.rearrange("p (t n) -> p t n", t=shape[0])

        lg, top8, topf, tw = listed(TT, N_EXP), listed(TT, 8), listed(TT, 8), listed(TT, 4)
        wts = listed(TT, N_EXP + 1)
        picked = listed(TT, N_EXP)
        rank = listed(TT, N_EXP + 1)
        wtmp = listed(40)
        overi = sb("overflow_experts", [1, 8], mybir.dt.int32)
        pick = [acc[:, 0, 256 * q:256 * q + 256].rearrange("p (t n) -> p t n", t=TT) for q in range(2)]
        pickT = [acc[:, 1, 256 * q:256 * q + 256].rearrange("p (t n) -> p t n", t=TT) for q in range(2)]
        ysb = fT[:, :, :].rearrange("p a n -> p (a n)")
        scratch = nc.dram_tensor("rel_scratch", [H, 512], F32)

        ps = [ctx.enter_context(nc.psum_tensor(f"bank{i}", [128, 512], F32)) for i in range(8)]

        def cst(name, p=128):
            a, w = CONST[name]
            return const[0:p, a:a + w]

        def prm(l, name, p0=0, p1=128):
            a, w = PAR[name]
            return par[p0:p1, l, a:a + w]

        ident, ones = cst("ident"), cst("ones")
        ones_all, minus_all = (cst(n).to_broadcast([128, 128]) for n in ("ones", "minus_ones"))

        const_in = sem("const_in")
        rel_saved = sem("rel_saved")
        bias_in = sem("bias_in")
        bias_turned = sem("bias_turned")
        bias_ready = sem("bias_ready")
        layer_in = sem("layer_in")
        gate2_in = sem("gate2_in")
        router_in = sem("router_in")
        out_saved = sem("out_saved")
        ring_full = [sem(f"ring_full{i}") for i in range(RING)]
        ring_free = [sem(f"ring_free{i}") for i in range(RING)]
        vec_seq = sem("vec_seq")
        act_seq = sem("act_seq")
        pool_seq = sem("pool_seq")
        rel_row = sem("rel_row_psum")
        rel_ready = sem("rel_row_ready")
        cond_exp = sem("cond_exp")
        x_sumsq = sem("x_sumsq")
        xn_ready = sem("xn_ready")
        xT_done = sem("xT_done")
        mod_ready = sem("mod_ready")
        hT_act = sem("hT_act")
        hT_vec = sem("hT_vec")
        acc_ready = sem("acc_ready")
        acc_reduced = sem("acc_reduced")
        mod_evac = sem("mod_evac")
        proj_done = sem("proj_done")
        proj_evac = sem("proj_evac")
        gate_abs = sem("gate_abs")
        gate_ln = sem("gate_ln")
        gate_rows = sem("gate_rows_ready")
        gate_T = sem("gate_T")
        gate_cols = sem("gate_cols_ready")
        nm_exp = sem("nm_exp")
        conv_done = sem("conv_done")
        conv_exp = sem("conv_exp")
        mqk_ready = sem("mqk_ready")
        sumsq_ready = sem("sumsq_ready")
        rstd_ready = sem("rstd_ready")
        fox_norm = sem("fox_norm")
        fox_T = sem("fox_T")
        fox_T_evac = sem("fox_T_evac")
        nsa_norm = sem("nsa_norm")
        nsa_T = sem("nsa_T")
        nsa_T_evac = sem("nsa_T_evac")
        gates_exp = sem("gates_exp")
        cmpx_ready = sem("cmpx_ready")
        cmp_done = sem("cmp_done")
        kcn_ready = sem("kcn_ready")
        vpad_ready = sem("vpad_ready")
        kv_T = sem("kv_T")
        kv_T_evac = sem("kv_T_evac")
        cmp_scores = sem("cmp_scores")
        cmp_shift = sem("cmp_shift")
        cmp_exp = sem("cmp_exp")
        cmp_probs = sem("cmp_probs")
        cmp_pT = sem("cmp_pT")
        cmp_pT_evac = sem("cmp_pT_evac")
        cmp_out = sem("cmp_out")
        head_scores = sem("head_scores")
        head_free = [sem(f"head_free{i}") for i in range(2)]
        head_shift = [sem(f"head_shift{i}") for i in range(2)]
        head_exp = sem("head_exp")
        stick_sp = sem("stick_softplus")
        stick_masked = sem("stick_masked")
        head_second = sem("head_second")
        head_pT = sem("head_pT")
        head_pv = sem("head_pv")
        o_free = sem("o_free")
        mo_exp = sem("mo_exp")
        mix_ready = sem("mix_ready")
        mixT_done = sem("mixT_done")
        mixT_act = sem("mixT_act")
        mixT_vec = sem("mixT_vec")
        wout_done = sem("wout_done")
        x_mixed = sem("x_mixed")
        ffn = {n: sem("ffn_" + n) for n in ("g", "u", "tanh", "h", "T", "T_evac", "d", "seq")}
        moe, over = ({n: sem(f"{p}_{n}") for n in (
            "g", "u", "tanh", "h", "T", "T_evac", "d", "onehot", "turned", "turn_evac", "gathered", "in_act", "in_vec",
            "y_act", "y_vec", "scattered", "added", "act_seq", "vec_seq", "act_left",
            "vec_left")} for p in ("moe", "over"))
        picked_ready = sem("picked_ready")
        rank_done = sem("rank_done")
        over_ready = sem("over_ready")
        x_final = sem("x_final")
        router_done = sem("router_done")
        router_shift = sem("router_shift")
        router_exp = sem("router_exp")

        def slot_of(i):
            return i % RING

        def loaded(eng, n, base=0):
            eng.wait_ge(ring_full[slot_of(n)], base * 16 + 16 * (n // RING + 1))

        def slot_view(i, w):
            return ring[:, slot_of(i), 0:KC * w].rearrange("p (k n) -> p k n", k=KC)

        def slot_down(i, w):
            return ring[:, slot_of(i), 0:(w // 128) * D].rearrange("p (f n) -> p f n", n=D)

        block = ctx.enter_context(nc.Block())

        @block.sync
        def _(sp):
            sp.dma_start(const[:, :], t["const"]).then_inc(const_in, 16)
            sp.dma_start(par[:, :, :], t["par"].rearrange("l p n -> p l n")).then_inc(const_in, 16)
            sp.dma_start(onehot, t["onehot"]).then_inc(const_in, 16)
            sp.dma_start(reverse, t["reverse"]).then_inc(const_in, 16)
            sp.dma_start(future, t["future"]).then_inc(const_in, 16)
            sp.dma_start(table[:, :], t["rel_bias"]).then_inc(const_in, 16)
            sp.dma_start(ccol[:, :], t["c_cols"]).then_inc(const_in, 16)
            for tt in range(TT):
                sp.dma_start(x[:, tt, :], t["x"][0, tt * 128:tt * 128 + 128, :]).then_inc(const_in, 16)

            def put(n, dst, src, base=0):
                if n >= RING or not isinstance(base, int):
                    sp.wait_ge(ring_free[slot_of(n)], base + n // RING)
                sp.dma_start(dst, src).then_inc(ring_full[slot_of(n)], 16)

            def swiglu_load(n, m, c0, w, j, base=0):
                if j < 2:
                    put(n, slot_view(n, w), m[:, c0:c0 + w].rearrange("(k p) n -> p k n", p=128), base)
                else:
                    put(n, slot_down(n, w), m[c0:c0 + w, :].rearrange("(f p) n -> p f n", p=128), base)

            def side_loads(l):
                sp.dma_start(gate[:, 0, :], t["ada_b"][l:l + 1, 2 * D:3 * D].to_broadcast([128, D])).then_inc(layer_in, 16)
                sp.dma_start(wgate[:, :, :], t["w_gates"][l].rearrange("(k p) n -> p k n", p=128)).then_inc(layer_in, 16)
                sp.dma_start(cmpw[0:DH, :, :], t["nsa_cmp_wk"][l].rearrange("(j d) e -> d j e", d=DH)).then_inc(layer_in, 16)
                sp.dma_start(cmpw[DH:128, :, :], t["nsa_cmp_wv"][l].rearrange("(j d) e -> d j e", d=DH)).then_inc(layer_in, 16)

            for n, (l, kind, c) in enumerate(SEQ):
                if n == 4:
                    side_loads(0)
                if (l, kind, c) == (0, "ffn", 9):
                    sp.wait_ge(x_mixed, 1)
                    side_loads(1)
                if kind == "ffn":
                    c0, w = FF_UNITS[c // 3]
                    swiglu_load(n, t[("ffn_wg", "ffn_wu", "ffn_wd")[c % 3]][0], c0, w, c % 3)
                    continue
                c0, w = WIN[c] if kind == "win" else (512 * c, 512)
                m = t[{"ada": "ada_w", "win": "w_in", "wout": "w_out"}[kind]]
                put(n, slot_view(n, w), m[l, :, c0:c0 + w].rearrange("(k p) n -> p k n", p=128))
            sp.dma_start(rw[:, :, :], t["moe_router_w"][0].rearrange("(k p) n -> p k n", p=128)).then_inc(router_in, 16)
            experts = [t[n].rearrange("a e r c -> (a e r) c") for n in ("moe_wg", "moe_wu", "moe_wd")]

            def expert_loads(e, base):
                for u, (c0, w) in enumerate(FE_UNITS):
                    for j, rows in enumerate((D, D, D_FE)):
                        swiglu_load(3 * u + j, experts[j][bass.ds(e * rows, rows), :], c0, w, j, base)

            first = FIRST_EXPERT // RING
            with sp.Fori(0, N_EXP) as e:
                expert_loads(e, e * 3 + first)
            sp.wait_ge(over_ready, 1)
            n_over = sp.value_load(overi[0:1, OVER:OVER + 1], min_val=0, max_val=OVER)
            with sp.Fori(0, OVER) as i:
                with sp.If(i < n_over):
                    e = sp.value_load(overi[0:1, bass.ds(i, 1)], min_val=0, max_val=N_EXP - 1)
                    expert_loads(e, i * 3 + (first + 3 * N_EXP))
            sp.wait_ge(x_final, 2)
            for tt in range(TT):
                sp.dma_start(out[0, tt * 128:tt * 128 + 128, :], x[:, tt, :]).then_inc(out_saved, 16)
            sp.wait_ge(out_saved, 16 * TT)

        @block.gpsimd
        def _(pool):
            do = Ordered(pool, pool_seq)
            for a in (vpad[:, :, :], vblk[:, :, :], pc[:, :, :, :]):
                do(nc.gpsimd.memset(a, 0.0))
            do(nc.gpsimd.memset(mv[:, :, :, DH:DH + 1], 1.0))

        @block.scalar
        def _(act):
            do = Ordered(act, act_seq)
            act.wait_ge(const_in, 144)
            act.activation(cond[:, :], ccol[:, :], ACT.Exp, scale=-1.0).then_inc(cond_exp, 1)

            def rstd(n, p, cols, width):
                do(act.activation(small[0:p, 32:32 + cols], ss[0:p, 0:cols], ACT.Ln, scale=1.0 / width, bias=epsb[0:p, :]))
                return act.activation(rs[0:p, 0:cols], small[0:p, 32:32 + cols], ACT.Exp, scale=-0.5)

            def norm(l, which):
                n = 2 * l + which
                if n:
                    act.wait_ge(x_mixed if which else x_final, l + 1 if which else l)
                for tt in range(TT):
                    do(act.activation(dump, x[:, tt, :], ACT.Square, accum_out=ss[:, tt:tt + 1]))
                do(rstd(n, 128, TT, D), x_sumsq)
                if n == 0:
                    relative_bias()
                if n == 2:
                    act.dma_start(gate[:, 1, :], t["ada_b"][1:2, 5 * D:6 * D].to_broadcast([128, D])).then_inc(gate2_in, 16)
                act.wait_ge(mod_ready, n + 1)
                for k in ACT_CHUNKS:
                    act.wait_ge(xT_done, KC * n + (k | 1) + 1)
                    do(act.activation(hT[:, k, :], ps[k // 2][:, 256 * (k % 2):256 * (k % 2) + 256], ACT.Identity,
                                      scale=scaleA[:, which, k:k + 1], bias=modc[:, (24 if which else 0) + k:(24 if which else 0) + k + 1]), hT_act)

            def mixer(l):
                for n, (c, g) in enumerate(GROUPS):
                    act.wait_ge(proj_done, NG * l + n + 1)
                    b = ps[n % 4]
                    halves = b[:, :].rearrange("p (a n) -> p a n", a=2)
                    if c is None:
                        do(act.activation(graw[:, :], b[0:36, 0:S], ACT.Copy))
                        do(act.activation(ng[:, :, 0:12], b[:, 256:288].rearrange("p (a n) -> p a n", a=2)[:, :, 0:12], ACT.Copy), proj_evac)
                    elif c == 0:
                        do(act.activation(qkraw[:, 2 * g:2 * g + 2, 3:3 + S], halves, ACT.Copy), proj_evac)
                    elif c == 1:
                        do(act.activation(mv[:, g, :, 0:DH], b[:, 0:256].rearrange("p (h d) -> p h d", h=H), ACT.Copy))
                        do(act.activation(mo[:, g, :], b[:, 256:512], ACT.Copy), proj_evac)
                    elif c == 2:
                        do(act.activation(fqk[:, g, :, :], b[:, :].rearrange("p (h d) -> p h d", h=8), ACT.Copy), proj_evac)
                    elif c == 3:
                        do(act.activation(fv[:, g, :], b[:, 0:256], ACT.Copy), proj_evac)
                    elif c == 4:
                        do(act.activation(sT[:, 2 * g:2 * g + 2, :], halves, ACT.Copy, scale=1.0 if g else DH ** -0.5), proj_evac)
                    elif c == 5:
                        do(act.activation(sv[:, g, :], b[:, 0:256], ACT.Copy))
                        do(act.activation(nqk[:, g, 0:4, :], b[:, 256:512].rearrange("p (h d) -> p h d", h=H), ACT.Copy), proj_evac)
                    elif g == 0:
                        do(act.activation(kvT[:, :], b[:, 0:S], ACT.Copy), proj_evac)
                    else:
                        kv = b[:, 0:256].rearrange("p (a b d) -> p a b d", a=2, b=2)
                        do(act.activation(nqk[:, g - 1, 4:6, :], kv[:, :, 0, :], ACT.Copy))
                        do(act.activation(nqk[:, g - 1, 6, :], kv[:, 0, 0, :], ACT.Copy))
                        do(act.activation(nv[:, g - 1, :, :], kv[:, :, 1, :], ACT.Copy), proj_evac)
                    if n == 1:
                        act.wait_ge(gate_abs, l + 1)
                        do(act.activation(gl[:, :], gl[:, :], ACT.Exp, scale=-1.0))
                        do(act.activation(gl[:, :], gl[:, :], ACT.Ln, bias=1.0), gate_ln)
                    if n == 4:
                        act.wait_ge(conv_done, l + 1)
                        do(act.activation(mqkT[:, :, :], conv[:, :, :], ACT.Exp, scale=-1.0), conv_exp)
                        act.wait_ge(gate_cols, l + 1)
                        do(act.activation(expnm[:, :, :], gcol[:, :, 4:8], ACT.Exp), nm_exp)
                    if n == 9:
                        act.wait_ge(sumsq_ready, 4 * l + 1)
                        do(rstd(0, 128, 16, DH), rstd_ready)
                act.wait_ge(sumsq_ready, 4 * l + 2)
                do(rstd(0, 128, 14, DH), rstd_ready)
                do(act.activation(ng[:, :, 0:12], ng[:, :, 0:12], ACT.Exp, scale=-1.0), gates_exp)
                act.wait_ge(sumsq_ready, 4 * l + 3)
                do(rstd(0, NCMP, 1, DH), rstd_ready)

                def exp_shifted(i):
                    kind, h = HEADS[i]
                    act.wait_ge(head_shift[i % 2], NH // 2 * l + i // 2 + 1)
                    e = prob[:, i % 2, :]
                    if kind == "mlstm":
                        do(act.activation(e[:, 0:256], e[:, 0:256], ACT.Exp, bias=gcol[:, 0, h:h + 1]))
                        do(act.activation(e[:, 256:384], e[:, 256:384], ACT.Exp, bias=gcol[:, 1, h:h + 1]), head_exp)
                    elif kind == "stick":
                        do(act.activation(probT[:, i % 2, :], probT[:, i % 2, :], ACT.Exp), head_exp)
                    else:
                        for tt, (a, b) in enumerate(((0, 128), (128, 384))):
                            do(act.activation(e[:, a:b], e[:, a:b], ACT.Exp, bias=nmax[:, i % 2, tt:tt + 1],
                                              accum_out=lsum[:, i // H, h, tt:tt + 1]), head_exp if tt else None)

                for i in range(NH + 1):
                    if i < NH and HEADS[i][0] == "stick":
                        act.wait_ge(head_scores, NH * l + i + 1)
                        act.wait_ge(head_second, N_B * l + count(BKINDS, i - 2))
                        e = prob[:, i % 2, :]
                        do(act.activation(e, ps[i % 2][:, 0:384], ACT.Abs))
                        do(act.activation(e, e, ACT.Exp, scale=-1.0))
                        do(act.activation(e, e, ACT.Ln, bias=1.0), stick_sp)
                    if i >= 1 and HEADS[i - 1][0] == "stick":
                        exp_shifted(i - 1)
                    if i < NH and HEADS[i][0] != "stick":
                        exp_shifted(i)
                    if i == H + 2:
                        act.wait_ge(sumsq_ready, 4 * l + 4)
                        do(rstd(0, 128, 8, DH), rstd_ready)
                        do(act.activation(mo[:, :, :], mo[:, :, :], ACT.Exp, scale=-1.0), mo_exp)
                act.wait_ge(cmp_shift, l + 1)
                do(act.activation(pc[:, :, :, 0:NCMP], pc[:, :, :, 0:NCMP], ACT.Exp), cmp_exp)
                for k in ACT_CHUNKS:
                    act.wait_ge(mixT_done, KC * l + (k | 1) + 1)
                    do(act.activation(hT[:, k, :], ps[k // 2][:, 256 * (k % 2):256 * (k % 2) + 256], ACT.Copy,
                                      scale=prm(l, "out_g")[:, k:k + 1]), mixT_act)

            def swiglu(f, steps, base, do, after=lambda j: None):
                for j in range(len(steps) + 1):
                    if j < len(steps):
                        st = steps[j]
                        act.wait_ge(f["g"], base + j + 1)
                        if st.last:
                            act.sem_inc(ring_free[slot_of(st.loads[0])], 1)
                        if j:
                            act.wait_ge(f["h"], base + j)
                        do(act.activation(hsig[:, 0:st.w], ps[4][:, 0:st.w], ACT.Tanh, scale=0.5), f["tanh"])
                    if j:
                        w = steps[j - 1].w
                        act.wait_ge(f["T"], base + j)
                        if j >= 3:
                            act.wait_ge(f["d"], base + j - 2)
                        do(act.activation(hbT[:, (j - 1) % 2, 0:w], ps[6][:, 0:w], ACT.Copy), f["T_evac"])
                    after(j)

            def gathered_in(f, tile, count, do):
                act.wait_ge(f["gathered"], count)
                for k in range(4):
                    do(act.activation(hT[:, k, 128 * tile:128 * tile + 128], ps[2][:, 128 * k:128 * k + 128], ACT.Identity,
                                      scale=scaleA[:, 1, k:k + 1], bias=modc[:, 24 + k:25 + k]), f["in_act"] if k == 3 else None)

            def y_out(f, downs, do):
                act.wait_ge(f["d"], downs)
                do(act.activation(ysb[:, 0:512], ps[0][:, :], ACT.Copy), f["y_act"])

            epsb = small[:, 63:64]
            dump = fT[:, :, :].rearrange("p k n -> p (k n)")

            def relative_bias():
                act.wait_ge(rel_ready, 1)
                act.dma_start(scratch.ap(), relrow[:, :]).then_inc(rel_saved, 16)
                act.wait_ge(rel_saved, 16)
                sc = scratch.ap()
                for h in range(H):
                    for col, w, at in ((0, 128, 128), (128, 256, 0)):
                        src = bass.AP(sc.tensor, h * 512 + at, [[1, 128], [1, w]])
                        act.dma_start(bias[:, h, col:col + w], src).then_inc(bias_in, 16)
            act.dma_start(gate[:, 1, :], t["ada_b"][0:1, 5 * D:6 * D].to_broadcast([128, D])).then_inc(gate2_in, 16)
            act.wait_ge(vec_seq, 1)
            norm(0, 0)
            mixer(0)
            norm(0, 1)
            swiglu(ffn, dense_steps(), 0, do)
            norm(1, 0)
            mixer(1)
            norm(1, 1)
            act.wait_ge(router_shift, 1)
            do(act.activation(tw[:, :, 0:1], tw[:, :, 0:1], ACT.Exp), router_exp)
            gathered_in(moe, 0, 1, do)
            act.sem_inc(moe["y_act"], 1)
            with act.Fori(0, N_EXP // 2) as i:
                doe = Ordered(act, moe["act_seq"])
                doe.base = {id(moe["act_seq"]): i * 6, id(moe["tanh"]): i * 14, id(moe["T_evac"]): i * 14,
                            id(moe["in_act"]): i * 2 + 1, id(moe["y_act"]): i * 2 + 1}

                def after(j):
                    if j in (3, 10):
                        gathered_in(moe, 1 - j // 7, i * 2 + (j // 7 + 2), doe)
                    if j in (7, 14):
                        y_out(moe, i * 14 + j, doe)

                swiglu(moe, expert_steps(0, 0) + expert_steps(1, 0), i * 14, doe, after)
                assert doe.n[id(moe["act_seq"])] == 6
            act.wait_ge(over_ready, 1)
            n_over = act.value_load(overi[0:1, OVER:OVER + 1], min_val=0, max_val=OVER)
            with act.Fori(0, OVER) as i:
                with act.If(i < n_over):
                    doe = Ordered(act, over["act_seq"])
                    doe.base = {id(over["act_seq"]): i * 3, id(over["tanh"]): i * 7, id(over["T_evac"]): i * 7,
                                id(over["in_act"]): i, id(over["y_act"]): i}
                    gathered_in(over, 0, i + 1, doe)
                    swiglu(over, expert_steps(0, 0), i * 7, doe)
                    y_out(over, i * 7 + 7, doe)
                    act.sem_inc(over["act_left"], 1)
                    assert doe.n[id(over["act_seq"])] == 3

        @block.tensor
        def _(pe):
            mm = nc.tensor.matmul

            def transpose_norm(n):
                pe.wait_ge(xn_ready, n + 1)
                for k in range(KC):
                    for tt in range(TT):
                        o = ps[k // 2][:, 256 * (k % 2) + 128 * tt:256 * (k % 2) + 128 * tt + 128]
                        last = nc.tensor.transpose(o, xn[:, tt, 128 * k:128 * k + 128], ident)
                    last.then_inc(xT_done, 1)

            def ada_reduce(l, c):
                pe.wait_ge(acc_ready, 12 * l + c + 1)
                if l:
                    pe.wait_ge(mod_evac, 12 * l + c)
                elif c >= 2:
                    pe.wait_ge(mod_evac, c - 1)
                b = ps[7] if l else ps[6 + c % 2]
                if c in (4, 5, 10, 11):
                    last = mm(b[:, :], ones_all, acc[:, c % 2, :], start=True, stop=True)
                else:
                    for q in range(4):
                        last = mm(b[:, q:q + 1], acc[:, c % 2, 128 * q:128 * q + 128], ones, start=True, stop=True)
                last.then_inc(acc_reduced, 1)

            def mixer(l):
                transpose_norm(2 * l)
                for c in range(4) if l == 0 else (10, 11):
                    ada_reduce(l, c)
                pe.wait_ge(hT_act, 4 * (2 * l + 1))
                pe.wait_ge(hT_vec, 4 * (2 * l + 1))
                pe.wait_ge(layer_in, 64 * (l + 1))
                for n, (c, g) in enumerate(GROUPS):
                    b = ps[n % 4]
                    if n >= 4:
                        pe.wait_ge(proj_evac, NG * l + n - 3)
                    if c is None:
                        for k in range(KC):
                            mm(b[0:36, 0:S], wgate[:, k, 0:36], hT[:, k, :], start=k == 0, stop=k == KC - 1)
                        for tt in range(TT):
                            for k in range(KC):
                                last = mm(b[:, 256 + 16 * tt:268 + 16 * tt], hT[:, k, 128 * tt:128 * tt + 128], wgate[:, k, 36:48],
                                          start=k == 0, stop=k == KC - 1)
                        last.then_inc(proj_done, 1)
                        continue
                    i = AT[(l, "win", c)]
                    w = slot_view(i, WIN[c][1])
                    loaded(pe, i)
                    if c in (0, 4):
                        for q in range(2):
                            for k in range(KC):
                                last = mm(b[:, 256 * q:256 * q + 256], w[:, k, 128 * (2 * g + q):128 * (2 * g + q) + 128],
                                          hT[:, k, :], start=k == 0, stop=k == KC - 1)
                    elif c == 6 and g == 0:
                        for k in range(KC):
                            last = mm(b[:, 0:S], w[:, k, 0:128], hT[:, k, :], start=k == 0, stop=k == KC - 1)
                    else:
                        tt, c0 = (g - 1, 128) if c == 6 else (g, 0)
                        cols = 512 if WIN[c][1] == 512 else 256
                        for k in range(KC):
                            last = mm(b[:, 0:cols], hT[:, k, 128 * tt:128 * tt + 128], w[:, k, c0:c0 + cols],
                                      start=k == 0, stop=k == KC - 1)
                    last.then_inc(proj_done, 1)
                    if g == (2 if c == 6 else 1):
                        pe.wait_ge(proj_done, NG * l + n + 1)
                        pe.sem_inc(ring_free[slot_of(i)], 1)
                    if n == 4:
                        pe.wait_ge(gate_rows, l + 1)
                        for tt in range(TT):
                            for r, at, w_ in ((ucap, 0, 4), (nmrow, 4, 4), (cumf, 8, 8)):
                                last = nc.tensor.transpose(ps[5][:, 16 * tt + at:16 * tt + at + w_], r[0:w_, 128 * tt:128 * tt + 128],
                                                           ident[0:w_, 0:w_])
                        last.then_inc(gate_T, 1)
                    if (l, n) == (0, 2):
                        pe.wait_ge(bias_in, 8 * 16)
                        for h in range(H):
                            last = mm(ps[4 + h][:, 0:384], reverse, bias[:, h, :], start=True, stop=True)
                        last.then_inc(bias_turned, 1)
                        pe.wait_ge(bias_ready, 1)
                    if n in ADA_AFTER and l == 0:
                        ada_reduce(l, ADA_AFTER[n])
                    if n == 13:
                        pe.wait_ge(fox_norm, l + 1)
                        for a in range(2):
                            for q in range(2):
                                for tt in range(TT):
                                    v = 4 * a + 2 * q
                                    last = nc.tensor.transpose(ps[4 + a][:, 256 * q + 128 * tt:256 * q + 128 * tt + 128],
                                                               fqk[:, tt, v:v + 2, :].rearrange("p v d -> p (v d)"), ident)
                            last.then_inc(fox_T, 1)
                pe.wait_ge(mod_evac, 12 * l + 12)
                pe.wait_ge(cmpx_ready, l + 1)
                for j in range(32):
                    mm(ps[6][0:NCMP, 0:DH], cmpx[0:DH, j, :], cmpw[0:DH, j, :], start=j == 0, stop=j == 31)
                for j in range(32):
                    last = mm(ps[7][0:DH, 0:NCMP], cmpw[DH:128, j, :], cmpx[DH:128, j, :], start=j == 0, stop=j == 31)
                last.then_inc(cmp_done, 1)
                pe.wait_ge(nsa_norm, l + 1)
                pe.wait_ge(fox_T_evac, 2 * (l + 1))
                for a in range(2):
                    for q in range(2):
                        v = 2 * q if a == 0 else 4 + q
                        for tt in range(TT):
                            last = nc.tensor.transpose(ps[4 + a][:, 256 * q + 128 * tt:256 * q + 128 * tt + 128],
                                                       nqk[:, tt, v:v + 2, :].rearrange("p v d -> p (v d)"), ident)
                    last.then_inc(nsa_T, 1)
                pe.wait_ge(kcn_ready, l + 1)
                pe.wait_ge(vpad_ready, l + 1)
                nc.tensor.transpose(ps[6][:, 0:NCMP], kcn[:, :, :].rearrange("p a d -> p (a d)"), ident[0:NCMP, 0:NCMP])
                last = nc.tensor.transpose(ps[7][:, 0:DH], vpad[:, :, :].rearrange("p h n -> p (h n)"), ident[0:DH, 0:DH])
                last.then_inc(kv_T, 1)

                def first(i):
                    kind, h = HEADS[i]
                    b = ps[i % 2]
                    if i >= 2:
                        pe.wait_ge(head_free[i % 2], NH // 2 * l + i // 2)
                    elif i == 0:
                        pe.wait_ge(proj_evac, NG * l + NG)
                        pe.wait_ge(mqk_ready, l + 1)
                    if kind in ("mlstm", "stick"):
                        T_ = mqkT if kind == "mlstm" else sT
                        p0 = DH * (h % 2)
                        q, k = T_[p0:p0 + DH, h // 2, :], T_[p0:p0 + DH, 2 + h // 2, :]
                        mm(b[:, 0:256], k[:, 0:128], q, start=True, stop=False, skip_group_check=True)
                        last = mm(b[:, 256:384], k[:, 128:256], q[:, 128:256], start=False, stop=True, skip_group_check=True)
                        if kind == "mlstm":
                            last = mm(ps[2 + i % 2][:, 0:256], ident[0:H, h:h + 1].to_broadcast([H, 128]), negm[:, :],
                                      start=True, stop=True)
                    else:
                        r = slice(DH * (h % 2), DH * (h % 2) + DH)
                        if kind == "fox":
                            q, k = fT[r, h // 2, :], fT[r, 2 + h // 2, :]
                        else:
                            q, k = nT[r, h // 2, :], nT[r, 2 + ((h % 2) ^ (kind == "win")), :]
                        fox = kind == "fox"
                        mm(b[:, 0:128], q[:, 0:128], k[:, 0:128], start=True, stop=not fox, skip_group_check=True)
                        last = mm(b[:, 128:384], q[:, 128:256], k, start=False, stop=not fox, skip_group_check=True)
                        if fox:
                            sel = ident[0:8, H + h:H + h + 1].to_broadcast([8, 128])
                            mm(b[:, 0:128], sel, negf[:, 0:128], start=False, stop=True, skip_group_check=True)
                            last = mm(b[:, 128:384], sel, negf[:, :], start=False, stop=True, skip_group_check=True)
                    last.then_inc(head_scores, 1)

                def second(i):
                    kind, h = HEADS[i]
                    if kind == "mlstm":
                        return
                    e = prob[:, i % 2, :]
                    if kind == "stick":
                        pe.wait_ge(stick_masked, N_STICK * l + h + 1)
                        b = ps[i % 2]
                        tri = cst("minus_tri")
                        mm(b[:, 0:256], tri, e[:, 0:256], start=False, stop=False, skip_group_check=True)
                        mm(b[:, 128:256], minus_all, e[:, 256:384], start=False, stop=False, skip_group_check=True)
                        last = mm(b[:, 256:384], tri, e[:, 256:384], start=False, stop=True, skip_group_check=True)
                    else:
                        pe.wait_ge(head_exp, NH * l + i + 1)
                        for q in range(3):
                            last = nc.tensor.transpose(ps[2 + i % 2][:, 128 * q:128 * q + 128], e[:, 128 * q:128 * q + 128], ident)
                    last.then_inc(head_second, 1)

                def third(i):
                    kind, h = HEADS[i]
                    gi = i // H
                    if kind == "stick":
                        pe.wait_ge(head_exp, NH * l + i + 1)
                    else:
                        pe.wait_ge(head_pT, N_P * l + count(PKINDS, i))
                    if h == 0:
                        if gi >= 2:
                            pe.wait_ge(o_free, 5 * l + gi - 1)
                        elif gi == 0:
                            pe.wait_ge(nsa_T_evac, 2 * l + 2)
                        else:
                            pe.wait_ge(kv_T_evac, l + 1)
                    if kind == "mlstm":
                        v = [mv[:, tt, h, :] for tt in range(TT)]
                    elif kind in ("fox", "stick"):
                        v = [(fv if kind == "fox" else sv)[:, tt, DH * h:DH * h + DH] for tt in range(TT)]
                    else:
                        v = [nv[:, tt, int(kind == "win"), :] for tt in range(TT)]
                    w = v[0].shape[-1]
                    pt = probT[:, i % 2, :]
                    o = [ps[4 + 2 * (gi % 2) + tt][:, w * h:w * h + w] for tt in range(TT)]
                    mm(o[0], pt[:, 0:128], v[0], start=True, stop=True)
                    mm(o[1], pt[:, 128:256], v[0], start=True, stop=False)
                    last = mm(o[1], pt[:, 256:384], v[1], start=False, stop=True)
                    last.then_inc(head_pv, 1)

                for i in range(NH + 2):
                    if i < NH:
                        first(i)
                    if 0 <= i - 1 < NH:
                        second(i - 1)
                    if i >= 2:
                        third(i - 2)

                for b in range(2):
                    pe.wait_ge(head_free[b], NH // 2 * (l + 1))
                for tt in range(TT):
                    for h in range(H):
                        c0 = 16 * (2 * tt + h // 2)
                        r = slice(DH * (h % 2), DH * (h % 2) + DH)
                        last = mm(ps[h % 2][:, c0:c0 + NCMP], nT[r, h // 2, 128 * tt:128 * tt + 128], kcT[r, :], start=True, stop=True)
                last.then_inc(cmp_scores, 1)
                pe.wait_ge(cmp_probs, l + 1)
                for tt in range(TT):
                    last = nc.tensor.transpose(ps[3][:, 128 * tt:128 * tt + 128], pc[:, tt, :, :].rearrange("p h n -> p (h n)"), ident)
                last.then_inc(cmp_pT, 1)
                pe.wait_ge(cmp_pT_evac, l + 1)
                for tt in range(TT):
                    last = mm(ps[2][:, 256 * tt:256 * tt + 256], pcT[:, tt, :], vblk[:, :, :].rearrange("p h d -> p (h d)"),
                              start=True, stop=True)
                last.then_inc(cmp_out, 1)

                pe.wait_ge(mix_ready, l + 1)
                for k in range(KC):
                    for tt in range(TT):
                        o = ps[k // 2][:, 256 * (k % 2) + 128 * tt:256 * (k % 2) + 128 * tt + 128]
                        last = nc.tensor.transpose(o, mix[:, tt, 128 * k:128 * k + 128], ident)
                    last.then_inc(mixT_done, 1)
                pe.wait_ge(mixT_act, 4 * (l + 1))
                pe.wait_ge(mixT_vec, 4 * (l + 1))
                for half in range(2):
                    i = AT[(l, "wout", half)]
                    loaded(pe, i)
                    for tt in range(TT):
                        for k in range(KC):
                            last = mm(ps[4 + 2 * half + tt][:, :], hT[:, k, 128 * tt:128 * tt + 128], slot_view(i, 512)[:, k, :],
                                      start=k == 0, stop=k == KC - 1)
                        last.then_inc(wout_done, 1)
                    pe.wait_ge(wout_done, 4 * l + 2 * half + 2)
                    pe.sem_inc(ring_free[slot_of(i)], 1)

            def swiglu(f, steps, base, before_up=lambda j: None, before_down=lambda j: None, after=lambda j: None):
                def up(j, part):
                    st = steps[j]
                    n, w = st.loads[part], st.w
                    if st.first:
                        loaded(pe, n, st.rounds)
                    if j:
                        pe.wait_ge(f["h"], base + j)
                    for k in range(KC):
                        last = mm(ps[4 + part][:, 0:w], hT[:, k, 128 * st.tile:128 * st.tile + 128], slot_view(n, w)[:, k, :],
                                  start=k == 0, stop=k == KC - 1)
                    last.then_inc(f["gu"[part]], 1)

                def turn(j):
                    pe.wait_ge(f["h"], base + j + 1)
                    for q in range(steps[j].w // 128):
                        last = nc.tensor.transpose(ps[6][:, 128 * q:128 * q + 128], hbuf[:, j % 2, 128 * q:128 * q + 128], ident)
                    last.then_inc(f["T"], 1)

                def down(j):
                    st = steps[j]
                    nf = st.w // 128
                    if st.first:
                        loaded(pe, st.loads[2], st.rounds)
                    pe.wait_ge(f["T_evac"], base + j + 1)
                    for half in range(2):
                        for q in range(nf):
                            last = mm(ps[st.y + half][:, :], hbT[:, j % 2, 128 * q:128 * q + 128],
                                      slot_down(st.loads[2], st.w)[:, q, 512 * half:512 * half + 512],
                                      start=st.begin and q == 0, stop=st.end and q == nf - 1)
                    last.then_inc(f["d"], 1)

                def free_down(j):
                    if steps[j].last:
                        pe.wait_ge(f["d"], base + j + 1)
                        pe.sem_inc(ring_free[slot_of(steps[j].loads[2])], 1)

                for j in range(len(steps) + 1):
                    if j < len(steps):
                        before_up(j)
                        up(j, 0)
                    if j >= 2:
                        free_down(j - 2)
                    if j:
                        turn(j - 1)
                    if j < len(steps):
                        up(j, 1)
                    if j:
                        before_down(j - 1)
                        down(j - 1)
                    after(j)
                free_down(len(steps) - 1)

            def gather(f, q, count, added=None):
                pe.wait_ge(f["onehot"], count)
                for tt in range(TT):
                    last = nc.tensor.transpose(ps[7][:, 128 * tt:128 * tt + 128], pick[q][:, tt, :], ident)
                last.then_inc(f["turned"], 1)
                if added is not None:
                    pe.wait_ge(f["added"], added)
                for k in range(KC):
                    for tt in range(TT):
                        last = mm(ps[2 + k // 4][:, 128 * (k % 4):128 * (k % 4) + 128], xn[:, tt, 128 * k:128 * k + 128],
                                  pick[q][:, tt, :], start=tt == 0, stop=tt == TT - 1)
                last.then_inc(f["gathered"], 1)

            def scatter(f, q, half, y_count, turns, added=None):
                pe.wait_ge(f["y_vec" if half else "y_act"], y_count)
                pe.wait_ge(f["turn_evac"], turns)
                if added is not None:
                    pe.wait_ge(f["added"], added)
                for tt in range(TT):
                    last = mm(ps[2 + tt][:, :], pickT[q][:, tt, :], ysb[:, 512 * half:512 * half + 512], start=True, stop=True)
                last.then_inc(f["scattered"], 1)

            pe.wait_ge(const_in, 144)
            mm(ps[0][0:H, :], table[:, :], onehot, start=True, stop=True).then_inc(rel_row, 1)
            pe.wait_ge(rel_ready, 1)
            mixer(0)
            transpose_norm(1)
            pe.wait_ge(hT_act, 8)
            pe.wait_ge(hT_vec, 8)
            swiglu(ffn, dense_steps(), 0, after=lambda j: ada_reduce(1, j - 2) if 2 <= j < 12 else None)
            mixer(1)
            transpose_norm(3)
            pe.wait_ge(hT_act, 16)
            pe.wait_ge(hT_vec, 16)
            pe.wait_ge(router_in, 16)
            for tt in range(TT):
                for k in range(KC):
                    last = mm(ps[7][:, 8 * tt:8 * tt + 8], hT[:, k, 128 * tt:128 * tt + 128], rw[:, k, :], start=k == 0, stop=k == KC - 1)
            last.then_inc(router_done, 1)
            pe.wait_ge(picked_ready, 1)
            for tt in range(TT):
                c = ps[6][:, 8 * tt:8 * tt + 8]
                mm(c, ones_all, picked[:, 0, :], start=True, stop=False)
                if tt:
                    mm(c, ones_all, picked[:, 1, :], start=False, stop=False)
                mm(c, cst("minus_tri"), picked[:, tt, :], start=False, stop=True)
            for tt in range(TT):
                last = mm(ps[6][:, 16:24], ones_all, picked[:, tt, :], start=tt == 0, stop=tt == TT - 1)
            last.then_inc(rank_done, 1)
            gather(moe, 0, 1)
            first = FIRST_EXPERT // RING
            with pe.Fori(0, N_EXP // 2) as i:
                def before_up(j):
                    if j in (0, 7):
                        pe.wait_ge(moe["in_act"], i * 2 + (j // 7 + 1))
                        pe.wait_ge(moe["in_vec"], i * 2 + (j // 7 + 1))

                def before_down(j):
                    if j in (0, 7):
                        pe.wait_ge(moe["y_act"], i * 2 + (j // 7 + 1))
                        pe.wait_ge(moe["y_vec"], i * 2 + (j // 7 + 1))

                def after(j):
                    q, u = divmod(j, 7)
                    if j == 14:
                        return
                    if u == 1:
                        scatter(moe, 1 - q, 0, i * 2 + (q + 1), i * 2 + (q + 1))
                    if u == 2:
                        scatter(moe, 1 - q, 1, i * 2 + (q + 1), i * 2 + (q + 1), i * 4 + (2 * q + 1))
                    if u == 3:
                        gather(moe, 1 - q, i * 2 + (q + 2), i * 4 + (2 * q + 2))

                swiglu(moe, expert_steps(0, i * 6 + first) + expert_steps(1, i * 6 + (first + 3)), i * 14, before_up, before_down, after)
            for half in range(2):
                scatter(moe, 1, half, N_EXP + 1, N_EXP, 2 * N_EXP + half)
            pe.wait_ge(over_ready, 1)
            n_over = pe.value_load(overi[0:1, OVER:OVER + 1], min_val=0, max_val=OVER)
            with pe.Fori(0, OVER) as i:
                with pe.If(i < n_over):
                    gather(over, 0, i + 1)
                    pe.wait_ge(over["in_act"], i + 1)
                    pe.wait_ge(over["in_vec"], i + 1)
                    swiglu(over, expert_steps(0, i * 3 + (first + 3 * N_EXP)), i * 7)
                    scatter(over, 0, 0, i + 1, i + 1)
                    scatter(over, 0, 1, i + 1, i + 1, i * 2 + 1)

        @block.vector
        def _(dve):
            do = Ordered(dve, vec_seq)
            V = nc.vector
            TTop, TS, STT = V.tensor_tensor, V.tensor_scalar, V.scalar_tensor_tensor
            do(V.memset(small[:, 63:64], EPS))
            dve.wait_ge(const_in, 144)
            dve.wait_ge(rel_row, 1)
            do(TTop(relrow[:, :], ps[0][0:H, :], future, ALU.add), rel_ready)
            dve.wait_ge(cond_exp, 1)
            do(TS(cond[:, :], cond[:, :], 1.0, None, ALU.add))
            do(V.reciprocal(cond[:, :], cond[:, :]))
            do(TTop(cond[:, :], cond[:, :], ccol[:, :], ALU.mult))

            def ada_sum(l, c):
                i = AT[(l, "ada", c)]
                loaded(dve, i)
                if 12 * l + c >= 2:
                    dve.wait_ge(acc_reduced, 12 * l + c - 1)
                w, a = slot_view(i, 512), acc[:, c % 2, :]
                do(TS(a, w[:, 0, :], cond[:, 0:1], None, ALU.mult))
                for k in range(1, KC):
                    ins = STT(a, w[:, k, :], cond[:, k:k + 1], a, ALU.mult, ALU.add)
                    do(ins, acc_ready if k == KC - 1 else None)
                dve.sem_inc(ring_free[slot_of(i)], 1)

            def ada_take(l, c):
                dve.wait_ge(acc_reduced, 12 * l + c + 1)
                b = ps[7] if l else ps[6 + c % 2]
                if c in (4, 5, 10, 11):
                    if c == 4:
                        dve.wait_ge(layer_in, 64 * (l + 1))
                    if c == 10:
                        dve.wait_ge(gate2_in, 16 * (l + 1))
                    g = gate[:, c // 6, 512 * (c % 2):512 * (c % 2) + 512]
                    do(TTop(g, b[:, :], g, ALU.add), mod_evac)
                else:
                    do(TTop(modc[:, 4 * c:4 * c + 4], b[:, 0:4], prm(l, "ada_b")[:, 4 * c:4 * c + 4], ALU.add), mod_evac)

            def mod_scale(l, which):
                sc = modc[:, 24 * which + 8:24 * which + 16]
                do(STT(scaleA[:, which, :], sc, 1.0, prm(l, "norm2" if which else "norm1"), ALU.add, ALU.mult), mod_ready)

            def normalise(n):
                dve.wait_ge(x_sumsq, n + 1)
                for tt in range(TT):
                    do(TS(xn[:, tt, :], x[:, tt, :], rs[:, tt:tt + 1], None, ALU.mult), xn_ready if tt else None)

            def modulate(n, which):
                for k in VEC_CHUNKS:
                    dve.wait_ge(xT_done, KC * n + (k | 1) + 1)
                    do(TS(hT[:, k, :], ps[k // 2][:, 256 * (k % 2):256 * (k % 2) + 256], scaleA[:, which, k:k + 1],
                          modc[:, 24 * which + k:24 * which + k + 1], ALU.mult, ALU.add), hT_vec)

            def bc(ap, n):
                s = list(ap.shape)
                return (ap.rearrange("p (a o) -> p a o", o=1) if len(s) == 2 else ap.rearrange("p a (b o) -> p a b o", o=1)).to_broadcast(s + [n])

            def sumsq(src, dst, n):
                for a in range(0, n, 8):
                    m = min(8, n - a)
                    sq = wide[0:src.shape[0], 0:m * DH].rearrange("p (a d) -> p a d", d=DH)
                    do(TTop(sq, src[:, a:a + m, :], src[:, a:a + m, :], ALU.mult))
                    last = V.tensor_reduce(dst[:, a:a + m], sq, AX.X, ALU.add)
                    if a + m < n:
                        do(last)
                return last

            def mixer(l):
                ada_sum0, ada_take0 = ((lambda c: ada_sum(0, c)), (lambda c: ada_take(0, c))) if l == 0 else (lambda c: None,) * 2
                normalise(2 * l)
                do(V.memset(qkraw[:, :, 0:3], 0.0))
                if l == 0:
                    for c in range(4):
                        ada_sum(0, c)
                        if c:
                            ada_take(0, c - 1)
                    ada_take(0, 3)
                    mod_scale(0, 0)
                else:
                    ada_take(1, 10)
                    ada_take(1, 11)
                modulate(2 * l, 0)
                dve.wait_ge(proj_evac, NG * l + 1)
                gb = prm(l, "gate_bias")
                do(TS(gz[:, :], graw[0:8, :], gb[0:8, :], None, ALU.add))
                do(TS(ig0[:, :], graw[32:36, :], gb[32:36, :], None, ALU.add))
                nb = prm(l, "nsa_gate_b").rearrange("p (o n) -> p o n", o=1).to_broadcast([128, TT, 12])
                do(TTop(ng[:, :, 0:12], ng[:, :, 0:12], nb, ALU.add))
                do(STT(gl[:, :], gz[:, :], -1.0, gz[:, :], ALU.mult, ALU.max), gate_abs)
                dve.wait_ge(gate_ln, l + 1)
                do(STT(gz[:, :], gz[:, :], 0.0, gl[:, :], ALU.min, ALU.subtract))
                do(TS(gl[:, :], gl[:, :], 0.0, 1.0, ALU.mult, ALU.add))
                do(V.tensor_tensor_scan(cumf[:, :], gl[:, :], gz[:, :], 0.0, ALU.mult, ALU.add))
                do(TS(negf[:, :], cumf[:, :], -1.0, None, ALU.mult))
                do(TTop(ucap, cumf[0:H, :], ig0, ALU.subtract))
                do(V.tensor_tensor_scan(negm[:, :], ucap, ucap, 0.0, ALU.min, ALU.min))
                do(TTop(ucap, ig0, cumf[0:H, :], ALU.subtract))
                do(TTop(nmrow, negm[:, :], cumf[0:H, :], ALU.subtract), gate_rows)
                dve.wait_ge(proj_evac, NG * l + 3)
                if l == 0:
                    dve.wait_ge(pool_seq, 4)
                cw = prm(l, "conv")
                for q in range(4):
                    o = conv[:, q, :]
                    do(TS(o, qkraw[:, q, 3:3 + S], cw[:, 4 * q:4 * q + 1], None, ALU.mult))
                    for j in range(1, 4):
                        ins = STT(o, qkraw[:, q, 3 - j:3 - j + S], cw[:, 4 * q + j:4 * q + j + 1], o, ALU.mult, ALU.add)
                        do(ins, conv_done if (q, j) == (3, 3) else None)
                if l == 0:
                    dve.wait_ge(bias_turned, 1)
                    for h in range(H):
                        do(V.tensor_copy(bias[:, h, :], ps[4 + h][:, 0:384]), bias_ready if h == H - 1 else None)
                dve.wait_ge(gate_T, l + 1)
                do(V.tensor_copy(gcol[:, :, :], ps[5][:, 0:32].rearrange("p (a n) -> p a n", a=2)), gate_cols)
                ada_sum0(4)
                ada_sum0(5)
                dve.wait_ge(conv_exp, l + 1)
                wv = mqkT
                do(TS(wv[:, :, :], wv[:, :, :], 1.0, None, ALU.add))
                do(V.reciprocal(wv[:, :, :], wv[:, :, :]))
                do(TTop(mqkT[:, 0:2, :], conv[:, 0:2, :], wv[:, 0:2, :], ALU.mult))
                do(STT(mqkT[:, 2:4, :], conv[:, 2:4, :], DH ** -0.5, wv[:, 2:4, :], ALU.mult, ALU.mult), mqk_ready)
                ada_take0(4)
                ada_sum0(6)
                ada_take0(5)
                ada_sum0(7)
                dve.wait_ge(proj_evac, NG * l + 7)
                fall = fqk[:, :, :, :].rearrange("p t v d -> p (t v) d")
                do(sumsq(fall, ss[:, 0:16], 16), sumsq_ready)
                ada_take0(6)
                ada_sum0(8)
                ada_take0(7)
                ada_sum0(9)
                dve.wait_ge(rstd_ready, 4 * l + 1)
                do(TTop(fall, fall, bc(rs[:, 0:16], DH), ALU.mult), fox_norm)
                fg = small[:, 0:1]
                do(TS(fg, prm(l, "fox_q"), DH ** -0.5, None, ALU.mult))
                do(TS(small[:, 2:3], prm(l, "nsa_q"), DH ** -0.5, None, ALU.mult))
                ada_take0(8)
                ada_sum0(10)
                ada_take0(9)
                ada_sum0(11)
                ada_take0(10)
                ada_take0(11)
                if l == 0:
                    mod_scale(0, 1)
                for a in range(2):
                    dve.wait_ge(fox_T, 2 * l + a + 1)
                    do(TS(fT[:, 2 * a:2 * a + 2, :], ps[4 + a][:, :].rearrange("p (h n) -> p h n", h=2),
                          prm(l, "fox_k") if a else fg, None, ALU.mult), fox_T_evac)
                dve.wait_ge(proj_evac, NG * l + 14)
                for n in range(NCMP):
                    last = TTop(cmpx[:, :, n], kvT[:, 16 * n:16 * n + 32], prm(l, "cmp_pos"), ALU.add)
                    do(last, cmpx_ready if n == NCMP - 1 else None)
                dve.wait_ge(proj_evac, NG * l + NG)
                nall = nqk[:, :, :, :].rearrange("p t v d -> p (t v) d")
                do(sumsq(nall, ss[:, 0:14], 14), sumsq_ready)
                dve.wait_ge(rstd_ready, 4 * l + 2)
                do(TTop(nall, nall, bc(rs[:, 0:14], DH), ALU.mult), nsa_norm)
                dve.wait_ge(cmp_done, l + 1)
                do(V.tensor_copy(kcn[:, :, :], ps[6][0:NCMP, 0:DH].rearrange("p (o d) -> p o d", o=1).to_broadcast([NCMP, 2, DH])))
                vv = ps[7][0:DH, 0:NCMP].rearrange("p (o n) -> p o n", o=1).to_broadcast([DH, H, NCMP])
                do(V.tensor_copy(vpad[:, :, 0:NCMP], vv), vpad_ready)
                do(sumsq(kcn[:, 0:1, :], ss[0:NCMP, 0:1], 1), sumsq_ready)
                dve.wait_ge(rstd_ready, 4 * l + 3)
                do(TS(kcn[:, :, :], kcn[:, :, :], rs[0:NCMP, 0:1], None, ALU.mult), kcn_ready)
                dve.wait_ge(nsa_T, 2 * l + 1)
                do(TS(nT[:, 0:2, :], ps[4][:, :].rearrange("p (h n) -> p h n", h=2), small[:, 2:3], None, ALU.mult), nsa_T_evac)
                dve.wait_ge(nsa_T, 2 * l + 2)
                for q in range(2):
                    do(TS(nT[:, 2 + q, :], ps[5][:, 256 * q:256 * q + 256], prm(l, "nsa_k")[:, 1 + q:2 + q], None, ALU.mult),
                       nsa_T_evac if q else None)
                dve.wait_ge(kv_T, l + 1)
                do(TS(kcT[:, :], ps[6][:, 0:NCMP], prm(l, "nsa_k")[:, 0:1], None, ALU.mult))
                for h in range(H):
                    r = slice(32 * h, 32 * h + NCMP)
                    do(V.tensor_copy(vblk[r, h, :], ps[7][r, 0:DH]), kv_T_evac if h == H - 1 else None)
                dve.wait_ge(gates_exp, l + 1)
                do(TS(ng[:, :, 0:12], ng[:, :, 0:12], 1.0, None, ALU.add))
                do(V.reciprocal(ng[:, :, 0:12], ng[:, :, 0:12]))

                if l == 0:
                    do(V.memset(biasc[:, :, :], -1e30))
                    do(V.tensor_copy(biasc[:, 0:4, 0:7], bias[:, :, 31:128:16]))
                    do(V.tensor_copy(biasc[:, 4:8, :], bias[:, :, 128 + 31:384:16]))

                def part1(i):
                    kind, h = HEADS[i]
                    e, b = prob[:, i % 2, :], ps[i % 2][:, 0:384]
                    if kind == "stick":
                        dve.wait_ge(stick_sp, N_STICK * l + h + 1)
                        do(STT(e, b, 0.0, e, ALU.max, ALU.add))
                        do(STT(e, cst("strict_T"), 0.0, e, ALU.is_ge, ALU.mult), stick_masked)
                        return
                    dve.wait_ge(head_scores, NH * l + i + 1)
                    if i >= 2 and HEADS[i - 2][0] in BKINDS:
                        dve.wait_ge(head_second, N_B * l + count(BKINDS, i - 2))
                    if kind == "mlstm":
                        m = ps[2 + i % 2]
                        mask = cst("causal_T")
                        do(TTop(e[:, 0:256], m[:, 0:256], mask[:, 0:256], ALU.add))
                        do(TTop(e[:, 256:384], m[:, 128:256], mask[:, 256:384], ALU.add), head_shift[i % 2])
                        return
                    if kind == "fox":
                        for tt, (c0, c1) in enumerate(((0, 128), (128, 384))):
                            do(STT(e[:, c0:c1], b[:, c0:c1], gcol[:, tt, 12 + h:13 + h], cst("causal")[:, c0:c1], ALU.add, ALU.add),
                               head_free[i % 2] if tt else None)
                    else:
                        do(TTop(e, b, bias[:, h, :], ALU.add), head_free[i % 2])
                    do(V.tensor_reduce(nmax[:, i % 2, 0:1], e[:, 0:128], AX.X, ALU.max, negate=True))
                    do(V.tensor_reduce(nmax[:, i % 2, 1:2], e[:, 128:384], AX.X, ALU.max, negate=True), head_shift[i % 2])

                def part2(i):
                    kind, h = HEADS[i]
                    e, b, pt = prob[:, i % 2, :], ps[i % 2][:, 0:384], probT[:, i % 2, :]
                    if i >= 2:
                        dve.wait_ge(head_pv, NH * l + i - 1)
                    if kind == "mlstm":
                        dve.wait_ge(head_exp, NH * l + i + 1)
                        do(TTop(pt, b, e, ALU.mult), head_pT)
                        do.also(head_free[i % 2])
                    elif kind == "stick":
                        dve.wait_ge(head_second, N_B * l + count(BKINDS, i))
                        do(TTop(pt, b, cst("strict_T"), ALU.add), head_shift[i % 2])
                        do.also(head_free[i % 2])
                    else:
                        dve.wait_ge(head_second, N_B * l + count(BKINDS, i))
                        do(V.tensor_copy(pt, ps[2 + i % 2][:, 0:384]), head_pT)

                def finish(gi):
                    kind = HEADS[H * gi][0]
                    dve.wait_ge(head_pv, NH * l + H * gi + H)
                    o = [ps[4 + 2 * (gi % 2) + tt] for tt in range(TT)]
                    cols = {"mlstm": 0, "fox": 256, "stick": 512}.get(kind, 768)
                    dst = [mix[:, tt, cols:cols + 256].rearrange("p (h d) -> p h d", h=H) for tt in range(TT)]
                    if kind == "mlstm":
                        for tt in range(TT):
                            ov = o[tt][:, 0:H * (DH + 1)].rearrange("p (h d) -> p h d", h=H)
                            dn = small[:, 8:12]
                            do(V.tensor_copy(dn.rearrange("p (h o) -> p h o", o=1), ov[:, :, DH:DH + 1]))
                            do(STT(dn, dn, -1.0, dn, ALU.mult, ALU.max))
                            do(TTop(dn, dn, expnm[:, tt, :], ALU.max))
                            do(V.reciprocal(dn, dn))
                            do(TTop(mh[:, tt, :, :], ov[:, :, 0:DH], bc(dn, DH), ALU.mult), o_free if tt else None)
                        mall = mh[:, :, :, :].rearrange("p t h d -> p (t h) d")
                        do(sumsq(mall, ss[:, 0:8], 8), sumsq_ready)
                        return
                    if kind == "stick":
                        for tt in range(TT):
                            do(V.tensor_copy(dst[tt], o[tt][:, 0:256].rearrange("p (h d) -> p h d", h=H)), o_free if tt else None)
                        return
                    do(V.reciprocal(rl[:, :, :], lsum[:, gi, :, :]))
                    if kind in ("sel", "win"):
                        gcolumn = 1 if kind == "sel" else 2
                        gv = ng[:, :, 0:12].rearrange("p t (h c) -> p h t c", c=3)[:, :, :, gcolumn]
                        do(TTop(rl[:, :, :], rl[:, :, :], gv, ALU.mult))
                    for tt in range(TT):
                        ov = o[tt][:, 0:256].rearrange("p (h d) -> p h d", h=H)
                        r = rl[:, :, tt:tt + 1].to_broadcast([128, H, DH])
                        if kind == "win":
                            wd = wide[:, 256 * tt:256 * tt + 256].rearrange("p (h d) -> p h d", h=H)
                            do(TTop(wd, ov, r, ALU.mult), o_free if tt else None)
                            do(TTop(dst[tt], dst[tt], wd, ALU.add))
                        else:
                            do(TTop(dst[tt], ov, r, ALU.mult), o_free if tt else None)

                def finish_mlstm():
                    dve.wait_ge(rstd_ready, 4 * l + 4)
                    mall = mh[:, :, :, :].rearrange("p t h d -> p (t h) d")
                    do(TTop(mall, mall, bc(rs[:, 0:8], DH), ALU.mult))
                    dve.wait_ge(mo_exp, l + 1)
                    do(TS(mo[:, :, :], mo[:, :, :], 1.0, None, ALU.add))
                    do(V.reciprocal(mo[:, :, :], mo[:, :, :]))
                    do(TTop(mix[:, :, 0:256], mh[:, :, :, :].rearrange("p t h d -> p t (h d)"), mo[:, :, :], ALU.mult))

                for i in range(NH + 2):
                    if i < NH:
                        part1(i)
                    if 0 <= i - 1 < NH:
                        part2(i - 1)
                    if i >= 2 and (i - 2) % H == H - 1:
                        finish((i - 2) // H)
                    if i == H + 3:
                        finish_mlstm()

                dve.wait_ge(cmp_scores, l + 1)
                pcv = pc[:, :, :, 0:NCMP].rearrange("p t h n -> p (t h) n")
                for q in range(2):
                    sc = ps[q][:, 0:64].rearrange("p (a n) -> p a n", a=4)[:, :, 0:NCMP]
                    do(TTop(pcv[:, q:8:2, :], sc, biasc[:, q:8:2, :], ALU.add))
                do(V.tensor_reduce(small[:, 16:24], pcv, AX.X, ALU.max))
                do(TTop(pcv, pcv, bc(small[:, 16:24], NCMP), ALU.subtract), cmp_shift)
                dve.wait_ge(cmp_exp, l + 1)
                do(V.tensor_reduce(small[:, 16:24], pcv, AX.X, ALU.add))
                do(V.reciprocal(small[:, 16:24], small[:, 16:24]))
                g0 = ng[:, :, 0:12].rearrange("p t (h c) -> p t h c", c=3)[:, :, :, 0]
                s3 = small[:, 16:24].rearrange("p (t h) -> p t h", t=TT)
                do(TTop(s3, s3, g0, ALU.mult))
                do(TTop(pcv, pcv, bc(small[:, 16:24], NCMP), ALU.mult))
                for tt in range(TT):
                    valid = cst("valid_cmp")[:, NCMP * tt:NCMP * tt + NCMP].rearrange("p (o n) -> p o n", o=1).to_broadcast([128, H, NCMP])
                    do(TTop(pc[:, tt, :, 0:NCMP], pc[:, tt, :, 0:NCMP], valid, ALU.mult), cmp_probs if tt else None)
                dve.wait_ge(cmp_pT, l + 1)
                do(V.tensor_copy(pcT[:, :, :], ps[3][:, 0:256].rearrange("p (t n) -> p t n", t=TT)), cmp_pT_evac)
                dve.wait_ge(cmp_out, l + 1)
                do(TTop(mix[:, :, 768:1024], mix[:, :, 768:1024], ps[2][:, :].rearrange("p (t n) -> p t n", t=TT), ALU.add), mix_ready)
                for k in VEC_CHUNKS:
                    dve.wait_ge(mixT_done, KC * l + (k | 1) + 1)
                    do(TS(hT[:, k, :], ps[k // 2][:, 256 * (k % 2):256 * (k % 2) + 256], prm(l, "out_g")[:, k:k + 1], None, ALU.mult), mixT_vec)
                for half in range(2):
                    for tt in range(TT):
                        dve.wait_ge(wout_done, 4 * l + 2 * half + tt + 1)
                        xs = x[:, tt, 512 * half:512 * half + 512]
                        do(TTop(wide[:, 0:512], ps[4 + 2 * half + tt][:, :], gate[:, 0, 512 * half:512 * half + 512], ALU.mult))
                        do(TTop(xs, xs, wide[:, 0:512], ALU.add), x_mixed if (half, tt) == (1, 1) else None)

            def swiglu(f, steps, base, do, between=lambda j: None):
                for j, st in enumerate(steps):
                    sg, hb = hsig[:, 0:st.w], hbuf[:, j % 2, 0:st.w]
                    dve.wait_ge(f["tanh"], base + j + 1)
                    if j >= 2:
                        dve.wait_ge(f["T"], base + j - 1)
                    do(STT(hb, sg, 1.0, ps[4][:, 0:st.w], ALU.add, ALU.mult))
                    dve.wait_ge(f["u"], base + j + 1)
                    if st.last:
                        dve.sem_inc(ring_free[slot_of(st.loads[1])], 1)
                    do(STT(hb, hb, 0.5, ps[5][:, 0:st.w], ALU.mult, ALU.mult), f["h"])
                    between(j)

            def onehot_of(f, q, e, do, shift=0.0):
                for tt in range(TT):
                    r = rank[:, tt, bass.ds(e, 1)]
                    if shift:
                        do(TS(wtmp[:, tt:tt + 1], r, -shift, None, ALU.add))
                        r = wtmp[:, tt:tt + 1]
                    do(TS(pick[q][:, tt, :], cst("iota"), r, None, ALU.is_equal), f["onehot"] if tt else None)

            def gathered_in(f, q, count, do):
                dve.wait_ge(f["turned"], count)
                do(V.tensor_copy(pickT[q], ps[7][:, 0:256].rearrange("p (t n) -> p t n", t=TT)), f["turn_evac"])
                dve.wait_ge(f["gathered"], count)
                for k in range(4, KC):
                    do(TS(hT[:, k, 128 * q:128 * q + 128], ps[3][:, 128 * (k - 4):128 * (k - 4) + 128], scaleA[:, 1, k:k + 1],
                          modc[:, 24 + k:25 + k], ALU.mult, ALU.add), f["in_vec"] if k == KC - 1 else None)

            def y_out(f, downs, do):
                dve.wait_ge(f["d"], downs)
                do(V.tensor_copy(ysb[:, 512:1024], ps[1][:, :]), f["y_vec"])

            def add_in(f, half, column, count, do):
                dve.wait_ge(f["scattered"], count)
                for tt in range(TT):
                    ya = yacc[:, tt, 512 * half:512 * half + 512]
                    do(STT(ya, ps[2 + tt][:, :], wts[:, tt, bass.ds(column, 1)], ya, ALU.mult, ALU.add), f["added"] if tt else None)

            def add_residual(tt, half, y):
                xs, g = x[:, tt, 512 * half:512 * half + 512], gate[:, 1, 512 * half:512 * half + 512]
                do(TTop(wide[:, 0:512], y, g, ALU.mult))
                do(TTop(xs, xs, wide[:, 0:512], ALU.add), x_final if (tt, half) == (1, 1) else None)

            mixer(0)
            normalise(1)
            modulate(1, 1)

            def modulation(j):
                c = j - 1
                if 0 <= c < 12:
                    ada_sum(1, c)
                if 1 <= c < 11:
                    ada_take(1, c - 1)
                if c in (4, 10):
                    mod_scale(1, c // 10)

            swiglu(ffn, dense_steps(), 0, do, modulation)
            dve.wait_ge(ffn["d"], TT * len(FF_UNITS))
            for tt in range(TT):
                for half in range(2):
                    add_residual(tt, half, ps[2 * tt + half][:, :])
            mixer(1)
            normalise(3)
            modulate(3, 1)
            dve.wait_ge(router_done, 1)
            for tt in range(TT):
                do(TTop(lg[:, tt, :], ps[7][:, 8 * tt:8 * tt + 8], prm(1, "router_b"), ALU.add))
                do(V.max(top8[:, tt, :], lg[:, tt, :]))
                do(V.max_index(topi[:, tt, :], top8[:, tt, :], lg[:, tt, :]))
            do(V.tensor_copy(topf[:, :, :], topi[:, :, :]))
            do(TTop(tw[:, :, 0:1], top8[:, :, 1:2], top8[:, :, 0:1], ALU.subtract), router_shift)
            dve.wait_ge(router_exp, 1)
            do(TS(tw[:, :, 1:2], tw[:, :, 0:1], 1.0, None, ALU.add))
            do(V.reciprocal(tw[:, :, 1:2], tw[:, :, 1:2]))
            do(TTop(tw[:, :, 2:3], tw[:, :, 0:1], tw[:, :, 1:2], ALU.mult))
            iota8 = cst("iota")[:, 0:N_EXP]
            for tt in range(TT):
                w, p, one = wts[:, tt, 1:N_EXP + 1], picked[:, tt, :], wtmp[:, 0:N_EXP]
                do(TS(p, iota8, topf[:, tt, 0:1], None, ALU.is_equal))
                do(TS(w, p, tw[:, tt, 1:2], None, ALU.mult))
                do(TS(one, iota8, topf[:, tt, 1:2], None, ALU.is_equal))
                do(STT(w, one, tw[:, tt, 2:3], w, ALU.mult, ALU.add))
                do(TTop(p, p, one, ALU.add), picked_ready if tt else None)
            do(V.memset(rank[:, :, :], 1000.0))
            do(V.memset(wts[:, :, 0:1], 0.0))
            do(V.memset(pickT[1], 0.0))
            do(V.memset(ysb, 0.0))
            do(V.memset(yacc[:, :, :], 0.0))
            dve.wait_ge(rank_done, 1)
            rk = rank[:, :, 0:N_EXP]
            do(STT(rk, picked[:, :, :], -1000.0, rk, ALU.mult, ALU.add))
            do(TTop(rk, rk, ps[6][:, 0:16].rearrange("p (t n) -> p t n", t=TT), ALU.add))
            onehot_of(moe, 0, 0, do)
            o_one, o_is, o_run, o_tmp, o_id = (wtmp[0:1, 8 * k:8 * k + 8] for k in range(5))
            do(V.memset(o_one, 1.0))
            do(TS(o_is, ps[6][0:1, 16:24], float(BLK), None, ALU.is_gt))
            do(V.tensor_tensor_scan(o_run, o_one, o_is, 0.0, ALU.mult, ALU.add))
            for k in range(OVER):
                do(TS(o_tmp, o_run, float(k + 1), None, ALU.is_equal))
                do(TTop(o_tmp, o_tmp, o_is, ALU.mult))
                do(TTop(o_tmp, o_tmp, cst("iota", 1)[:, 0:N_EXP], ALU.mult))
                do(V.tensor_reduce(o_id[:, k:k + 1], o_tmp, AX.X, ALU.add))
            do(V.tensor_copy(o_id[:, OVER:OVER + 1], o_run[:, 7:8]))
            do(V.tensor_copy(overi[0:1, 0:OVER + 1], o_id[:, 0:OVER + 1]), over_ready)
            gathered_in(moe, 0, 1, do)
            dve.sem_inc(moe["y_vec"], 1)
            per = 26
            with dve.Fori(0, N_EXP // 2) as i:
                doe = Ordered(dve, moe["vec_seq"])
                doe.base = {id(moe["vec_seq"]): i * per, id(moe["h"]): i * 14, id(moe["onehot"]): i * 2 + 1,
                            id(moe["turn_evac"]): i * 2 + 1, id(moe["in_vec"]): i * 2 + 1, id(moe["y_vec"]): i * 2 + 1,
                            id(moe["added"]): i * 4}

                def between(j):
                    q, u = divmod(j, 7)
                    if j == 7:
                        y_out(moe, i * 14 + 7, doe)
                    if u == 1:
                        onehot_of(moe, 1 - q, i * 2 + (q + 1), doe)
                        add_in(moe, 0, i * 2 + q, i * 4 + (2 * q + 1), doe)
                    if u == 2:
                        add_in(moe, 1, i * 2 + q, i * 4 + (2 * q + 2), doe)
                    if u == 3:
                        gathered_in(moe, 1 - q, i * 2 + (q + 2), doe)

                swiglu(moe, expert_steps(0, 0) + expert_steps(1, 0), i * 14, doe, between)
                y_out(moe, i * 14 + 14, doe)
                assert doe.n[id(moe["vec_seq"])] == per, doe.n[id(moe["vec_seq"])]
            for half in range(2):
                add_in(moe, half, N_EXP, 2 * N_EXP + half + 1, do)
            n_over = dve.value_load(overi[0:1, OVER:OVER + 1], min_val=0, max_val=OVER)
            per_over = 15
            with dve.Fori(0, OVER) as i:
                with dve.If(i < n_over):
                    e = dve.value_load(overi[0:1, bass.ds(i, 1)], min_val=0, max_val=N_EXP - 1)
                    doe = Ordered(dve, over["vec_seq"])
                    doe.base = {id(over["vec_seq"]): i * per_over, id(over["h"]): i * 7, id(over["onehot"]): i,
                                id(over["turn_evac"]): i, id(over["in_vec"]): i, id(over["y_vec"]): i,
                                id(over["added"]): i * 2}
                    onehot_of(over, 0, e, doe, float(BLK))
                    gathered_in(over, 0, i + 1, doe)
                    swiglu(over, expert_steps(0, 0), i * 7, doe)
                    y_out(over, i * 7 + 7, doe)
                    for half in range(2):
                        add_in(over, half, e + 1, i * 2 + (half + 1), doe)
                    dve.sem_inc(over["vec_left"], 1)
                    assert doe.n[id(over["vec_seq"])] == per_over, doe.n[id(over["vec_seq"])]
            for tt in range(TT):
                for half in range(2):
                    add_residual(tt, half, yacc[:, tt, 512 * half:512 * half + 512])


_RAW = ["x", "ada_w", "ada_b", "w_in", "w_out", "rel_bias", "nsa_cmp_wk", "nsa_cmp_wv", "ffn_wg", "ffn_wu", "ffn_wd",
        "moe_router_w", "moe_wg", "moe_wu", "moe_wd"]


def constants():
    import math

    import numpy as np
    f = np.float32
    c = np.zeros((128, CONST_W), f)

    def put(name, a):
        at, w = CONST[name]
        assert a.shape[1] == w, name
        c[:a.shape[0], at:at + w] = a

    p, j = np.arange(128)[:, None], np.arange(128)[None, :]
    zero = np.zeros((128, 128), f)
    big = f(-1e30)
    put("ident", np.eye(128, dtype=f))
    put("ones", np.ones((128, 1), f))
    put("minus_ones", -np.ones((128, 1), f))
    put("minus_tri", np.where(p >= j, f(-1), f(0)))
    for name, m in (("causal", j > p), ("causal_T", j < p), ("strict_T", j <= p)):
        d = np.where(m, big, f(0))
        put(name, np.concatenate([d, zero, d], 1))
    dist = 255 - np.arange(512)
    n = np.maximum(dist, 0)
    large = 16 + (np.log(np.maximum(n, 1).astype(f) / f(16)) / f(math.log(128 / 16)) * f(16)).astype(np.int32)
    bucket = np.where(n < 16, n, np.minimum(large, 31))
    onehot = ((np.arange(32)[:, None] == bucket[None, :]).astype(f))
    future = np.ascontiguousarray(np.broadcast_to(np.where(dist < 0, big, f(0)), (H, 512)))
    ends = 16 * np.arange(NCMP) + 31
    put("valid_cmp", np.concatenate([(ends[None, :] <= p + 128 * tt).astype(f) for tt in range(TT)], 1))
    put("iota", np.broadcast_to(np.arange(128, dtype=f), (128, 128)))
    return c, onehot, future


def parameters(i):
    import numpy as np
    out = np.zeros((DEPTH, 128, PAR_W), np.float32)
    for l in range(DEPTH):
        def at(name, p0, p1, k0=0, k1=None):
            a, w = PAR[name]
            return out[l, p0:p1, a + k0:a + (w if k1 is None else k1)]
        at("norm1", 0, 128)[:] = i["norm1_g"][l].reshape(8, 128).T
        at("norm2", 0, 128)[:] = i["norm2_g"][l].reshape(8, 128).T
        at("conv", 0, 128)[:] = i["mlstm_conv_w"][l].reshape(4, 4, 128).transpose(2, 1, 0).reshape(128, 16)
        at("gate_bias", 0, 4)[:, 0] = i["mlstm_gate_b"][l, 4:8]
        at("gate_bias", 4, 8)[:, 0] = i["fox_f_b"][l]
        at("gate_bias", 32, 36)[:, 0] = i["mlstm_gate_b"][l, 0:4]
        at("out_g", 0, 128)[:] = 1
        at("out_g", 0, 128, 0, 2)[:] = i["mlstm_out_g"][l].reshape(2, 128).T
        for p0 in (0, 64):
            at("fox_q", p0, p0 + 64)[:, 0] = i["fox_q_g"][l]
            at("fox_k", p0, p0 + 64)[:, 0] = i["fox_k_g"][l]
            at("nsa_q", p0, p0 + 64)[:, 0] = i["nsa_q_g"][l]
            at("nsa_k", p0, p0 + 64)[:] = i["nsa_k_g"][l][[0, 1, 2] if p0 == 0 else [0, 2, 1]].T
        at("cmp_pos", 0, 64)[:] = i["nsa_cmp_pos"][l].T
        at("cmp_pos", 64, 128)[:] = i["nsa_cmp_pos"][l].T
        at("nsa_gate_b", 0, 128)[:] = i["nsa_gate_b"][l][None]
        if l % 2:
            at("router_b", 0, 128)[:] = i["moe_router_b"][l // 2][None]
        at("ada_b", 0, 128)[:] = i["ada_b"][l].reshape(48, 128).T
    return out


def kernel(**inputs):
    import numpy as np
    import concourse.bacc as bacc
    from concourse.bass_utils import run_bass_kernel_spmd

    a = {n: np.ascontiguousarray(v) for n, v in inputs.items()}
    w_in = a["w_in"]
    gates = np.zeros((DEPTH, D, 48), w_in.dtype)
    gates[:, :, 0:4] = w_in[:, :, 1028:1032]
    gates[:, :, 4:8] = w_in[:, :, 1800:1804]
    gates[:, :, 32:36] = w_in[:, :, 1024:1028]
    gates[:, :, 36:48] = w_in[:, :, 3212:3224]
    arrays = {n: a[n] for n in _RAW}
    arrays["reverse"] = np.ascontiguousarray(np.eye(128, dtype=np.float32)[::-1])
    arrays["c_cols"] = np.ascontiguousarray(a["c"].reshape(KC, 128).T)
    arrays["w_gates"] = gates
    arrays["const"], arrays["onehot"], arrays["future"] = constants()
    arrays["par"] = parameters(a)

    nc = bacc.Bacc("TRN2", target_bir_lowering=False, num_devices=1)
    t = {n: nc.dram_tensor("in_" + n, v.shape, mybir.dt.from_np(v.dtype), kind="ExternalInput").ap() for n, v in arrays.items()}
    out = nc.dram_tensor("out", (1, S, D), F32, kind="ExternalOutput").ap()
    program(nc, t, out)
    r = run_bass_kernel_spmd(nc, [{"in_" + n: v for n, v in arrays.items()}], core_ids=[0])
    return r.results[0]["out"]
```

```python
from contextlib import ExitStack

import concourse.bass as bass
from concourse import mybir

F32 = mybir.dt.float32
U32 = mybir.dt.uint32
ALU = mybir.AluOpType
ACT = mybir.ActivationFunctionType
AX = mybir.AxisListType

D = 1024
KC = D // 128
TT = 2
S = 256
DEPTH = 2
H = 4
DH = 64
W_IN = 3224
D_FF = 2816
N_EXP = 8
D_FE = 3584
EPS = 1e-6
NCMP = 15
RING = 7
LOADS = 21
BLK = 128
OVER = 3
SLOT = KC * 512
ACT_CHUNKS, VEC_CHUNKS = (0, 1, 4, 5), (2, 3, 6, 7)
CONST = {}
_at = 0
for _n, _w in (("ident", 128), ("ones", 1), ("minus_ones", 1), ("minus_tri", 128), ("causal", 384),
               ("causal_T", 384), ("strict_T", 384), ("valid_cmp", 30), ("iota", 128)):
    CONST[_n] = (_at, _w)
    _at += _w
CONST_W = _at
PAR = {}
_at = 0
for _n, _w in (("norm1", 8), ("norm2", 8), ("conv", 16), ("gate_bias", 1), ("out_g", 8), ("fox_q", 1),
               ("fox_k", 1), ("nsa_q", 1), ("nsa_k", 3), ("cmp_pos", 32), ("nsa_gate_b", 12),
               ("router_b", 8), ("ada_b", 48)):
    PAR[_n] = (_at, _w)
    _at += _w
PAR_W = _at
WIN = ((0, 512), (512, 512), (1032, 512), (1544, 256), (1804, 512), (2316, 512), (2828, 384))
FF_UNITS = tuple((384 * u, 384 if u < 6 else 512) for u in range(7))
FE_UNITS = tuple((512 * u, 512) for u in range(7))
GROUPS = [(None, 0)] + [(c, g) for c in range(6) for g in range(2)] + [(6, g) for g in range(3)]
NG = len(GROUPS)
ADA_AFTER = {6: 4, 7: 5, 8: 6, 9: 7, 10: 8, 11: 9, 12: 10, 13: 11}
HEADS = [(k, h) for k in ("mlstm", "fox", "stick", "sel", "win") for h in range(H)]
NH = len(HEADS)


def count(kinds, i):
    return sum(k in kinds for k, _ in HEADS[:i + 1])


SOFT = ("fox", "sel", "win")
BKINDS = SOFT + ("stick",)
PKINDS = SOFT + ("mlstm",)
N_B, N_P, N_STICK = count(BKINDS, NH), count(PKINDS, NH), H
S0 = HEADS.index(("stick", 0))
assert S0 == 2 * H
PE_ORDER = [("first", 0), ("first", 1), ("compress", 0), ("nsa_T", 0), ("first", 2), ("kv_T", 0), ("first", 3), ("cmp_scores", 0),
            ("third", 0), ("third", 1), ("first", 4), ("cmp_turn", 0), ("third", 2), ("first", 5), ("third", 3)]
DVE_ORDER = [("part1", 0), ("part1", 1), ("nsa_norm", 0), ("k_cmp", 0), ("part2", 0), ("nsa_T", 0), ("part1", 2), ("part2", 1),
             ("kv_T", 0), ("part1", 3), ("gates", 0), ("cmp_shift", 0), ("part2", 2), ("cmp_probs", 0), ("part2", 3), ("part1", 4),
             ("cmp_turned", 0), ("part1", 5)]
for _i in range(6, NH + 3):
    if S0 + 2 <= _i < S0 + 4:
        PE_ORDER += [("second", _i - 2)] + ([("third", _i - 3)] if _i == S0 + 2 else [])
    else:
        PE_ORDER += [("first", _i), ("second", _i - 2)] if _i in (S0, S0 + 1) else [("second", _i - 2), ("first", _i)]
        if _i in (S0 + 4, S0 + 5):
            PE_ORDER += [("third", _i - 4)]
        elif _i == S0 + 6:
            PE_ORDER += [("third", _i - 4), ("third", _i - 3)]
        else:
            PE_ORDER += [("third", _i - 3)] if _i > 6 else [("cmp_out", 0)]
        if _i == S0 + 1:
            PE_ORDER += [("first", S0 + 2), ("first", S0 + 3)]
    DVE_ORDER += [("part2", _i - 2)] if _i != S0 + 1 else []
    if _i == S0:
        DVE_ORDER += [("part2", _i - 1)]
    DVE_ORDER += [("part1", _i)]
    DVE_ORDER += {6: [("cmp_take", 0)], S0 + 6: [("mlstm_end", 0)]}.get(_i, [])
    if _i >= H + 3 and (_i - 3) % H == 0:
        DVE_ORDER += [("finish", (_i - H - 3) // H)]
DVE_ORDER += [("finish", 4)]
PE_ORDER = [(k, i) for k, i in PE_ORDER if 0 <= i < NH]
DVE_ORDER = [(k, i) for k, i in DVE_ORDER if 0 <= i < NH]
assert sorted(i for k, i in PE_ORDER if k == "third") == list(range(NH)) and sum(k == "finish" for k, _ in DVE_ORDER) == 5
ACT_ORDER = [("exp", 0), ("exp", 1), ("k_cmp", 0), ("exp", 2), ("exp", 3), ("cmp_exp", 0)] + [("exp", i) for i in range(4, S0)]
ACT_ORDER += [("abs_exp", i) for i in range(S0, S0 + H)] + [("ln", i) for i in range(S0, S0 + H)]
ACT_ORDER += [("mlstm_rstd", 0)]
ACT_ORDER += [("exp", i) for k, i in DVE_ORDER if (k == "part1" and i >= S0 + H) or (k == "part2" and S0 <= i < S0 + H)]
ADA, WOUT = [("ada", c) for c in range(12)], [("wout", 0), ("wout", 1)]
WINS = [("win", c) for c in range(7)]
SEQ = [(0,) + k for k in ADA[:4] + WINS[:3] + ADA[4:6] + WINS[3:4] + ADA[6:8] + WINS[4:5] + ADA[8:10]
       + WINS[5:6] + ADA[10:] + WINS[6:] + WOUT]
for _u in range(7):
    SEQ += [(0, "ffn", 3 * _u + j) for j in range(3)] + [(1,) + k for k in ADA[2 * _u:2 * _u + 2]]
SEQ += [(1,) + k for k in WINS + WOUT]
AT = {k: n for n, k in enumerate(SEQ)}
FIRST_EXPERT = len(SEQ)
assert FIRST_EXPERT % RING == 0 and LOADS % RING == 0


class Step:

    def __init__(self, w, tile, y, loads, rounds, first, last, begin, end):
        self.w, self.tile, self.y, self.loads, self.rounds = w, tile, y, loads, rounds
        self.first, self.last, self.begin, self.end = first, last, begin, end


def dense_steps():
    return [Step(w, tt, 2 * tt, [AT[(0, "ffn", 3 * u + p)] for p in range(3)], 0, tt == 0, tt == TT - 1, u == 0, u == 6)
            for u, (_, w) in enumerate(FF_UNITS) for tt in range(TT)]


def expert_steps(tile, rounds):
    return [Step(w, tile, 0, [3 * u + p for p in range(3)], rounds, True, True, u == 0, u == 6)
            for u, (_, w) in enumerate(FE_UNITS)]


class Ordered:

    def __init__(self, eng, own):
        self.eng, self.own, self.n, self.base = eng, own, {}, {}

    def __call__(self, ins, sem=None):
        sem = self.own if sem is None else sem
        key = id(sem)
        self.n[key] = self.n.get(key, 0) + 1
        ins.then_inc(sem, 1)
        self.eng.wait_ge(sem, self.n[key] + self.base.get(key, 0))

    def also(self, sem):
        self.n[id(sem)] = self.n.get(id(sem), 0) + 1
        self.eng.sem_inc(sem, 1)


def program(nc, t, out):
    ctx = ExitStack()
    with ctx:
        def sb(name, shape, dt=F32):
            return ctx.enter_context(nc.sbuf_tensor(name, shape, dt))

        def sem(name):
            return ctx.enter_context(nc.semaphore(name))

        ring = sb("ring", [128, RING, SLOT])
        wide = sb("wide", [128, 512])
        x = sb("x_res", [128, TT, D])
        xn = sb("x_norm", [128, TT, D])
        mix = xn
        hT = sb("h_T", [128, KC, S])
        const = sb("const", [128, CONST_W])
        par = sb("par", [128, DEPTH, PAR_W])
        bias = sb("rel_bias_tiles", [128, H, 384])
        biasc = sb("rel_bias_cmp", [128, TT * H, NCMP])
        table = sb("table", [32, H])
        onehot, future = (hT[0:p, 2 * k:2 * k + 2, :].rearrange("p a n -> p (a n)") for k, p in enumerate((32, H)))
        negm = sb("neg_m_run", [H, S])
        ccol = sb("c_col", [128, KC])
        cond = sb("cond", [128, KC])
        acc = sb("ada_acc", [128, 2, 512])
        modc = sb("mod_cols", [128, 48])
        scaleA = sb("mod_scale", [128, 2, KC])
        gate = sb("gate_rows", [128, 2, D])
        cmp_region = sb("cmp_region", [128, 32 * DH])
        cmpw = cmp_region[:, :].rearrange("p (j d) -> p j d", d=DH)
        nT = cmp_region[:, 0:4 * S].rearrange("p (v n) -> p v n", n=S)
        pcT = cmp_region[:, 6 * S:7 * S].rearrange("p (t n) -> p t n", t=TT)
        small = sb("small", [128, 64])
        ss = sb("sumsq", [128, 32])
        rs = sb("rstd", [128, 32])
        prob = sb("prob", [128, 2, 384])
        probT = sb("prob_T", [128, 2, 384])
        hTf = hT[:, :, :].rearrange("p k n -> p (k n)")
        probs = [prob[:, 0, :], prob[:, 1, :]] + [hTf[:, 384 * q:384 * q + 384] for q in range(2)]
        probTs = [probT[:, 0, :], probT[:, 1, :]] + [hTf[:, 384 * q:384 * q + 384] for q in range(2, 4)]
        pf, pTf = (a[:, :, :].rearrange("p a n -> p (a n)") for a in (prob, probT))
        graw, gz = wide[0:48, 0:S], wide[0:8, S:2 * S]
        gl, ig0, nmrow = pTf[0:8, 0:S], pTf[0:H, S:2 * S], pTf[0:H, 2 * S:3 * S]
        ucap = pf[0:H, 2 * S:3 * S]
        reverse = pf[:, 384:512]
        wgate = pf[:, 0:KC * 48].rearrange("p (k n) -> p k n", k=KC)
        cumf = sb("cum_logf", [8, S])
        gcol = sb("gate_cols", [128, TT, 16])
        expnm = sb("exp_neg_m", [128, TT, H])
        ng = sb("nsa_gates", [128, TT, 16])
        qk_region = sb("m_s_region", [128, 4 * (3 + S)])
        qkraw = qk_region[:, :].rearrange("p (a n) -> p a n", a=4)
        sT = qk_region[:, 0:4 * S].rearrange("p (a n) -> p a n", a=4)
        hbuf = qk_region[:, 0:1024].rearrange("p (a n) -> p a n", a=2)
        mqkT = sb("m_qk_T", [128, 4, S])
        mv = sb("m_v", [128, TT, H, DH + 1])
        mo = sb("m_o", [128, TT, 256])
        mh = acc[:, 0, :].rearrange("p (t h d) -> p t h d", t=TT, h=H)
        fqk = xn[:, 0, :].rearrange("p (t v d) -> p t v d", t=TT, v=8)
        nqk = xn[:, 1, 0:896].rearrange("p (t v d) -> p t v d", t=TT, v=7)
        kvT = sb("cmp_kv_T", [128, S])
        fT = sb("f_qk_T", [128, 4, S])
        conv = fT
        negf = sb("neg_cum_logf", [8, S])
        fv = sb("f_v", [128, TT, 256])
        sv = sb("s_v", [128, TT, 256])
        hsig = sv[:, :, :].rearrange("p t n -> p (t n)")
        hbT = mqkT[:, :, :].rearrange("p (a b) n -> p a (b n)", a=2)
        relrow = hsig[0:H, :]
        nv = sb("n_v", [128, TT, 2, DH])
        cmpx = xn[:, 0, 0:32 * NCMP].rearrange("p (j n) -> p j n", n=NCMP)
        kcn = sb("k_cmp", [NCMP, 2, DH])
        kcT = sb("k_cmp_T", [128, NCMP])
        vpad = sb("v_cmp_T", [DH, H, 32])
        vblk = sb("v_cmp_blocks", [128, H, DH])
        pc = sb("p_cmp", [128, TT, H, 32])
        nmax = sb("neg_max", [128, 4, TT])
        lsum = sb("exp_sums", [128, 5, H, TT])
        rl = sb("inv_sums", [128, H, TT])
        rw = sb("router_w", [128, KC, N_EXP])
        topi = sb("top_index", [128, TT, 8], U32)
        at = [0]

        def listed(*shape):
            n = shape[-1]
            a = pf[:, at[0]:at[0] + (n if len(shape) == 1 else shape[0] * n)]
            at[0] += a.shape[-1]
            return a if len(shape) == 1 else a.rearrange("p (t n) -> p t n", t=shape[0])

        lg, top8, topf, tw = listed(TT, N_EXP), listed(TT, 8), listed(TT, 8), listed(TT, 4)
        wts = listed(TT, N_EXP + 1)
        picked = listed(TT, N_EXP)
        rank = listed(TT, N_EXP + 1)
        wtmp = listed(40)
        overi = sb("overflow_experts", [1, 8], mybir.dt.int32)
        pick = [acc[:, 0, 256 * q:256 * q + 256].rearrange("p (t n) -> p t n", t=TT) for q in range(2)]
        pickT = [acc[:, 1, 256 * q:256 * q + 256].rearrange("p (t n) -> p t n", t=TT) for q in range(2)]
        ysb = fT[:, :, :].rearrange("p a n -> p (a n)")
        scratch = nc.dram_tensor("rel_scratch", [H, 512], F32)

        ps = [ctx.enter_context(nc.psum_tensor(f"bank{i}", [128, 512], F32)) for i in range(8)]

        def cst(name, p=128):
            a, w = CONST[name]
            return const[0:p, a:a + w]

        def prm(l, name, p0=0, p1=128):
            a, w = PAR[name]
            return par[p0:p1, l, a:a + w]

        ident, ones = cst("ident"), cst("ones")
        ones_all, minus_all = (cst(n).to_broadcast([128, 128]) for n in ("ones", "minus_ones"))

        const_in = sem("const_in")
        x_in = sem("x_in")
        reverse_in = sem("reverse_in")
        rel_saved = sem("rel_saved")
        bias_in = sem("bias_in")
        bias_turned = sem("bias_turned")
        bias_ready = sem("bias_ready")
        gate_w_in = sem("gate_w_in")
        layer_in = sem("layer_in")
        gate2_in = sem("gate2_in")
        router_in = sem("router_in")
        out_saved = sem("out_saved")
        ring_full = [sem(f"ring_full{i}") for i in range(RING)]
        ring_free = [sem(f"ring_free{i}") for i in range(RING)]
        vec_seq = sem("vec_seq")
        act_seq = sem("act_seq")
        pool_seq = sem("pool_seq")
        rel_row = sem("rel_row_psum")
        rel_ready = sem("rel_row_ready")
        cond_exp = sem("cond_exp")
        x_sumsq = sem("x_sumsq")
        xn_ready = sem("xn_ready")
        xn_act = sem("xn_act")
        xT_done = sem("xT_done")
        mod_ready = sem("mod_ready")
        hT_act = sem("hT_act")
        hT_vec = sem("hT_vec")
        acc_ready = sem("acc_ready")
        acc_reduced = sem("acc_reduced")
        mod_evac = sem("mod_evac")
        proj_done = sem("proj_done")
        proj_evac = sem("proj_evac")
        gate_abs = sem("gate_abs")
        gate_ln = sem("gate_ln")
        gate_rows = sem("gate_rows_ready")
        gate_T = sem("gate_T")
        gate_cols = sem("gate_cols_ready")
        nm_exp = sem("nm_exp")
        conv_done = sem("conv_done")
        conv_tanh = sem("conv_tanh")
        mqk_ready = sem("mqk_ready")
        sumsq_ready = sem("sumsq_ready")
        rstd_ready = sem("rstd_ready")
        fox_norm = sem("fox_norm")
        fox_T = sem("fox_T")
        fox_T_evac = sem("fox_T_evac")
        nsa_norm = sem("nsa_norm")
        nsa_T = sem("nsa_T")
        nsa_T_evac = sem("nsa_T_evac")
        gates_exp = sem("gates_exp")
        cmpx_ready = sem("cmpx_ready")
        cmp_done = sem("cmp_done")
        kcn_ready = sem("kcn_ready")
        vpad_ready = sem("vpad_ready")
        kv_T = sem("kv_T")
        kv_T_evac = sem("kv_T_evac")
        cmp_scores = sem("cmp_scores")
        cmp_shift = sem("cmp_shift")
        cmp_exp = sem("cmp_exp")
        cmp_probs = sem("cmp_probs")
        cmp_pT = sem("cmp_pT")
        cmp_pT_evac = sem("cmp_pT_evac")
        cmp_out = sem("cmp_out")
        head_scores = sem("head_scores")
        head_shift = sem("head_shift")
        head_exp = sem("head_exp")
        stick_shift = sem("stick_shift")
        stick_exp = sem("stick_exp")
        cmp_taken = sem("cmp_taken")
        stick_sp = sem("stick_softplus")
        stick_masked = sem("stick_masked")
        head_second = sem("head_second")
        head_pT = sem("head_pT")
        head_pv = sem("head_pv")
        o_free = sem("o_free")
        mo_tanh = sem("mo_tanh")
        mix_ready = sem("mix_ready")
        mixT_done = sem("mixT_done")
        mixT_act = sem("mixT_act")
        mixT_vec = sem("mixT_vec")
        wout_done = sem("wout_done")
        x_mixed = sem("x_mixed")
        ffn = {n: sem("ffn_" + n) for n in ("g", "u", "tanh", "h", "T", "T_evac", "d", "y_0", "seq")}
        moe, over = ({n: sem(f"{p}_{n}") for n in (
            "g", "u", "tanh", "h", "T", "T_evac", "d", "onehot", "turned", "turn_evac", "gathered", "in_act", "in_vec",
            "y_0", "y_1", "scattered", "added", "act_seq", "vec_seq", "act_left",
            "vec_left")} for p in ("moe", "over"))
        picked_ready = sem("picked_ready")
        rank_done = sem("rank_done")
        over_ready = sem("over_ready")
        x_final = sem("x_final")
        router_done = sem("router_done")
        router_shift = sem("router_shift")
        router_exp = sem("router_exp")

        def slot_of(i):
            return i % RING

        def loaded(eng, n, base=0):
            eng.wait_ge(ring_full[slot_of(n)], base * 16 + 16 * (n // RING + 1))

        def slot_view(i, w):
            return ring[:, slot_of(i), 0:KC * w].rearrange("p (k n) -> p k n", k=KC)

        def slot_down(i, w):
            return ring[:, slot_of(i), 0:(w // 128) * D].rearrange("p (f n) -> p f n", n=D)

        block = ctx.enter_context(nc.Block())

        @block.sync
        def _(sp):
            for dst, src in ((ccol[:, :], "c_cols"), (table[:, :], "rel_bias"), (onehot, "onehot"), (future, "future"), (const[:, :], "const")):
                sp.dma_start(dst, t[src]).then_inc(const_in, 16)
            sp.dma_start(par[:, :, :], t["par"].rearrange("l p n -> p l n")).then_inc(const_in, 16)

            def put(n, dst, src, base=0):
                if n >= RING or not isinstance(base, int):
                    sp.wait_ge(ring_free[slot_of(n)], base + n // RING)
                sp.dma_start(dst, src).then_inc(ring_full[slot_of(n)], 16)

            def swiglu_load(n, m, c0, w, j, base=0):
                if j < 2:
                    put(n, slot_view(n, w), m[:, c0:c0 + w].rearrange("(k p) n -> p k n", p=128), base)
                else:
                    put(n, slot_down(n, w), m[c0:c0 + w, :].rearrange("(f p) n -> p f n", p=128), base)

            def gate_weights(l):
                sp.dma_start(wgate[:, :, :], t["w_gates"][l].rearrange("(k p) n -> p k n", p=128)).then_inc(gate_w_in, 16)

            def side_loads(l):
                sp.dma_start(gate[:, 0, :], t["ada_b"][l:l + 1, 2 * D:3 * D].to_broadcast([128, D])).then_inc(layer_in, 16)
                sp.dma_start(cmpw[0:DH, :, :], t["nsa_cmp_wk"][l].rearrange("(j d) e -> d j e", d=DH)).then_inc(layer_in, 16)
                sp.dma_start(cmpw[DH:128, :, :], t["nsa_cmp_wv"][l].rearrange("(j d) e -> d j e", d=DH)).then_inc(layer_in, 16)

            for n, (l, kind, c) in enumerate(SEQ):
                if n == 2:
                    for tt in range(TT):
                        sp.dma_start(x[:, tt, :], t["x"][0, tt * 128:tt * 128 + 128, :]).then_inc(x_in, 16)
                if n == 4:
                    gate_weights(0)
                    sp.dma_start(reverse, t["reverse"]).then_inc(reverse_in, 16)
                if n == RING:
                    side_loads(0)
                if (l, kind, c) == (0, "ffn", 9):
                    sp.wait_ge(x_mixed, TT)
                    gate_weights(1)
                    side_loads(1)
                if kind == "ffn":
                    c0, w = FF_UNITS[c // 3]
                    swiglu_load(n, t[("ffn_wg", "ffn_wu", "ffn_wd")[c % 3]][0], c0, w, c % 3)
                    continue
                c0, w = WIN[c] if kind == "win" else (512 * c, 512)
                m = t[{"ada": "ada_w", "win": "w_in", "wout": "w_out"}[kind]]
                put(n, slot_view(n, w), m[l, :, c0:c0 + w].rearrange("(k p) n -> p k n", p=128))
            sp.dma_start(rw[:, :, :], t["moe_router_w"][0].rearrange("(k p) n -> p k n", p=128)).then_inc(router_in, 16)
            experts = [t[n].rearrange("a e r c -> (a e r) c") for n in ("moe_wg", "moe_wu", "moe_wd")]

            def expert_loads(e, base):
                for u, (c0, w) in enumerate(FE_UNITS):
                    for j, rows in enumerate((D, D, D_FE)):
                        swiglu_load(3 * u + j, experts[j][bass.ds(e * rows, rows), :], c0, w, j, base)

            first = FIRST_EXPERT // RING
            with sp.Fori(0, N_EXP) as e:
                expert_loads(e, e * 3 + first)
            sp.wait_ge(over_ready, 1)
            n_over = sp.value_load(overi[0:1, OVER:OVER + 1], min_val=0, max_val=OVER)
            with sp.If(n_over > 0):
                with sp.Fori(0, OVER) as i:
                    with sp.If(i < n_over):
                        e = sp.value_load(overi[0:1, bass.ds(i, 1)], min_val=0, max_val=N_EXP - 1)
                        expert_loads(e, i * 3 + (first + 3 * N_EXP))
            sp.wait_ge(x_final, 2 * TT)
            for tt in range(TT):
                sp.dma_start(out[0, tt * 128:tt * 128 + 128, :], x[:, tt, :]).then_inc(out_saved, 16)
            sp.wait_ge(out_saved, 16 * TT)

        @block.gpsimd
        def _(pool):
            do = Ordered(pool, pool_seq)
            for a in (vpad[:, :, :], vblk[:, :, :], pc[:, :, :, :]):
                do(nc.gpsimd.memset(a, 0.0))
            do(nc.gpsimd.memset(mv[:, :, :, DH:DH + 1], 1.0))

        @block.scalar
        def _(act):
            do = Ordered(act, act_seq)
            act.wait_ge(const_in, 96)
            act.activation(cond[:, :], ccol[:, :], ACT.Exp, scale=-1.0).then_inc(cond_exp, 1)

            def rstd(n, p, cols, width):
                do(act.activation(small[0:p, 32:32 + cols], ss[0:p, 0:cols], ACT.Ln, scale=1.0 / width, bias=epsb[0:p, :]))
                return act.activation(rs[0:p, 0:cols], small[0:p, 32:32 + cols], ACT.Exp, scale=-0.5)

            def norm(l, which):
                n = 2 * l + which
                if n:
                    do(act.activation(small[:, 62:63], epsb, ACT.Ln))
                for tt in range(TT):
                    if n == 0:
                        act.wait_ge(x_in, 16 * TT)
                    else:
                        act.wait_ge(x_mixed if which else x_final, TT * (n // 2 + which - 1) + tt + 1)
                    do(act.activation(dump, x[:, tt, :], ACT.Square, accum_out=ss[:, tt:tt + 1]))
                do(rstd(n, 128, TT, D), x_sumsq)
                do(act.activation(xn[:, 1, :], x[:, 1, :], ACT.Copy, scale=rs[:, 1:2]), xn_act)
                if n == 0:
                    act.wait_ge(rel_ready, 1)
                    act.dma_start(scratch.ap(), relrow[:, :]).then_inc(rel_saved, 16)
                    act.dma_start(gate[:, 1, :], t["ada_b"][0:1, 5 * D:6 * D].to_broadcast([128, D])).then_inc(gate2_in, 16)
                if n == 2:
                    act.dma_start(gate[:, 1, :], t["ada_b"][1:2, 5 * D:6 * D].to_broadcast([128, D])).then_inc(gate2_in, 16)
                act.wait_ge(mod_ready, n + 1)
                for k in ACT_CHUNKS:
                    act.wait_ge(xT_done, KC * n + (k | 1) + 1)
                    do(act.activation(hT[:, k, :], ps[k // 2][:, 256 * (k % 2):256 * (k % 2) + 256], ACT.Identity,
                                      scale=scaleA[:, which, k:k + 1], bias=modc[:, (24 if which else 0) + k:(24 if which else 0) + k + 1]), hT_act)

            def mixer(l):
                for n, (c, g) in enumerate(GROUPS):
                    act.wait_ge(proj_done, NG * l + n + 1)
                    b = ps[n % 4]
                    halves = b[:, :].rearrange("p (a n) -> p a n", a=2)
                    if c is None:
                        do(act.activation(graw[:, :], b[0:48, 0:S], ACT.Copy), proj_evac)
                    elif c == 0:
                        do(act.activation(qkraw[:, 2 * g:2 * g + 2, 3:3 + S], halves, ACT.Copy), proj_evac)
                    elif c == 1:
                        do(act.activation(mv[:, g, :, 0:DH], b[:, 0:256].rearrange("p (h d) -> p h d", h=H), ACT.Copy))
                        do(act.activation(mo[:, g, :], b[:, 256:512], ACT.Copy), proj_evac)
                    elif c == 2:
                        do(act.activation(fqk[:, g, :, :], b[:, :].rearrange("p (h d) -> p h d", h=8), ACT.Copy), proj_evac)
                    elif c == 3:
                        do(act.activation(fv[:, g, :], b[:, 0:256], ACT.Copy), proj_evac)
                    elif c == 4:
                        do(act.activation(sT[:, 2 * g:2 * g + 2, :], halves, ACT.Copy, scale=1.0 if g else DH ** -0.5), proj_evac)
                    elif c == 5:
                        do(act.activation(sv[:, g, :], b[:, 0:256], ACT.Copy))
                        do(act.activation(nqk[:, g, 0:4, :], b[:, 256:512].rearrange("p (h d) -> p h d", h=H), ACT.Copy), proj_evac)
                    elif g == 0:
                        do(act.activation(kvT[:, :], b[:, 0:S], ACT.Copy), proj_evac)
                    else:
                        kv = b[:, 0:256].rearrange("p (a b d) -> p a b d", a=2, b=2)
                        do(act.activation(nqk[:, g - 1, 4:6, :], kv[:, :, 0, :], ACT.Copy))
                        do(act.activation(nqk[:, g - 1, 6, :], kv[:, 0, 0, :], ACT.Copy))
                        do(act.activation(nv[:, g - 1, :, :], kv[:, :, 1, :], ACT.Copy), proj_evac)
                    if n == 1:
                        act.wait_ge(gate_abs, l + 1)
                        do(act.activation(gl[:, :], gl[:, :], ACT.Exp, scale=-1.0))
                        do(act.activation(gl[:, :], gl[:, :], ACT.Ln, bias=1.0), gate_ln)
                    if (l, n) == (0, 2):
                        relative_bias()
                    if n == 4:
                        act.wait_ge(conv_done, l + 1)
                        do(act.activation(mqkT[:, :, :], conv[:, :, :], ACT.Tanh, scale=0.5), conv_tanh)
                        act.wait_ge(gate_cols, l + 1)
                        do(act.activation(expnm[:, :, :], gcol[:, :, 4:8], ACT.Exp), nm_exp)
                    if n == 9:
                        act.wait_ge(sumsq_ready, 4 * l + 1)
                        do(rstd(0, 128, 16, DH), rstd_ready)
                act.wait_ge(sumsq_ready, 4 * l + 2)
                do(rstd(0, 128, 14, DH), rstd_ready)
                do(act.activation(ng[:, :, 0:12], ng[:, :, 0:12], ACT.Exp, scale=-1.0), gates_exp)
                do(act.activation(mo[:, :, :], mo[:, :, :], ACT.Tanh, scale=0.5), mo_tanh)
                for step, i in ACT_ORDER:
                    kind, h = HEADS[i]
                    e = probs[i % 4]
                    if step == "k_cmp":
                        act.wait_ge(sumsq_ready, 4 * l + 3)
                        do(rstd(0, NCMP, 1, DH), rstd_ready)
                    elif step == "cmp_exp":
                        act.wait_ge(cmp_shift, l + 1)
                        do(act.activation(pc[:, :, :, 0:NCMP], pc[:, :, :, 0:NCMP], ACT.Exp), cmp_exp)
                    elif step == "abs_exp":
                        act.wait_ge(head_scores, NH * l + i + 1)
                        act.wait_ge(head_second, N_B * l + count(BKINDS, i - 4))
                        do(act.activation(e, ps[i % 4][:, 0:384], ACT.Abs))
                        do(act.activation(e, e, ACT.Exp, scale=-1.0))
                    elif step == "mlstm_rstd":
                        act.wait_ge(sumsq_ready, 4 * l + 4)
                        do(rstd(0, 128, 8, DH), rstd_ready)
                    elif step == "ln":
                        do(act.activation(e, e, ACT.Ln, bias=1.0), stick_sp)
                    elif kind == "stick":
                        act.wait_ge(stick_shift, N_STICK * l + h + 1)
                        do(act.activation(probTs[i % 4], probTs[i % 4], ACT.Exp), stick_exp)
                    else:
                        act.wait_ge(head_shift, N_P * l + count(PKINDS, i))
                        if kind == "mlstm":
                            do(act.activation(e[:, 0:256], e[:, 0:256], ACT.Exp, bias=gcol[:, 0, h:h + 1]))
                            do(act.activation(e[:, 256:384], e[:, 256:384], ACT.Exp, bias=gcol[:, 1, h:h + 1]), head_exp)
                            continue
                        for tt, (a, b) in enumerate(((0, 128), (128, 384))):
                            do(act.activation(e[:, a:b], e[:, a:b], ACT.Exp, bias=nmax[:, i % 4, tt:tt + 1],
                                              accum_out=lsum[:, i // H, h, tt:tt + 1]), head_exp if tt else None)
                for k in ACT_CHUNKS:
                    act.wait_ge(mixT_done, KC * l + (k | 1) + 1)
                    do(act.activation(hT[:, k, :], ps[k // 2][:, 256 * (k % 2):256 * (k % 2) + 256], ACT.Copy,
                                      scale=prm(l, "out_g")[:, k:k + 1]), mixT_act)

            def swiglu(f, steps, base, do, after=lambda j: None):
                for j in range(len(steps) + 1):
                    if j < len(steps):
                        st = steps[j]
                        act.wait_ge(f["g"], base + j + 1)
                        if st.last:
                            act.sem_inc(ring_free[slot_of(st.loads[0])], 1)
                        if j:
                            act.wait_ge(f["h"], base + j)
                        do(act.activation(hsig[:, 0:st.w], ps[4][:, 0:st.w], ACT.Tanh, scale=0.5), f["tanh"])
                    if j:
                        w = steps[j - 1].w
                        act.wait_ge(f["T"], base + j)
                        if j >= 3:
                            act.wait_ge(f["d"], base + j - 2)
                        do(act.activation(hbT[:, (j - 1) % 2, 0:w], ps[6][:, 0:w], ACT.Copy), f["T_evac"])
                    after(j)

            def gathered_in(f, tile, count, do):
                act.wait_ge(f["gathered"], count)
                for k in range(4):
                    do(act.activation(hT[:, k, 128 * tile:128 * tile + 128], ps[2][:, 128 * k:128 * k + 128], ACT.Identity,
                                      scale=scaleA[:, 1, k:k + 1], bias=modc[:, 24 + k:25 + k]), f["in_act"] if k == 3 else None)

            epsb = small[:, 63:64]
            dump = fT[:, :, :].rearrange("p k n -> p (k n)")

            def relative_bias():
                act.wait_ge(rel_saved, 16)
                sc = scratch.ap()
                for h in range(H):
                    for col, w, at in ((0, 128, 128), (128, 256, 0)):
                        src = bass.AP(sc.tensor, h * 512 + at, [[1, 128], [1, w]])
                        act.dma_start(bias[:, h, col:col + w], src).then_inc(bias_in, 16)
            act.wait_ge(vec_seq, 1)
            norm(0, 0)
            mixer(0)
            norm(0, 1)
            swiglu(ffn, dense_steps(), 0, do)
            norm(1, 0)
            mixer(1)
            norm(1, 1)
            act.wait_ge(router_shift, 1)
            do(act.activation(tw[:, :, 0:1], tw[:, :, 0:1], ACT.Exp), router_exp)
            gathered_in(moe, 0, 1, do)
            with act.Fori(0, N_EXP // 2) as i:
                doe = Ordered(act, moe["act_seq"])
                doe.base = {id(moe["act_seq"]): i * 6, id(moe["tanh"]): i * 14, id(moe["T_evac"]): i * 14,
                            id(moe["in_act"]): i * 2 + 1}

                def after(j):
                    if j in (3, 10):
                        gathered_in(moe, 1 - j // 7, i * 2 + (j // 7 + 2), doe)

                swiglu(moe, expert_steps(0, 0) + expert_steps(1, 0), i * 14, doe, after)
                assert doe.n[id(moe["act_seq"])] == 6
            act.wait_ge(over_ready, 1)
            n_over = act.value_load(overi[0:1, OVER:OVER + 1], min_val=0, max_val=OVER)
            with act.If(n_over > 0):
                with act.Fori(0, OVER) as i:
                    with act.If(i < n_over):
                        doe = Ordered(act, over["act_seq"])
                        doe.base = {id(over["act_seq"]): i * 3, id(over["tanh"]): i * 7, id(over["T_evac"]): i * 7,
                                    id(over["in_act"]): i}
                        gathered_in(over, 0, i + 1, doe)
                        swiglu(over, expert_steps(0, 0), i * 7, doe)
                        act.sem_inc(over["act_left"], 1)
                        assert doe.n[id(over["act_seq"])] == 3

        @block.tensor
        def _(pe):
            mm = nc.tensor.matmul

            def transpose_norm(n):
                pe.wait_ge(xn_ready, n + 1)
                pe.wait_ge(xn_act, n + 1)
                for k in range(KC):
                    for tt in range(TT):
                        o = ps[k // 2][:, 256 * (k % 2) + 128 * tt:256 * (k % 2) + 128 * tt + 128]
                        last = nc.tensor.transpose(o, xn[:, tt, 128 * k:128 * k + 128], ident)
                    last.then_inc(xT_done, 1)

            def ada_reduce(l, c):
                pe.wait_ge(acc_ready, 12 * l + c + 1)
                if l:
                    pe.wait_ge(mod_evac, 12 * l + c)
                elif c >= 2:
                    pe.wait_ge(mod_evac, c - 1)
                b = ps[7] if l else ps[6 + c % 2]
                if c in (4, 5, 10, 11):
                    last = mm(b[:, :], ones_all, acc[:, c % 2, :], start=True, stop=True)
                else:
                    for q in range(4):
                        last = mm(b[:, q:q + 1], acc[:, c % 2, 128 * q:128 * q + 128], ones, start=True, stop=True)
                last.then_inc(acc_reduced, 1)

            def mixer(l):
                if l == 0:
                    ada_reduce(0, 0)
                    ada_reduce(0, 1)
                transpose_norm(2 * l)
                if l == 0:
                    ada_reduce(0, 2)
                    ada_reduce(0, 3)
                pe.wait_ge(hT_act, 4 * (2 * l + 1))
                pe.wait_ge(hT_vec, 4 * (2 * l + 1))
                pe.wait_ge(gate_w_in, 16 * (l + 1))
                for n, (c, g) in enumerate(GROUPS):
                    b = ps[n % 4]
                    if n >= 4:
                        pe.wait_ge(proj_evac, NG * l + n - 3)
                    if c is None:
                        for k in range(KC):
                            last = mm(b[0:48, 0:S], wgate[:, k, :], hT[:, k, :], start=k == 0, stop=k == KC - 1)
                        last.then_inc(proj_done, 1)
                        continue
                    i = AT[(l, "win", c)]
                    w = slot_view(i, WIN[c][1])
                    loaded(pe, i)
                    if c in (0, 4):
                        for q in range(2):
                            for k in range(KC):
                                last = mm(b[:, 256 * q:256 * q + 256], w[:, k, 128 * (2 * g + q):128 * (2 * g + q) + 128],
                                          hT[:, k, :], start=k == 0, stop=k == KC - 1)
                    elif c == 6 and g == 0:
                        for k in range(KC):
                            last = mm(b[:, 0:S], w[:, k, 0:128], hT[:, k, :], start=k == 0, stop=k == KC - 1)
                    else:
                        tt, c0 = (g - 1, 128) if c == 6 else (g, 0)
                        cols = 512 if WIN[c][1] == 512 else 256
                        for k in range(KC):
                            last = mm(b[:, 0:cols], hT[:, k, 128 * tt:128 * tt + 128], w[:, k, c0:c0 + cols],
                                      start=k == 0, stop=k == KC - 1)
                    last.then_inc(proj_done, 1)
                    if g == (2 if c == 6 else 1):
                        pe.wait_ge(proj_done, NG * l + n + 1)
                        pe.sem_inc(ring_free[slot_of(i)], 1)
                    if n == 4:
                        pe.wait_ge(gate_rows, l + 1)
                        for tt in range(TT):
                            for r, at, w_ in ((ucap, 0, 4), (nmrow, 4, 4), (cumf, 8, 8)):
                                last = nc.tensor.transpose(ps[5][:, 16 * tt + at:16 * tt + at + w_], r[0:w_, 128 * tt:128 * tt + 128],
                                                           ident[0:w_, 0:w_])
                        for tt in range(TT):
                            last = nc.tensor.transpose(ps[4][:, 16 * tt:16 * tt + 16], graw[32:48, 128 * tt:128 * tt + 128],
                                                       ident[32:48, 32:48])
                        last.then_inc(gate_T, 1)
                    if (l, n) == (0, 5):
                        pe.wait_ge(gate_cols, 1)
                        pe.wait_ge(bias_in, 8 * 16)
                        pe.wait_ge(reverse_in, 16)
                        for h in range(H):
                            last = mm(ps[4 + h][:, 0:384], reverse, bias[:, h, :], start=True, stop=True)
                        last.then_inc(bias_turned, 1)
                    if (l, n) == (0, 6):
                        pe.wait_ge(bias_ready, 1)
                    if n in ADA_AFTER and l == 0:
                        ada_reduce(l, ADA_AFTER[n])
                    if n in (5, 7) and l:
                        ada_reduce(l, 10 + n // 6)
                    if n == 13:
                        pe.wait_ge(fox_norm, l + 1)
                        for a in range(2):
                            for q in range(2):
                                for tt in range(TT):
                                    v = 4 * a + 2 * q
                                    last = nc.tensor.transpose(ps[4 + a][:, 256 * q + 128 * tt:256 * q + 128 * tt + 128],
                                                               fqk[:, tt, v:v + 2, :].rearrange("p v d -> p (v d)"), ident)
                            last.then_inc(fox_T, 1)
                pe.wait_ge(mod_evac, 12 * l + 12)
                def first(i):
                    kind, h = HEADS[i]
                    b = ps[i % 2 if kind == "mlstm" else i % 4]
                    j = i - 2 if i < 6 else i - 4
                    if i == 0:
                        pe.wait_ge(proj_evac, NG * l + NG)
                        pe.wait_ge(mqk_ready, l + 1)
                    elif j >= 0 and HEADS[j][0] == "stick":
                        pe.wait_ge(stick_shift, N_STICK * l + HEADS[j][1] + 1)
                    elif j >= 0:
                        pe.wait_ge(head_pT, N_P * l + count(PKINDS, j))
                    if kind in ("mlstm", "stick"):
                        T_ = mqkT if kind == "mlstm" else sT
                        p0 = DH * (h % 2)
                        q, k = T_[p0:p0 + DH, h // 2, :], T_[p0:p0 + DH, 2 + h // 2, :]
                        mm(b[:, 0:256], k[:, 0:128], q, start=True, stop=False, skip_group_check=True)
                        last = mm(b[:, 256:384], k[:, 128:256], q[:, 128:256], start=False, stop=True, skip_group_check=True)
                        if kind == "mlstm":
                            last = mm(ps[2 + i % 2][:, 0:256], ident[0:H, h:h + 1].to_broadcast([H, 128]), negm[:, :],
                                      start=True, stop=True)
                    else:
                        r = slice(DH * (h % 2), DH * (h % 2) + DH)
                        if kind == "fox":
                            q, k = fT[r, h // 2, :], fT[r, 2 + h // 2, :]
                        else:
                            q, k = nT[r, h // 2, :], nT[r, 2 + ((h % 2) ^ (kind == "win")), :]
                        fox = kind == "fox"
                        mm(b[:, 0:128], q[:, 0:128], k[:, 0:128], start=True, stop=not fox, skip_group_check=True)
                        last = mm(b[:, 128:384], q[:, 128:256], k, start=False, stop=not fox, skip_group_check=True)
                        if fox:
                            sel = ident[0:8, H + h:H + h + 1].to_broadcast([8, 128])
                            mm(b[:, 0:128], sel, negf[:, 0:128], start=False, stop=True, skip_group_check=True)
                            last = mm(b[:, 128:384], sel, negf[:, :], start=False, stop=True, skip_group_check=True)
                    last.then_inc(head_scores, 1)

                def second(i):
                    kind, h = HEADS[i]
                    if kind == "mlstm":
                        return
                    e = probs[i % 4]
                    if kind == "stick":
                        pe.wait_ge(stick_masked, N_STICK * l + h + 1)
                        b = ps[i % 4]
                        tri = cst("minus_tri")
                        mm(b[:, 0:256], tri, e[:, 0:256], start=False, stop=False, skip_group_check=True)
                        mm(b[:, 128:256], minus_all, e[:, 256:384], start=False, stop=False, skip_group_check=True)
                        last = mm(b[:, 256:384], tri, e[:, 256:384], start=False, stop=True, skip_group_check=True)
                    else:
                        pe.wait_ge(head_exp, N_P * l + count(PKINDS, i))
                        for q in range(3):
                            last = nc.tensor.transpose(ps[i % 4][:, 128 * q:128 * q + 128], e[:, 128 * q:128 * q + 128], ident)
                    last.then_inc(head_second, 1)

                def third(i):
                    kind, h = HEADS[i]
                    gi = i // H
                    if kind == "stick":
                        pe.wait_ge(stick_exp, N_STICK * l + h + 1)
                    else:
                        pe.wait_ge(head_pT, N_P * l + count(PKINDS, i))
                    if h == 0:
                        if gi >= 2:
                            pe.wait_ge(o_free, 5 * l + gi - 1)
                        elif gi == 0:
                            pe.wait_ge(nsa_T_evac, 2 * l + 2)
                        else:
                            pe.wait_ge(cmp_taken, l + 1)
                    if kind == "mlstm":
                        v = [mv[:, tt, h, :] for tt in range(TT)]
                    elif kind in ("fox", "stick"):
                        v = [(fv if kind == "fox" else sv)[:, tt, DH * h:DH * h + DH] for tt in range(TT)]
                    else:
                        v = [nv[:, tt, int(kind == "win"), :] for tt in range(TT)]
                    w = v[0].shape[-1]
                    pt = probTs[i % 4]
                    o = [ps[4 + 2 * (gi % 2) + tt][:, w * h:w * h + w] for tt in range(TT)]
                    mm(o[0], pt[:, 0:128], v[0], start=True, stop=True)
                    mm(o[1], pt[:, 128:256], v[0], start=True, stop=False)
                    last = mm(o[1], pt[:, 256:384], v[1], start=False, stop=True)
                    last.then_inc(head_pv, 1)

                def compress(_):
                    pe.wait_ge(layer_in, 48 * (l + 1))
                    pe.wait_ge(cmpx_ready, l + 1)
                    for j in range(32):
                        mm(ps[6][0:NCMP, 0:DH], cmpx[0:DH, j, :], cmpw[0:DH, j, :], start=j == 0, stop=j == 31)
                    for j in range(32):
                        last = mm(ps[7][0:DH, 0:NCMP], cmpw[DH:128, j, :], cmpx[DH:128, j, :], start=j == 0, stop=j == 31)
                    last.then_inc(cmp_done, 1)

                def nsa_transposes(_):
                    pe.wait_ge(nsa_norm, l + 1)
                    pe.wait_ge(fox_T_evac, 2 * (l + 1))
                    for a in range(2):
                        for q in range(2):
                            v = 2 * q if a == 0 else 4 + q
                            for tt in range(TT):
                                last = nc.tensor.transpose(ps[4 + a][:, 256 * q + 128 * tt:256 * q + 128 * tt + 128],
                                                           nqk[:, tt, v:v + 2, :].rearrange("p v d -> p (v d)"), ident)
                        last.then_inc(nsa_T, 1)

                def kv_transposes(_):
                    pe.wait_ge(kcn_ready, l + 1)
                    pe.wait_ge(vpad_ready, l + 1)
                    nc.tensor.transpose(ps[6][:, 0:NCMP], kcn[:, :, :].rearrange("p a d -> p (a d)"), ident[0:NCMP, 0:NCMP])
                    last = nc.tensor.transpose(ps[7][:, 0:DH], vpad[:, :, :].rearrange("p h n -> p (h n)"), ident[0:DH, 0:DH])
                    last.then_inc(kv_T, 1)

                def compressed_scores(_):
                    pe.wait_ge(kv_T_evac, l + 1)
                    pe.wait_ge(nsa_T_evac, 2 * l + 2)
                    for tt in range(TT):
                        for h in range(H):
                            c0 = 16 * (2 * tt + h // 2)
                            r = slice(DH * (h % 2), DH * (h % 2) + DH)
                            last = mm(ps[6 + h % 2][:, c0:c0 + NCMP], nT[r, h // 2, 128 * tt:128 * tt + 128], kcT[r, :], start=True, stop=True)
                    last.then_inc(cmp_scores, 1)

                def cmp_turn(_):
                    pe.wait_ge(cmp_probs, l + 1)
                    for tt in range(TT):
                        last = nc.tensor.transpose(ps[6][:, 128 * tt:128 * tt + 128], pc[:, tt, :, :].rearrange("p h n -> p (h n)"), ident)
                    last.then_inc(cmp_pT, 1)

                def cmp_product(_):
                    pe.wait_ge(cmp_pT_evac, l + 1)
                    for tt in range(TT):
                        last = mm(ps[7][:, 256 * tt:256 * tt + 256], pcT[:, tt, :], vblk[:, :, :].rearrange("p h d -> p (h d)"),
                                  start=True, stop=True)
                    last.then_inc(cmp_out, 1)

                does = {"first": first, "second": second, "third": third, "compress": compress, "nsa_T": nsa_transposes,
                        "kv_T": kv_transposes, "cmp_scores": compressed_scores, "cmp_turn": cmp_turn, "cmp_out": cmp_product}
                for step, i in PE_ORDER:
                    does[step](i)

                pe.wait_ge(mix_ready, l + 1)
                for k in range(KC):
                    for tt in range(TT):
                        o = ps[k // 2][:, 256 * (k % 2) + 128 * tt:256 * (k % 2) + 128 * tt + 128]
                        last = nc.tensor.transpose(o, mix[:, tt, 128 * k:128 * k + 128], ident)
                    last.then_inc(mixT_done, 1)
                pe.wait_ge(mixT_act, 4 * (l + 1))
                pe.wait_ge(mixT_vec, 4 * (l + 1))
                for half in range(2):
                    i = AT[(l, "wout", half)]
                    loaded(pe, i)
                    for tt in range(TT):
                        for k in range(KC):
                            last = mm(ps[4 + 2 * half + tt][:, :], hT[:, k, 128 * tt:128 * tt + 128], slot_view(i, 512)[:, k, :],
                                      start=k == 0, stop=k == KC - 1)
                        last.then_inc(wout_done, 1)
                    pe.wait_ge(wout_done, 4 * l + 2 * half + 2)
                    pe.sem_inc(ring_free[slot_of(i)], 1)

            def swiglu(f, steps, base, before_up=lambda j: None, before_down=lambda j: None, after=lambda j: None):
                def up(j, part):
                    st = steps[j]
                    n, w = st.loads[part], st.w
                    if st.first:
                        loaded(pe, n, st.rounds)
                    if j:
                        pe.wait_ge(f["h"], base + j)
                    for k in range(KC):
                        last = mm(ps[4 + part][:, 0:w], hT[:, k, 128 * st.tile:128 * st.tile + 128], slot_view(n, w)[:, k, :],
                                  start=k == 0, stop=k == KC - 1)
                    last.then_inc(f["gu"[part]], 1)

                def turn(j):
                    pe.wait_ge(f["h"], base + j + 1)
                    for q in range(steps[j].w // 128):
                        last = nc.tensor.transpose(ps[6][:, 128 * q:128 * q + 128], hbuf[:, j % 2, 128 * q:128 * q + 128], ident)
                    last.then_inc(f["T"], 1)

                def down(j):
                    st = steps[j]
                    nf = st.w // 128
                    if st.first:
                        loaded(pe, st.loads[2], st.rounds)
                    pe.wait_ge(f["T_evac"], base + j + 1)
                    for half in range(2):
                        for q in range(nf):
                            last = mm(ps[st.y + half][:, :], hbT[:, j % 2, 128 * q:128 * q + 128],
                                      slot_down(st.loads[2], st.w)[:, q, 512 * half:512 * half + 512],
                                      start=st.begin and q == 0, stop=st.end and q == nf - 1)
                        if f is ffn and st.end and half == 0:
                            last.then_inc(f["y_0"], 1)
                    last.then_inc(f["d"], 1)

                def free_down(j):
                    if steps[j].last:
                        pe.wait_ge(f["d"], base + j + 1)
                        pe.sem_inc(ring_free[slot_of(steps[j].loads[2])], 1)

                for j in range(len(steps) + 1):
                    if j < len(steps):
                        before_up(j)
                        up(j, 0)
                    if j >= 2:
                        free_down(j - 2)
                    if j:
                        turn(j - 1)
                    if j < len(steps):
                        up(j, 1)
                    if j:
                        before_down(j - 1)
                        down(j - 1)
                    after(j)
                free_down(len(steps) - 1)

            def gather(f, q, count, added=None):
                pe.wait_ge(f["onehot"], count)
                for tt in range(TT):
                    last = nc.tensor.transpose(ps[7][:, 128 * tt:128 * tt + 128], pick[q][:, tt, :], ident)
                last.then_inc(f["turned"], 1)
                if added is not None:
                    pe.wait_ge(f["added"], added)
                for k in range(KC):
                    for tt in range(TT):
                        last = mm(ps[2 + k // 4][:, 128 * (k % 4):128 * (k % 4) + 128], xn[:, tt, 128 * k:128 * k + 128],
                                  pick[q][:, tt, :], start=tt == 0, stop=tt == TT - 1)
                last.then_inc(f["gathered"], 1)

            def scatter(f, q, half, y_count, turns, added=None, bank=2):
                pe.wait_ge(f["y_1" if half else "y_0"], y_count)
                pe.wait_ge(f["turn_evac"], turns)
                if added is not None:
                    pe.wait_ge(f["added"], added)
                for tt in range(TT):
                    last = mm(ps[bank + tt][:, :], pickT[q][:, tt, :], ysb[:, 512 * half:512 * half + 512], start=True, stop=True)
                last.then_inc(f["scattered"], 1)

            pe.wait_ge(const_in, 96)
            mm(ps[0][0:H, :], table[:, :], onehot, start=True, stop=True).then_inc(rel_row, 1)
            pe.wait_ge(rel_ready, 1)
            mixer(0)
            transpose_norm(1)
            pe.wait_ge(hT_act, 8)
            pe.wait_ge(hT_vec, 8)
            swiglu(ffn, dense_steps(), 0, after=lambda j: ada_reduce(1, j - 1) if 1 <= j < 11 else None)
            mixer(1)
            transpose_norm(3)
            pe.wait_ge(hT_act, 16)
            pe.wait_ge(hT_vec, 16)
            pe.wait_ge(router_in, 16)
            for tt in range(TT):
                for k in range(KC):
                    last = mm(ps[7][:, 8 * tt:8 * tt + 8], hT[:, k, 128 * tt:128 * tt + 128], rw[:, k, :], start=k == 0, stop=k == KC - 1)
            last.then_inc(router_done, 1)
            pe.wait_ge(picked_ready, 1)
            for tt in range(TT):
                c = ps[6][:, 8 * tt:8 * tt + 8]
                mm(c, ones_all, picked[:, 0, :], start=True, stop=False)
                if tt:
                    mm(c, ones_all, picked[:, 1, :], start=False, stop=False)
                mm(c, cst("minus_tri"), picked[:, tt, :], start=False, stop=True)
            for tt in range(TT):
                last = mm(ps[6][:, 16:24], ones_all, picked[:, tt, :], start=tt == 0, stop=tt == TT - 1)
            last.then_inc(rank_done, 1)
            gather(moe, 0, 1)
            first = FIRST_EXPERT // RING
            with pe.Fori(0, N_EXP // 2) as i:
                def before_up(j):
                    if j in (0, 7):
                        pe.wait_ge(moe["in_act"], i * 2 + (j // 7 + 1))
                        pe.wait_ge(moe["in_vec"], i * 2 + (j // 7 + 1))

                def before_down(j):
                    if j in (0, 7):
                        pe.wait_ge(moe["y_0"], i * 2 + (j // 7 + 1))
                        pe.wait_ge(moe["y_1"], i * 2 + (j // 7 + 1))

                def after(j):
                    q, u = divmod(j, 7)
                    if j == 14:
                        return
                    if u == 1:
                        scatter(moe, 1 - q, 0, i * 2 + (q + 1), i * 2 + (q + 1))
                    if u == 2:
                        scatter(moe, 1 - q, 1, i * 2 + (q + 1), i * 2 + (q + 1), i * 4 + (2 * q + 1))
                    if u == 3:
                        gather(moe, 1 - q, i * 2 + (q + 2), i * 4 + (2 * q + 2))

                swiglu(moe, expert_steps(0, i * 6 + first) + expert_steps(1, i * 6 + (first + 3)), i * 14, before_up, before_down, after)
            for half in range(2):
                scatter(moe, 1, half, N_EXP + 1, N_EXP, None if half else 2 * N_EXP, bank=6 if half else 2)
            pe.wait_ge(over_ready, 1)
            n_over = pe.value_load(overi[0:1, OVER:OVER + 1], min_val=0, max_val=OVER)
            with pe.If(n_over > 0):
                with pe.Fori(0, OVER) as i:
                    with pe.If(i < n_over):
                        gather(over, 0, i + 1)
                        pe.wait_ge(over["in_act"], i + 1)
                        pe.wait_ge(over["in_vec"], i + 1)
                        swiglu(over, expert_steps(0, i * 3 + (first + 3 * N_EXP)), i * 7)
                        scatter(over, 0, 0, i + 1, i + 1)
                        scatter(over, 0, 1, i + 1, i + 1, i * 2 + 1)

        @block.vector
        def _(dve):
            do = Ordered(dve, vec_seq)
            V = nc.vector
            TTop, TS, STT = V.tensor_tensor, V.tensor_scalar, V.scalar_tensor_tensor
            do(V.memset(small[:, 63:64], EPS))
            dve.wait_ge(const_in, 96)
            dve.wait_ge(rel_row, 1)
            do(TTop(relrow[:, :], ps[0][0:H, :], future, ALU.add), rel_ready)
            dve.wait_ge(cond_exp, 1)
            do(TS(cond[:, :], cond[:, :], 1.0, None, ALU.add))
            do(V.reciprocal(cond[:, :], cond[:, :]))
            do(TTop(cond[:, :], cond[:, :], ccol[:, :], ALU.mult))

            def ada_sum(l, c):
                i = AT[(l, "ada", c)]
                loaded(dve, i)
                if 12 * l + c >= 2:
                    dve.wait_ge(acc_reduced, 12 * l + c - 1)
                w, a = slot_view(i, 512), acc[:, c % 2, :]
                do(TS(a, w[:, 0, :], cond[:, 0:1], None, ALU.mult))
                for k in range(1, KC):
                    ins = STT(a, w[:, k, :], cond[:, k:k + 1], a, ALU.mult, ALU.add)
                    do(ins, acc_ready if k == KC - 1 else None)
                dve.sem_inc(ring_free[slot_of(i)], 1)

            def ada_take(l, c):
                dve.wait_ge(acc_reduced, 12 * l + c + 1)
                b = ps[7] if l else ps[6 + c % 2]
                if c in (4, 5, 10, 11):
                    if c == 4:
                        dve.wait_ge(layer_in, 48 * (l + 1))
                    if c == 10:
                        dve.wait_ge(gate2_in, 16 * (l + 1))
                    g = gate[:, c // 6, 512 * (c % 2):512 * (c % 2) + 512]
                    do(TTop(g, b[:, :], g, ALU.add), mod_evac)
                else:
                    do(TTop(modc[:, 4 * c:4 * c + 4], b[:, 0:4], prm(l, "ada_b")[:, 4 * c:4 * c + 4], ALU.add), mod_evac)

            def mod_scale(l, which):
                sc = modc[:, 24 * which + 8:24 * which + 16]
                do(STT(scaleA[:, which, :], sc, 1.0, prm(l, "norm2" if which else "norm1"), ALU.add, ALU.mult), mod_ready)

            def normalise(n):
                dve.wait_ge(x_sumsq, n + 1)
                do(TS(xn[:, 0, :], x[:, 0, :], rs[:, 0:1], None, ALU.mult), xn_ready)

            def modulate(n, which):
                for k in VEC_CHUNKS:
                    dve.wait_ge(xT_done, KC * n + (k | 1) + 1)
                    do(TS(hT[:, k, :], ps[k // 2][:, 256 * (k % 2):256 * (k % 2) + 256], scaleA[:, which, k:k + 1],
                          modc[:, 24 * which + k:24 * which + k + 1], ALU.mult, ALU.add), hT_vec)

            def bc(ap, n):
                s = list(ap.shape)
                return (ap.rearrange("p (a o) -> p a o", o=1) if len(s) == 2 else ap.rearrange("p a (b o) -> p a b o", o=1)).to_broadcast(s + [n])

            def sumsq(src, dst, n):
                for a in range(0, n, 8):
                    m = min(8, n - a)
                    sq = wide[0:src.shape[0], 0:m * DH].rearrange("p (a d) -> p a d", d=DH)
                    do(TTop(sq, src[:, a:a + m, :], src[:, a:a + m, :], ALU.mult))
                    last = V.tensor_reduce(dst[:, a:a + m], sq, AX.X, ALU.add)
                    if a + m < n:
                        do(last)
                return last

            def mixer(l):
                ada_sum0, ada_take0 = ((lambda c: ada_sum(0, c)), (lambda c: ada_take(0, c))) if l == 0 else (lambda c: None,) * 2
                if l == 0:
                    ada_sum(0, 0)
                    ada_sum(0, 1)
                    ada_take(0, 0)
                normalise(2 * l)
                do(V.memset(qkraw[:, :, 0:3], 0.0))
                if l == 0:
                    for c in range(2, 4):
                        ada_sum(0, c)
                        ada_take(0, c - 1)
                    ada_take(0, 3)
                    mod_scale(0, 0)
                modulate(2 * l, 0)
                dve.wait_ge(proj_evac, NG * l + 1)
                gb = prm(l, "gate_bias")
                do(TS(gz[:, :], graw[0:8, :], gb[0:8, :], None, ALU.add))
                do(TS(ig0[:, :], graw[32:36, :], gb[32:36, :], None, ALU.add))
                do(STT(gl[:, :], gz[:, :], -1.0, gz[:, :], ALU.mult, ALU.max), gate_abs)
                dve.wait_ge(gate_ln, l + 1)
                do(STT(gz[:, :], gz[:, :], 0.0, gl[:, :], ALU.min, ALU.subtract))
                do(TS(gl[:, :], gl[:, :], 0.0, 1.0, ALU.mult, ALU.add))
                do(V.tensor_tensor_scan(cumf[:, :], gl[:, :], gz[:, :], 0.0, ALU.mult, ALU.add))
                do(TS(negf[:, :], cumf[:, :], -1.0, None, ALU.mult))
                do(TTop(ucap, cumf[0:H, :], ig0, ALU.subtract))
                do(V.tensor_tensor_scan(negm[:, :], ucap, ucap, 0.0, ALU.min, ALU.min))
                do(TTop(ucap, ig0, cumf[0:H, :], ALU.subtract))
                do(TTop(nmrow, negm[:, :], cumf[0:H, :], ALU.subtract), gate_rows)
                dve.wait_ge(proj_evac, NG * l + 3)
                if l == 0:
                    dve.wait_ge(pool_seq, 4)
                cw = prm(l, "conv")
                for q in range(4):
                    o = conv[:, q, :]
                    do(TS(o, qkraw[:, q, 3:3 + S], cw[:, 4 * q:4 * q + 1], None, ALU.mult))
                    for j in range(1, 4):
                        ins = STT(o, qkraw[:, q, 3 - j:3 - j + S], cw[:, 4 * q + j:4 * q + j + 1], o, ALU.mult, ALU.add)
                        do(ins, conv_done if (q, j) == (3, 3) else None)
                dve.wait_ge(gate_T, l + 1)
                do(V.tensor_copy(gcol[:, :, :], ps[5][:, 0:32].rearrange("p (a n) -> p a n", a=2)))
                nb = prm(l, "nsa_gate_b").rearrange("p (o n) -> p o n", o=1).to_broadcast([128, TT, 12])
                do(TTop(ng[:, :, 0:12], ps[4][:, 0:32].rearrange("p (a n) -> p a n", a=2)[:, :, 4:16], nb, ALU.add), gate_cols)
                ada_sum0(4)
                ada_sum0(5)
                if l == 0:
                    dve.wait_ge(bias_turned, 1)
                    for h in range(H):
                        do(V.tensor_copy(bias[:, h, :], ps[4 + h][:, 0:384]), bias_ready if h == H - 1 else None)
                dve.wait_ge(conv_tanh, l + 1)
                do(STT(mqkT[:, :, :], mqkT[:, :, :], 1.0, conv[:, :, :], ALU.add, ALU.mult), mqk_ready)
                if l:
                    ada_take(1, 10)
                    ada_take(1, 11)
                ada_take0(4)
                ada_sum0(6)
                ada_take0(5)
                ada_sum0(7)
                dve.wait_ge(proj_evac, NG * l + 7)
                fall = fqk[:, :, :, :].rearrange("p t v d -> p (t v) d")
                do(sumsq(fall, ss[:, 0:16], 16), sumsq_ready)
                ada_take0(6)
                ada_sum0(8)
                ada_take0(7)
                ada_sum0(9)
                dve.wait_ge(rstd_ready, 4 * l + 1)
                do(TTop(fall, fall, bc(rs[:, 0:16], DH), ALU.mult), fox_norm)
                fg = small[:, 0:1]
                do(TS(fg, prm(l, "fox_q"), DH ** -0.5, None, ALU.mult))
                do(TS(small[:, 2:3], prm(l, "nsa_q"), DH ** -0.5, None, ALU.mult))
                ada_take0(8)
                ada_sum0(10)
                ada_take0(9)
                ada_sum0(11)
                ada_take0(10)
                ada_take0(11)
                if l == 0:
                    mod_scale(0, 1)
                for a in range(2):
                    dve.wait_ge(fox_T, 2 * l + a + 1)
                    do(TS(fT[:, 2 * a:2 * a + 2, :], ps[4 + a][:, :].rearrange("p (h n) -> p h n", h=2),
                          prm(l, "fox_k") if a else fg, None, ALU.mult), fox_T_evac)
                dve.wait_ge(proj_evac, NG * l + 14)
                for n in range(NCMP):
                    last = TTop(cmpx[:, :, n], kvT[:, 16 * n:16 * n + 32], prm(l, "cmp_pos"), ALU.add)
                    do(last, cmpx_ready if n == NCMP - 1 else None)
                dve.wait_ge(proj_evac, NG * l + NG)
                nall = nqk[:, :, :, :].rearrange("p t v d -> p (t v) d")
                do(sumsq(nall, ss[:, 0:14], 14), sumsq_ready)
                def part1(i):
                    kind, h = HEADS[i]
                    e = probs[i % 4]
                    if kind == "stick":
                        b = ps[i % 4][:, 0:384]
                        dve.wait_ge(stick_sp, N_STICK * l + h + 1)
                        do(STT(e, b, 0.0, e, ALU.max, ALU.add))
                        do(STT(e, cst("strict_T"), 0.0, e, ALU.is_ge, ALU.mult), stick_masked)
                        return
                    dve.wait_ge(head_scores, NH * l + i + 1)
                    if i >= 4 and HEADS[i - 4][0] in BKINDS:
                        dve.wait_ge(head_second, N_B * l + count(BKINDS, i - 4))
                    if kind == "mlstm":
                        m = ps[2 + i % 2]
                        mask = cst("causal_T")
                        do(TTop(e[:, 0:256], m[:, 0:256], mask[:, 0:256], ALU.add))
                        do(TTop(e[:, 256:384], m[:, 128:256], mask[:, 256:384], ALU.add), head_shift)
                        return
                    b = ps[i % 4][:, 0:384]
                    if kind == "fox":
                        for tt, (c0, c1) in enumerate(((0, 128), (128, 384))):
                            do(STT(e[:, c0:c1], b[:, c0:c1], gcol[:, tt, 12 + h:13 + h], cst("causal")[:, c0:c1], ALU.add, ALU.add))
                    else:
                        do(TTop(e, b, bias[:, h, :], ALU.add))
                    do(V.tensor_reduce(nmax[:, i % 4, 0:1], e[:, 0:128], AX.X, ALU.max, negate=True))
                    do(V.tensor_reduce(nmax[:, i % 4, 1:2], e[:, 128:384], AX.X, ALU.max, negate=True), head_shift)

                def part2(i):
                    kind, h = HEADS[i]
                    e, b, pt = probs[i % 4], ps[i % 2 if kind == "mlstm" else i % 4][:, 0:384], probTs[i % 4]
                    if i >= 4:
                        dve.wait_ge(head_pv, NH * l + i - 3)
                    if kind == "mlstm":
                        dve.wait_ge(head_exp, N_P * l + count(PKINDS, i))
                        do(STT(pt, b, 0.25 * DH ** -0.5, e, ALU.mult, ALU.mult), head_pT)
                    elif kind == "stick":
                        dve.wait_ge(head_second, N_B * l + count(BKINDS, i))
                        do(TTop(pt, b, cst("strict_T"), ALU.add), stick_shift)
                    else:
                        dve.wait_ge(head_second, N_B * l + count(BKINDS, i))
                        do(V.tensor_copy(pt, b), head_pT)

                def finish(gi):
                    kind = HEADS[H * gi][0]
                    dve.wait_ge(head_pv, NH * l + H * gi + H)
                    o = [ps[4 + 2 * (gi % 2) + tt] for tt in range(TT)]
                    cols = {"mlstm": 0, "fox": 256, "stick": 512}.get(kind, 768)
                    dst = [mix[:, tt, cols:cols + 256].rearrange("p (h d) -> p h d", h=H) for tt in range(TT)]
                    if kind == "mlstm":
                        for tt in range(TT):
                            ov = o[tt][:, 0:H * (DH + 1)].rearrange("p (h d) -> p h d", h=H)
                            dn = small[:, 8:12]
                            do(V.tensor_copy(dn.rearrange("p (h o) -> p h o", o=1), ov[:, :, DH:DH + 1]))
                            do(STT(dn, dn, -1.0, dn, ALU.mult, ALU.max))
                            do(TTop(dn, dn, expnm[:, tt, :], ALU.max))
                            do(V.reciprocal(dn, dn))
                            do(TTop(mh[:, tt, :, :], ov[:, :, 0:DH], bc(dn, DH), ALU.mult), o_free if tt else None)
                        mall = mh[:, :, :, :].rearrange("p t h d -> p (t h) d")
                        do(sumsq(mall, ss[:, 0:8], 8), sumsq_ready)
                        return
                    if kind == "stick":
                        for tt in range(TT):
                            do(V.tensor_copy(dst[tt], o[tt][:, 0:256].rearrange("p (h d) -> p h d", h=H)), o_free if tt else None)
                        return
                    do(V.reciprocal(rl[:, :, :], lsum[:, gi, :, :]))
                    if kind in ("sel", "win"):
                        gcolumn = 1 if kind == "sel" else 2
                        gv = ng[:, :, 0:12].rearrange("p t (h c) -> p h t c", c=3)[:, :, :, gcolumn]
                        do(TTop(rl[:, :, :], rl[:, :, :], gv, ALU.mult))
                    for tt in range(TT):
                        ov = o[tt][:, 0:256].rearrange("p (h d) -> p h d", h=H)
                        r = rl[:, :, tt:tt + 1].to_broadcast([128, H, DH])
                        if kind in ("sel", "win"):
                            wd = wide[:, 256 * tt:256 * tt + 256].rearrange("p (h d) -> p h d", h=H)
                            do(TTop(wd, ov, r, ALU.mult), o_free if tt else None)
                            do(TTop(dst[tt], dst[tt], wd, ALU.add), mix_ready if (kind, tt) == ("win", 1) else None)
                        else:
                            do(TTop(dst[tt], ov, r, ALU.mult), o_free if tt else None)

                def finish_mlstm(_):
                    dve.wait_ge(rstd_ready, 4 * l + 4)
                    mall = mh[:, :, :, :].rearrange("p t h d -> p (t h) d")
                    do(TS(rs[:, 0:8], rs[:, 0:8], 0.5, None, ALU.mult))
                    do(TTop(mall, mall, bc(rs[:, 0:8], DH), ALU.mult))
                    dve.wait_ge(mo_tanh, l + 1)
                    do(STT(mix[:, :, 0:256], mo[:, :, :], 1.0, mh[:, :, :, :].rearrange("p t h d -> p t (h d)"), ALU.add, ALU.mult))

                pcv = pc[:, :, :, 0:NCMP].rearrange("p t h n -> p (t h) n")

                def nsa_scale(_):
                    dve.wait_ge(rstd_ready, 4 * l + 2)
                    do(TTop(nall, nall, bc(rs[:, 0:14], DH), ALU.mult), nsa_norm)

                def k_compressed(_):
                    dve.wait_ge(cmp_done, l + 1)
                    do(V.tensor_copy(kcn[:, :, :], ps[6][0:NCMP, 0:DH].rearrange("p (o d) -> p o d", o=1).to_broadcast([NCMP, 2, DH])))
                    vv = ps[7][0:DH, 0:NCMP].rearrange("p (o n) -> p o n", o=1).to_broadcast([DH, H, NCMP])
                    do(V.tensor_copy(vpad[:, :, 0:NCMP], vv), vpad_ready)
                    do(sumsq(kcn[:, 0:1, :], ss[0:NCMP, 0:1], 1), sumsq_ready)

                def nsa_columns(_):
                    dve.wait_ge(rstd_ready, 4 * l + 3)
                    do(TS(kcn[:, :, :], kcn[:, :, :], rs[0:NCMP, 0:1], None, ALU.mult), kcn_ready)
                    dve.wait_ge(nsa_T, 2 * l + 1)
                    do(TS(nT[:, 0:2, :], ps[4][:, :].rearrange("p (h n) -> p h n", h=2), small[:, 2:3], None, ALU.mult), nsa_T_evac)
                    dve.wait_ge(nsa_T, 2 * l + 2)
                    for q in range(2):
                        do(TS(nT[:, 2 + q, :], ps[5][:, 256 * q:256 * q + 256], prm(l, "nsa_k")[:, 1 + q:2 + q], None, ALU.mult),
                           nsa_T_evac if q else None)

                def kv_columns(_):
                    dve.wait_ge(kv_T, l + 1)
                    do(TS(kcT[:, :], ps[6][:, 0:NCMP], prm(l, "nsa_k")[:, 0:1], None, ALU.mult))
                    for h in range(H):
                        r = slice(32 * h, 32 * h + NCMP)
                        do(V.tensor_copy(vblk[r, h, :], ps[7][r, 0:DH]), kv_T_evac if h == H - 1 else None)

                def nsa_gates(_):
                    dve.wait_ge(gates_exp, l + 1)
                    do(TS(ng[:, :, 0:12], ng[:, :, 0:12], 1.0, None, ALU.add))
                    do(V.reciprocal(ng[:, :, 0:12], ng[:, :, 0:12]))

                    if l == 0:
                        do(V.memset(biasc[:, :, :], -1e30))
                        do(V.tensor_copy(biasc[:, 0:4, 0:7], bias[:, :, 31:128:16]))
                        do(V.tensor_copy(biasc[:, 4:8, :], bias[:, :, 128 + 31:384:16]))

                def cmp_exponents(_):
                    dve.wait_ge(cmp_scores, l + 1)
                    for q in range(2):
                        sc = ps[6 + q][:, 0:64].rearrange("p (a n) -> p a n", a=4)[:, :, 0:NCMP]
                        do(TTop(pcv[:, q:8:2, :], sc, biasc[:, q:8:2, :], ALU.add))
                    do(V.tensor_reduce(small[:, 16:24], pcv, AX.X, ALU.max))
                    do(TTop(pcv, pcv, bc(small[:, 16:24], NCMP), ALU.subtract), cmp_shift)

                def cmp_weights(_):
                    dve.wait_ge(cmp_exp, l + 1)
                    do(V.tensor_reduce(small[:, 16:24], pcv, AX.X, ALU.add))
                    do(V.reciprocal(small[:, 16:24], small[:, 16:24]))
                    g0 = ng[:, :, 0:12].rearrange("p t (h c) -> p t h c", c=3)[:, :, :, 0]
                    s3 = small[:, 16:24].rearrange("p (t h) -> p t h", t=TT)
                    do(TTop(s3, s3, g0, ALU.mult))
                    do(TTop(pcv, pcv, bc(small[:, 16:24], NCMP), ALU.mult))
                    for tt in range(TT):
                        valid = cst("valid_cmp")[:, NCMP * tt:NCMP * tt + NCMP].rearrange("p (o n) -> p o n", o=1).to_broadcast([128, H, NCMP])
                        do(TTop(pc[:, tt, :, 0:NCMP], pc[:, tt, :, 0:NCMP], valid, ALU.mult), cmp_probs if tt else None)

                def cmp_turned(_):
                    dve.wait_ge(cmp_pT, l + 1)
                    do(V.tensor_copy(pcT[:, :, :], ps[6][:, 0:256].rearrange("p (t n) -> p t n", t=TT)), cmp_pT_evac)

                def cmp_take(_):
                    dve.wait_ge(cmp_out, l + 1)
                    do(V.tensor_copy(mix[:, :, 768:1024], ps[7][:, :].rearrange("p (t n) -> p t n", t=TT)), cmp_taken)

                does = {"part1": part1, "part2": part2, "finish": finish, "mlstm_end": finish_mlstm, "nsa_norm": nsa_scale, "k_cmp": k_compressed, "nsa_T": nsa_columns,
                        "kv_T": kv_columns, "gates": nsa_gates, "cmp_shift": cmp_exponents, "cmp_probs": cmp_weights, "cmp_turned": cmp_turned, "cmp_take": cmp_take}
                for step, i in DVE_ORDER:
                    does[step](i)
                for k in VEC_CHUNKS:
                    dve.wait_ge(mixT_done, KC * l + (k | 1) + 1)
                    do(TS(hT[:, k, :], ps[k // 2][:, 256 * (k % 2):256 * (k % 2) + 256], prm(l, "out_g")[:, k:k + 1], None, ALU.mult), mixT_vec)
                for half in range(2):
                    for tt in range(TT):
                        dve.wait_ge(wout_done, 4 * l + 2 * half + tt + 1)
                        xs = x[:, tt, 512 * half:512 * half + 512]
                        do(TTop(wide[:, 0:512], ps[4 + 2 * half + tt][:, :], gate[:, 0, 512 * half:512 * half + 512], ALU.mult))
                        do(TTop(xs, xs, wide[:, 0:512], ALU.add), x_mixed if half == 1 else None)

            def swiglu(f, steps, base, do, between=lambda j: None):
                for j, st in enumerate(steps):
                    sg, hb = hsig[:, 0:st.w], hbuf[:, j % 2, 0:st.w]
                    dve.wait_ge(f["tanh"], base + j + 1)
                    if j >= 2:
                        dve.wait_ge(f["T"], base + j - 1)
                    do(STT(hb, sg, 1.0, ps[4][:, 0:st.w], ALU.add, ALU.mult))
                    dve.wait_ge(f["u"], base + j + 1)
                    if st.last:
                        dve.sem_inc(ring_free[slot_of(st.loads[1])], 1)
                    do(STT(hb, hb, 0.5, ps[5][:, 0:st.w], ALU.mult, ALU.mult), f["h"])
                    between(j)

            def onehot_of(f, q, e, do, shift=0.0):
                for tt in range(TT):
                    r = rank[:, tt, bass.ds(e, 1)]
                    if shift:
                        do(TS(wtmp[:, tt:tt + 1], r, -shift, None, ALU.add))
                        r = wtmp[:, tt:tt + 1]
                    do(TS(pick[q][:, tt, :], cst("iota"), r, None, ALU.is_equal), f["onehot"] if tt else None)

            def gathered_in(f, q, count, do):
                dve.wait_ge(f["turned"], count)
                do(V.tensor_copy(pickT[q], ps[7][:, 0:256].rearrange("p (t n) -> p t n", t=TT)), f["turn_evac"])
                dve.wait_ge(f["gathered"], count)
                for k in range(4, KC):
                    do(TS(hT[:, k, 128 * q:128 * q + 128], ps[3][:, 128 * (k - 4):128 * (k - 4) + 128], scaleA[:, 1, k:k + 1],
                          modc[:, 24 + k:25 + k], ALU.mult, ALU.add), f["in_vec"] if k == KC - 1 else None)

            def y_out(f, downs, do):
                dve.wait_ge(f["d"], downs)
                for half in range(2):
                    c = slice(512 * half, 512 * half + 512)
                    do(TTop(ysb[:, c], ps[half][:, :], gate[:, 1, c], ALU.mult), f["y_1" if half else "y_0"])

            def add_in(f, half, column, count, do, bank=2):
                dve.wait_ge(f["scattered"], count)
                for tt in range(TT):
                    xs = x[:, tt, 512 * half:512 * half + 512]
                    do(STT(xs, ps[bank + tt][:, :], wts[:, tt, bass.ds(column, 1)], xs, ALU.mult, ALU.add), f["added"] if tt else None)

            def add_residual(tt, half, y):
                xs, g = x[:, tt, 512 * half:512 * half + 512], gate[:, 1, 512 * half:512 * half + 512]
                do(TTop(wide[:, 0:512], y, g, ALU.mult))
                do(TTop(xs, xs, wide[:, 0:512], ALU.add), x_final if half == 1 else None)

            mixer(0)
            normalise(1)
            modulate(1, 1)

            def modulation(j):
                c = j
                if c < 12:
                    ada_sum(1, c)
                if 1 <= c < 11:
                    ada_take(1, c - 1)
                if c in (4, 10):
                    mod_scale(1, c // 10)

            swiglu(ffn, dense_steps(), 0, do, modulation)
            for tt in range(TT):
                dve.wait_ge(ffn["y_0"], tt + 1)
                add_residual(tt, 0, ps[2 * tt][:, :])
                dve.wait_ge(ffn["d"], TT * len(FF_UNITS) - 1 + tt)
                add_residual(tt, 1, ps[2 * tt + 1][:, :])
            mixer(1)
            normalise(3)
            modulate(3, 1)
            do(V.memset(rank[:, :, :], 1000.0))
            do(V.memset(wts[:, :, 0:1], 0.0))
            do(V.memset(pickT[1], 0.0))
            do(V.memset(ysb, 0.0))
            dve.wait_ge(router_done, 1)
            for tt in range(TT):
                do(TTop(lg[:, tt, :], ps[7][:, 8 * tt:8 * tt + 8], prm(1, "router_b"), ALU.add))
                do(V.max(top8[:, tt, :], lg[:, tt, :]))
                do(V.max_index(topi[:, tt, :], top8[:, tt, :], lg[:, tt, :]))
            do(V.tensor_copy(topf[:, :, :], topi[:, :, :]))
            do(TTop(tw[:, :, 0:1], top8[:, :, 1:2], top8[:, :, 0:1], ALU.subtract), router_shift)
            iota8 = cst("iota")[:, 0:N_EXP]
            for tt in range(TT):
                p = picked[:, tt, :]
                do(TS(p, iota8, topf[:, tt, 0:1], None, ALU.is_equal))
                do(STT(p, iota8, topf[:, tt, 1:2], p, ALU.is_equal, ALU.add), picked_ready if tt else None)
            dve.wait_ge(router_exp, 1)
            do(TS(tw[:, :, 1:2], tw[:, :, 0:1], 1.0, None, ALU.add))
            do(V.reciprocal(tw[:, :, 1:2], tw[:, :, 1:2]))
            do(TTop(tw[:, :, 2:3], tw[:, :, 0:1], tw[:, :, 1:2], ALU.mult))
            dve.wait_ge(rank_done, 1)
            rk = rank[:, :, 0:N_EXP]
            do(STT(rk, picked[:, :, :], -1000.0, rk, ALU.mult, ALU.add))
            do(TTop(rk, rk, ps[6][:, 0:16].rearrange("p (t n) -> p t n", t=TT), ALU.add))
            onehot_of(moe, 0, 0, do)
            o_one, o_is, o_run, o_tmp, o_id = (wtmp[0:1, 8 * k:8 * k + 8] for k in range(5))
            do(V.memset(o_one, 1.0))
            do(TS(o_is, ps[6][0:1, 16:24], float(BLK), None, ALU.is_gt))
            do(V.tensor_tensor_scan(o_run, o_one, o_is, 0.0, ALU.mult, ALU.add))
            for k in range(OVER):
                do(TS(o_tmp, o_run, float(k + 1), None, ALU.is_equal))
                do(TTop(o_tmp, o_tmp, o_is, ALU.mult))
                do(TTop(o_tmp, o_tmp, cst("iota", 1)[:, 0:N_EXP], ALU.mult))
                do(V.tensor_reduce(o_id[:, k:k + 1], o_tmp, AX.X, ALU.add))
            do(V.tensor_copy(o_id[:, OVER:OVER + 1], o_run[:, 7:8]))
            do(V.tensor_copy(overi[0:1, 0:OVER + 1], o_id[:, 0:OVER + 1]), over_ready)
            gathered_in(moe, 0, 1, do)
            for tt in range(TT):
                w, one = wts[:, tt, 1:N_EXP + 1], wtmp[:, 0:N_EXP]
                do(TS(w, iota8, topf[:, tt, 0:1], tw[:, tt, 1:2], ALU.is_equal, ALU.mult))
                do(TS(one, iota8, topf[:, tt, 1:2], tw[:, tt, 2:3], ALU.is_equal, ALU.mult))
                do(TTop(w, w, one, ALU.add))
            dve.sem_inc(moe["y_0"], 1)
            dve.sem_inc(moe["y_1"], 1)
            per = 26
            with dve.Fori(0, N_EXP // 2) as i:
                doe = Ordered(dve, moe["vec_seq"])
                doe.base = {id(moe["vec_seq"]): i * per, id(moe["h"]): i * 14, id(moe["onehot"]): i * 2 + 1,
                            id(moe["turn_evac"]): i * 2 + 1, id(moe["in_vec"]): i * 2 + 1, id(moe["y_0"]): i * 2 + 1, id(moe["y_1"]): i * 2 + 1,
                            id(moe["added"]): i * 4}

                def between(j):
                    q, u = divmod(j, 7)
                    if j == 7:
                        y_out(moe, i * 14 + 7, doe)
                    if u == 1:
                        onehot_of(moe, 1 - q, i * 2 + (q + 1), doe)
                        add_in(moe, 0, i * 2 + q, i * 4 + (2 * q + 1), doe)
                    if u == 2:
                        add_in(moe, 1, i * 2 + q, i * 4 + (2 * q + 2), doe)
                    if u == 3:
                        gathered_in(moe, 1 - q, i * 2 + (q + 2), doe)

                swiglu(moe, expert_steps(0, 0) + expert_steps(1, 0), i * 14, doe, between)
                y_out(moe, i * 14 + 14, doe)
                assert doe.n[id(moe["vec_seq"])] == per, doe.n[id(moe["vec_seq"])]
            do.base[id(moe["added"])] = 2 * N_EXP
            for half in range(2):
                add_in(moe, half, N_EXP, 2 * N_EXP + half + 1, do, bank=6 if half else 2)
            n_over = dve.value_load(overi[0:1, OVER:OVER + 1], min_val=0, max_val=OVER)
            per_over = 15
            with dve.If(n_over > 0):
                with dve.Fori(0, OVER) as i:
                    with dve.If(i < n_over):
                        e = dve.value_load(overi[0:1, bass.ds(i, 1)], min_val=0, max_val=N_EXP - 1)
                        doe = Ordered(dve, over["vec_seq"])
                        doe.base = {id(over["vec_seq"]): i * per_over, id(over["h"]): i * 7, id(over["onehot"]): i,
                                    id(over["turn_evac"]): i, id(over["in_vec"]): i, id(over["y_0"]): i, id(over["y_1"]): i,
                                    id(over["added"]): i * 2}
                        onehot_of(over, 0, e, doe, float(BLK))
                        gathered_in(over, 0, i + 1, doe)
                        swiglu(over, expert_steps(0, 0), i * 7, doe)
                        y_out(over, i * 7 + 7, doe)
                        for half in range(2):
                            add_in(over, half, e + 1, i * 2 + (half + 1), doe)
                        dve.sem_inc(over["vec_left"], 1)
                        assert doe.n[id(over["vec_seq"])] == per_over, doe.n[id(over["vec_seq"])]
            dve.sem_inc(x_final, TT)


_RAW = ["x", "ada_w", "ada_b", "w_in", "w_out", "rel_bias", "nsa_cmp_wk", "nsa_cmp_wv", "ffn_wg", "ffn_wu", "ffn_wd",
        "moe_router_w", "moe_wg", "moe_wu", "moe_wd"]


def constants():
    import math

    import numpy as np
    f = np.float32
    c = np.zeros((128, CONST_W), f)

    def put(name, a):
        at, w = CONST[name]
        assert a.shape[1] == w, name
        c[:a.shape[0], at:at + w] = a

    p, j = np.arange(128)[:, None], np.arange(128)[None, :]
    zero = np.zeros((128, 128), f)
    big = f(-1e30)
    put("ident", np.eye(128, dtype=f))
    put("ones", np.ones((128, 1), f))
    put("minus_ones", -np.ones((128, 1), f))
    put("minus_tri", np.where(p >= j, f(-1), f(0)))
    for name, m in (("causal", j > p), ("causal_T", j < p), ("strict_T", j <= p)):
        d = np.where(m, big, f(0))
        put(name, np.concatenate([d, zero, d], 1))
    dist = 255 - np.arange(512)
    n = np.maximum(dist, 0)
    large = 16 + (np.log(np.maximum(n, 1).astype(f) / f(16)) / f(math.log(128 / 16)) * f(16)).astype(np.int32)
    bucket = np.where(n < 16, n, np.minimum(large, 31))
    onehot = ((np.arange(32)[:, None] == bucket[None, :]).astype(f))
    future = np.ascontiguousarray(np.broadcast_to(np.where(dist < 0, big, f(0)), (H, 512)))
    ends = 16 * np.arange(NCMP) + 31
    put("valid_cmp", np.concatenate([(ends[None, :] <= p + 128 * tt).astype(f) for tt in range(TT)], 1))
    put("iota", np.broadcast_to(np.arange(128, dtype=f), (128, 128)))
    return c, onehot, future


def parameters(i):
    import numpy as np
    out = np.zeros((DEPTH, 128, PAR_W), np.float32)
    for l in range(DEPTH):
        def at(name, p0, p1, k0=0, k1=None):
            a, w = PAR[name]
            return out[l, p0:p1, a + k0:a + (w if k1 is None else k1)]
        at("norm1", 0, 128)[:] = i["norm1_g"][l].reshape(8, 128).T
        at("norm2", 0, 128)[:] = i["norm2_g"][l].reshape(8, 128).T
        at("conv", 0, 128)[:] = i["mlstm_conv_w"][l].reshape(4, 4, 128).transpose(2, 1, 0).reshape(128, 16)
        at("gate_bias", 0, 4)[:, 0] = i["mlstm_gate_b"][l, 4:8]
        at("gate_bias", 4, 8)[:, 0] = i["fox_f_b"][l]
        at("gate_bias", 32, 36)[:, 0] = i["mlstm_gate_b"][l, 0:4]
        at("out_g", 0, 128)[:] = 1
        at("out_g", 0, 128, 0, 2)[:] = i["mlstm_out_g"][l].reshape(2, 128).T
        for p0 in (0, 64):
            at("fox_q", p0, p0 + 64)[:, 0] = i["fox_q_g"][l]
            at("fox_k", p0, p0 + 64)[:, 0] = i["fox_k_g"][l]
            at("nsa_q", p0, p0 + 64)[:, 0] = i["nsa_q_g"][l]
            at("nsa_k", p0, p0 + 64)[:] = i["nsa_k_g"][l][[0, 1, 2] if p0 == 0 else [0, 2, 1]].T
        at("cmp_pos", 0, 64)[:] = i["nsa_cmp_pos"][l].T
        at("cmp_pos", 64, 128)[:] = i["nsa_cmp_pos"][l].T
        at("nsa_gate_b", 0, 128)[:] = i["nsa_gate_b"][l][None]
        if l % 2:
            at("router_b", 0, 128)[:] = i["moe_router_b"][l // 2][None]
        at("ada_b", 0, 128)[:] = i["ada_b"][l].reshape(48, 128).T
    return out


def kernel(**inputs):
    import numpy as np
    import concourse.bacc as bacc
    from concourse.bass_utils import run_bass_kernel_spmd

    a = {n: np.ascontiguousarray(v) for n, v in inputs.items()}
    w_in = a["w_in"]
    gates = np.zeros((DEPTH, D, 48), w_in.dtype)
    gates[:, :, 0:4] = w_in[:, :, 1028:1032]
    gates[:, :, 4:8] = w_in[:, :, 1800:1804]
    gates[:, :, 32:36] = w_in[:, :, 1024:1028]
    gates[:, :, 36:48] = w_in[:, :, 3212:3224]
    arrays = {n: a[n] for n in _RAW}
    arrays["reverse"] = np.ascontiguousarray(np.eye(128, dtype=np.float32)[::-1])
    arrays["c_cols"] = np.ascontiguousarray(a["c"].reshape(KC, 128).T)
    arrays["w_gates"] = gates
    arrays["const"], arrays["onehot"], arrays["future"] = constants()
    arrays["par"] = parameters(a)

    nc = bacc.Bacc("TRN2", target_bir_lowering=False, num_devices=1)
    t = {n: nc.dram_tensor("in_" + n, v.shape, mybir.dt.from_np(v.dtype), kind="ExternalInput").ap() for n, v in arrays.items()}
    out = nc.dram_tensor("out", (1, S, D), F32, kind="ExternalOutput").ap()
    program(nc, t, out)
    r = run_bass_kernel_spmd(nc, [{"in_" + n: v for n, v in arrays.items()}], core_ids=[0])
    return r.results[0]["out"]
```
